# Optimizing a Trainium2 kernel written in Bass

```python
import math
import jax, jax.numpy as jnp
from jax import lax
import numpy as np

D_MODEL = 2048
BATCH = 1
SEQ = 256
DEPTH = 1

RET_HEADS = 4
RET_QK_DIM = 64
RET_V_DIM = 128
RET_WIDTH = RET_HEADS * RET_V_DIM
RET_CHUNK = 128
RET_COLS = 2 * RET_HEADS * RET_QK_DIM + 2 * RET_WIDTH

RWKV_HEADS = 8
RWKV_HEAD_DIM = 64
RWKV_WIDTH = RWKV_HEADS * RWKV_HEAD_DIM
RWKV_DECAY_RANK = 96
RWKV_A_RANK = 96
RWKV_GATE_RANK = 256
RWKV_GN_EPS = 64e-5
RWKV_COLS = 3 * RWKV_WIDTH + RWKV_DECAY_RANK + RWKV_A_RANK + RWKV_GATE_RANK

MOBA_HEADS = 8
MOBA_HEAD_DIM = 128
MOBA_WIDTH = MOBA_HEADS * MOBA_HEAD_DIM
MOBA_BLOCK = 256
MOBA_TOPK = 3
MOBA_Q_CHUNK = 32
MOBA_COLS = 3 * MOBA_WIDTH
NEG_INF = -1e30

MIX_WIDTH = RET_WIDTH + RWKV_WIDTH + MOBA_WIDTH
IN_COLS = RET_COLS + RWKV_COLS + MOBA_COLS

D_FF = 5632
CONV_WIDTH = 3
NORM_EPS = 1e-6


def rms_norm(x, g):
    xf = x.astype(jnp.float32)
    y = xf * lax.rsqrt(jnp.mean(xf * xf, axis=-1, keepdims=True) + NORM_EPS)
    return (y * g.astype(jnp.float32)).astype(x.dtype)

def token_shift(x):
    return jnp.pad(x, ((0, 0), (1, 0), (0, 0)))[:, :-1]

def retention_chunkwise(q, k, v):
    B, S, H, Dk = q.shape
    Dv = v.shape[-1]
    C = RET_CHUNK
    N = S // C
    f32 = jnp.float32
    log_g = jnp.log1p(-jnp.exp2(-5.0 - jnp.arange(H, dtype=f32)))

    def chunks(a, d):
        return a.astype(f32).reshape(B, N, C, H, d).transpose(1, 0, 3, 2, 4)

    qc_all = chunks(q, Dk)
    kc_all = chunks(k, Dk) * (Dk ** -0.5)
    vc_all = chunks(v, Dv)
    idx = jnp.arange(C, dtype=f32)
    diff = idx[:, None] - idx[None, :]
    inner_decay = jnp.where(diff >= 0, jnp.exp(log_g[:, None, None] * jnp.maximum(diff, 0.0)), 0.0)
    q_decay = jnp.exp(log_g[:, None] * (idx + 1.0))[..., None]
    k_decay = jnp.exp(log_g[:, None] * (C - 1.0 - idx))[..., None]
    chunk_decay = jnp.exp(log_g * C)[:, None, None]

    def step(R, inp):
        qc, kc, vc = inp
        inner = jnp.einsum('bhid,bhjd->bhij', qc, kc) * inner_decay
        o = jnp.einsum('bhij,bhjv->bhiv', inner, vc) + jnp.einsum('bhid,bhdv->bhiv', qc, R) * q_decay
        R = R * chunk_decay + jnp.einsum('bhjd,bhjv->bhdv', kc * k_decay, vc)
        return R, o

    R0 = jnp.zeros((B, H, Dk, Dv), f32)
    _, o = lax.scan(step, R0, (qc_all, kc_all, vc_all))
    return o.transpose(1, 0, 3, 2, 4).reshape(B, S, H, Dv)

def rwkv7_time_mix(r, k, v, wd, wa, wg, w0, w_up, a0, a_up, g_up, k_k, k_a, r_k, ln_w, ln_b):
    B, S, C = r.shape
    H, N = RWKV_HEADS, RWKV_HEAD_DIM
    f32 = jnp.float32
    r, k, v = r.astype(f32), k.astype(f32), v.astype(f32)
    w_log = -jax.nn.softplus(-(w0 + jnp.tanh(wd.astype(f32)) @ w_up)) - 0.5
    decay = jnp.exp(-jnp.exp(w_log))
    a = jax.nn.sigmoid(a0 + wa.astype(f32) @ a_up)
    g = jax.nn.sigmoid(wg.astype(f32)) @ g_up
    kk = (k * k_k).reshape(B, S, H, N)
    kk = kk / jnp.maximum(jnp.sqrt(jnp.sum(kk * kk, axis=-1, keepdims=True)), 1e-12)
    k = k * (1.0 + (a - 1.0) * k_a)

    def heads_tm(z):
        return jnp.moveaxis(z.reshape(B, S, H, N), 1, 0)

    def step(state, inp):
        r_t, w_t, k_t, v_t, kk_t, a_t = inp
        sa = jnp.einsum('bhij,bhj->bhi', state, -kk_t)
        state = (state * w_t[:, :, None, :]
                 + sa[..., None] * (kk_t * a_t)[:, :, None, :]
                 + v_t[..., None] * k_t[:, :, None, :])
        y = jnp.einsum('bhij,bhj->bhi', state, r_t)
        return state, y

    s0 = jnp.zeros((B, H, N, N), f32)
    _, y = lax.scan(step, s0, (heads_tm(r), heads_tm(decay), heads_tm(k), heads_tm(v),
                               jnp.moveaxis(kk, 1, 0), heads_tm(a)))
    y = jnp.moveaxis(y, 0, 1)
    mean = jnp.mean(y, axis=-1, keepdims=True)
    var = jnp.mean((y - mean) ** 2, axis=-1, keepdims=True)
    y = ((y - mean) * lax.rsqrt(var + RWKV_GN_EPS)).reshape(B, S, C) * ln_w + ln_b
    rh, kh, vh = r.reshape(B, S, H, N), k.reshape(B, S, H, N), v.reshape(B, S, H, N)
    bonus = (jnp.sum(rh * kh * r_k, axis=-1, keepdims=True) * vh).reshape(B, S, C)
    return (y + bonus) * g

def moba_attention(q, k, v):
    B, S, H, D = q.shape
    L = MOBA_BLOCK
    NB = -(-S // L)
    P = NB * L
    topk = min(MOBA_TOPK, NB)
    QC = MOBA_Q_CHUNK
    f32 = jnp.float32
    slopes = jnp.exp2(-8.0 * jnp.arange(1, H + 1, dtype=f32) / H)
    qh = q.astype(f32).transpose(0, 2, 1, 3) * (D ** -0.5)
    pad = ((0, 0), (0, 0), (0, P - S), (0, 0))
    kh = jnp.pad(k.astype(f32).transpose(0, 2, 1, 3), pad)
    vh = jnp.pad(v.astype(f32).transpose(0, 2, 1, 3), pad)
    kb = kh.reshape(B, H, NB, L, D)
    vb = vh.reshape(B, H, NB, L, D)
    k_mean = jnp.mean(kb, axis=3)
    gate = jnp.einsum('bhsd,bhnd->bhsn', qh, k_mean)
    q_block = jnp.arange(S) // L
    fully_past = jnp.arange(NB)[None, :] < q_block[:, None]
    gate = jnp.where(fully_past, gate, -jnp.inf)
    _, sel = lax.top_k(gate, topk)
    b_ix = jnp.arange(B)[:, None, None, None]
    h_ix = jnp.arange(H)[None, :, None, None]
    offs = jnp.arange(L)

    def chunk(ci):
        q0 = ci * QC
        qc = lax.dynamic_slice_in_dim(qh, q0, QC, axis=2)
        sc = lax.dynamic_slice_in_dim(sel, q0, QC, axis=2)
        t = q0 + jnp.arange(QC)
        bq = q0 // L
        kg = kb[b_ix, h_ix, sc]
        vg = vb[b_ix, h_ix, sc]
        s_sel = jnp.einsum('bhqd,bhqnld->bhqnl', qc, kg)
        dist_sel = (t[:, None, None] - (sc[..., None] * L + offs)).astype(f32)
        s_sel = jnp.where((sc < bq)[..., None],
                          s_sel - slopes[:, None, None, None] * dist_sel, NEG_INF)
        ko = lax.dynamic_slice_in_dim(kh, bq * L, L, axis=2)
        vo = lax.dynamic_slice_in_dim(vh, bq * L, L, axis=2)
        s_own = jnp.einsum('bhqd,bhld->bhql', qc, ko)
        dist_own = t[:, None] - (bq * L + offs)[None, :]
        s_own = jnp.where(dist_own >= 0,
                          s_own - slopes[:, None, None] * dist_own.astype(f32), NEG_INF)
        scores = jnp.concatenate([s_sel.reshape(B, H, QC, topk * L), s_own], axis=-1)
        p = jax.nn.softmax(scores, axis=-1)
        p_sel = p[..., :topk * L].reshape(B, H, QC, topk, L)
        p_own = p[..., topk * L:]
        return (jnp.einsum('bhqnl,bhqnld->bhqd', p_sel, vg)
                + jnp.einsum('bhql,bhld->bhqd', p_own, vo))

    out = lax.map(chunk, jnp.arange(S // QC))
    return out.transpose(1, 0, 3, 2, 4).reshape(B, S, H * D)

def hybrid_mixer(h, w_in, w_out, mu, w0, w_up, a0, a_up, g_up, k_k, k_a, r_k, ln_w, ln_b):
    B, S, _ = h.shape
    proj = h @ w_in
    o0 = 0
    qk = RET_HEADS * RET_QK_DIM
    rq = proj[..., o0:o0 + qk].reshape(B, S, RET_HEADS, RET_QK_DIM)
    rk = proj[..., o0 + qk:o0 + 2 * qk].reshape(B, S, RET_HEADS, RET_QK_DIM)
    rv = proj[..., o0 + 2 * qk:o0 + 2 * qk + RET_WIDTH].reshape(B, S, RET_HEADS, RET_V_DIM)
    rg = proj[..., o0 + 2 * qk + RET_WIDTH:o0 + RET_COLS].astype(jnp.float32)
    ro = retention_chunkwise(rq, rk, rv)
    ro = ro * lax.rsqrt(jnp.mean(ro * ro, axis=-1, keepdims=True) + NORM_EPS)
    ret_out = ro.reshape(B, S, RET_WIDTH) * jax.nn.silu(rg)
    rw = proj[..., RET_COLS:RET_COLS + RWKV_COLS]
    rw = rw + (token_shift(rw) - rw) * mu
    c1 = RWKV_WIDTH
    c2 = 2 * RWKV_WIDTH
    c3 = 3 * RWKV_WIDTH
    c4 = c3 + RWKV_DECAY_RANK
    c5 = c4 + RWKV_A_RANK
    rwkv_out = rwkv7_time_mix(rw[..., :c1], rw[..., c1:c2], rw[..., c2:c3],
                              rw[..., c3:c4], rw[..., c4:c5], rw[..., c5:],
                              w0, w_up, a0, a_up, g_up, k_k, k_a, r_k, ln_w, ln_b)
    m0 = RET_COLS + RWKV_COLS
    mq = proj[..., m0:m0 + MOBA_WIDTH].reshape(B, S, MOBA_HEADS, MOBA_HEAD_DIM)
    mk = proj[..., m0 + MOBA_WIDTH:m0 + 2 * MOBA_WIDTH].reshape(B, S, MOBA_HEADS, MOBA_HEAD_DIM)
    mv = proj[..., m0 + 2 * MOBA_WIDTH:m0 + 3 * MOBA_WIDTH].reshape(B, S, MOBA_HEADS, MOBA_HEAD_DIM)
    moba_out = moba_attention(mq, mk, mv)
    mixed = jnp.concatenate([ret_out.astype(h.dtype), rwkv_out.astype(h.dtype),
                             moba_out.astype(h.dtype)], axis=-1)
    return mixed @ w_out

def conv_glu_ffn(h, w_up, conv_w, conv_b, w_down):
    S = h.shape[1]
    u = h @ w_up
    up = jnp.pad(u, ((0, 0), (CONV_WIDTH - 1, 0), (0, 0)))
    u = sum(conv_w[j] * up[:, j:j + S] for j in range(CONV_WIDTH)) + conv_b
    val, gate = jnp.split(u, 2, axis=-1)
    return (jax.nn.silu(gate) * val) @ w_down

def first_inputs(seed: int = 0) -> dict:
    key = jax.random.key(seed)
    ks = jax.random.split(key, 24)
    D, L = D_MODEL, DEPTH
    f32 = jnp.float32

    def nrm(k, shape, scale):
        return jax.random.normal(k, shape, f32) * scale

    ratio = (jnp.arange(RWKV_WIDTH, dtype=f32) / (RWKV_WIDTH - 1)) ** 0.85
    return {
        "x": nrm(ks[0], (BATCH, SEQ, D), 1.0),
        "c": nrm(ks[1], (BATCH, D), 1.0),
        "w_in": nrm(ks[2], (L, D, IN_COLS), D ** -0.5),
        "w_out": nrm(ks[3], (L, MIX_WIDTH, D), MIX_WIDTH ** -0.5),
        "rwkv_mu": jax.random.uniform(ks[4], (L, RWKV_COLS), f32),
        "rwkv_w0": (-6.5 + 5.0 * ratio)[None, :] + nrm(ks[5], (L, RWKV_WIDTH), 0.1),
        "rwkv_w_up": nrm(ks[6], (L, RWKV_DECAY_RANK, RWKV_WIDTH), 0.1 * RWKV_DECAY_RANK ** -0.5),
        "rwkv_a0": nrm(ks[7], (L, RWKV_WIDTH), 0.1),
        "rwkv_a_up": nrm(ks[8], (L, RWKV_A_RANK, RWKV_WIDTH), RWKV_A_RANK ** -0.5),
        "rwkv_g_up": nrm(ks[9], (L, RWKV_GATE_RANK, RWKV_WIDTH), RWKV_GATE_RANK ** -0.5),
        "rwkv_k_k": 0.85 + nrm(ks[10], (L, RWKV_WIDTH), 0.05),
        "rwkv_k_a": 1.0 + nrm(ks[11], (L, RWKV_WIDTH), 0.05),
        "rwkv_r_k": -0.04 + nrm(ks[12], (L, RWKV_HEADS, RWKV_HEAD_DIM), 0.1),
        "rwkv_ln_w": 1.0 + nrm(ks[13], (L, RWKV_WIDTH), 0.05),
        "rwkv_ln_b": nrm(ks[14], (L, RWKV_WIDTH), 0.02),
        "w_ffn_up": nrm(ks[15], (L, D, 2 * D_FF), D ** -0.5),
        "ffn_conv_w": nrm(ks[16], (L, CONV_WIDTH, 2 * D_FF), CONV_WIDTH ** -0.5),
        "ffn_conv_b": nrm(ks[17], (L, 2 * D_FF), 0.02),
        "w_ffn_down": nrm(ks[18], (L, D_FF, D), D_FF ** -0.5),
        "w_ada": nrm(ks[19], (L, D, 6 * D), 0.5 * D ** -0.5),
        "b_ada": nrm(ks[20], (L, 6 * D), 0.02),
        "norm_mix": 1.0 + nrm(ks[21], (L, D), 0.05),
        "norm_ffn": 1.0 + nrm(ks[22], (L, D), 0.05),
        "norm_final": 1.0 + nrm(ks[23], (D,), 0.05),
    }

def first_block(x, c, w_in, w_out, rwkv_mu, rwkv_w0, rwkv_w_up, rwkv_a0, rwkv_a_up, rwkv_g_up,
              rwkv_k_k, rwkv_k_a, rwkv_r_k, rwkv_ln_w, rwkv_ln_b, w_ffn_up, ffn_conv_w,
              ffn_conv_b, w_ffn_down, w_ada, b_ada, norm_mix, norm_ffn, norm_final):
    c_act = jax.nn.silu(c)
    for l in range(DEPTH):
        mod = (c_act @ w_ada[l] + b_ada[l])[:, None, :]
        sh1, sc1, g1, sh2, sc2, g2 = jnp.split(mod, 6, axis=-1)
        h = rms_norm(x, norm_mix[l]) * (1.0 + sc1) + sh1
        x = x + g1 * hybrid_mixer(h, w_in[l], w_out[l], rwkv_mu[l], rwkv_w0[l], rwkv_w_up[l],
                                  rwkv_a0[l], rwkv_a_up[l], rwkv_g_up[l], rwkv_k_k[l],
                                  rwkv_k_a[l], rwkv_r_k[l], rwkv_ln_w[l], rwkv_ln_b[l])
        h = rms_norm(x, norm_ffn[l]) * (1.0 + sc2) + sh2
        x = x + g2 * conv_glu_ffn(h, w_ffn_up[l], ffn_conv_w[l], ffn_conv_b[l], w_ffn_down[l])
    return rms_norm(x, norm_final)


D_MIX = D_MODEL
D_FOURIER = D_MIX // 2
N_FOURIER_GROUPS = 4
FOURIER_GROUP = D_FOURIER // N_FOURIER_GROUPS
D_MLSTM = D_MIX - D_FOURIER
N_MLSTM_HEADS = 4
HEAD_V = D_MLSTM // N_MLSTM_HEADS
HEAD_QK = HEAD_V // 2
D_QK = N_MLSTM_HEADS * HEAD_QK
N_GATES = 4 * N_MLSTM_HEADS
D_IN = D_FOURIER + 2 * D_QK + 2 * D_MLSTM + N_GATES
CHUNK = 64
CONV_W = 3
N_MOD = 6
EPS = 1e-6
M_INIT = -1e30


def rms_norm_2(x, w):
    xf = x.astype(jnp.float32)
    y = xf * lax.rsqrt(jnp.mean(xf * xf, axis=-1, keepdims=True) + EPS)
    return (y * w.astype(jnp.float32)).astype(x.dtype)

def modulate(h, shift, scale):
    return h * (1 + scale[:, None, :]) + shift[:, None, :]

def fourier_mix(u):
    B, S, _ = u.shape
    ug = u.astype(jnp.float32).reshape(B, S, N_FOURIER_GROUPS, FOURIER_GROUP)
    y = jnp.fft.fft2(ug, axes=(1, 3), norm="ortho").real
    return y.reshape(B, S, D_FOURIER).astype(u.dtype)

def mlstm_chunkwise(q, k, v, ig, fg):
    B, H, S, Dk = q.shape
    Dv = v.shape[-1]
    NC = S // CHUNK
    lf = jax.nn.log_sigmoid(fg)
    q = q.reshape(B, H, NC, CHUNK, Dk) * (Dk ** -0.5)
    k = k.reshape(B, H, NC, CHUNK, Dk)
    v = v.reshape(B, H, NC, CHUNK, Dv)
    ig = ig.reshape(B, H, NC, CHUNK)
    lf = lf.reshape(B, H, NC, CHUNK)
    b = jnp.cumsum(lf, axis=-1)
    g = b[..., -1]

    a = g[..., None] - b + ig
    m_loc = jnp.max(a, axis=-1)
    w_loc = jnp.exp(a - m_loc[..., None])
    C_loc = jnp.einsum('bhclv,bhclk->bhcvk', v * w_loc[..., None], k)
    n_loc = jnp.einsum('bhcl,bhclk->bhck', w_loc, k)

    def step(carry, inp):
        C, n, m = carry
        g_c, m_c, C_c, n_c = inp
        m_new = jnp.maximum(g_c + m, m_c)
        s_old = jnp.exp(g_c + m - m_new)
        s_loc = jnp.exp(m_c - m_new)
        C_new = s_old[..., None, None] * C + s_loc[..., None, None] * C_c
        n_new = s_old[..., None] * n + s_loc[..., None] * n_c
        return (C_new, n_new, m_new), (C, n, m)

    init = (jnp.zeros((B, H, Dv, Dk), jnp.float32),
            jnp.zeros((B, H, Dk), jnp.float32),
            jnp.full((B, H), M_INIT, jnp.float32))
    xs = (jnp.moveaxis(g, 2, 0), jnp.moveaxis(m_loc, 2, 0),
          jnp.moveaxis(C_loc, 2, 0), jnp.moveaxis(n_loc, 2, 0))
    _, (C_st, n_st, m_st) = lax.scan(step, init, xs)
    C_st = jnp.moveaxis(C_st, 0, 2)
    n_st = jnp.moveaxis(n_st, 0, 2)
    m_st = jnp.moveaxis(m_st, 0, 2)

    tri = jnp.tril(jnp.ones((CHUNK, CHUNK), dtype=bool))
    Dlog = jnp.where(tri, b[..., :, None] - b[..., None, :] + ig[..., None, :], -jnp.inf)
    inter = b + m_st[..., None]
    m_row = jnp.maximum(jnp.max(Dlog, axis=-1), inter)
    P = jnp.exp(Dlog - m_row[..., None]) * jnp.einsum('bhcjd,bhctd->bhcjt', q, k)
    s_inter = jnp.exp(inter - m_row)
    num = (jnp.einsum('bhcjt,bhctv->bhcjv', P, v)
           + s_inter[..., None] * jnp.einsum('bhcjk,bhcvk->bhcjv', q, C_st))
    den = jnp.sum(P, axis=-1) + s_inter * jnp.einsum('bhcjk,bhck->bhcj', q, n_st)
    h = num / jnp.maximum(jnp.abs(den), jnp.exp(-m_row))[..., None]
    return h.reshape(B, H, S, Dv)

def mlstm_bidirectional(q_in, k_in, v_in, gates, mlstm_norm_w):
    B, S, _ = q_in.shape
    H = N_MLSTM_HEADS
    q = q_in.astype(jnp.float32).reshape(B, S, H, HEAD_QK).transpose(0, 2, 1, 3)
    k = k_in.astype(jnp.float32).reshape(B, S, H, HEAD_QK).transpose(0, 2, 1, 3)
    v = v_in.astype(jnp.float32).reshape(B, S, H, HEAD_V).transpose(0, 2, 1, 3)
    gt = gates.astype(jnp.float32).reshape(B, S, 4, H).transpose(2, 0, 3, 1)
    i_f, f_f, i_b, f_b = gt[0], gt[1], gt[2], gt[3]
    h_fwd = mlstm_chunkwise(q, k, v, i_f, f_f)
    h_bwd = jnp.flip(mlstm_chunkwise(jnp.flip(q, 2), jnp.flip(k, 2), jnp.flip(v, 2),
                                     jnp.flip(i_b, 2), jnp.flip(f_b, 2)), 2)
    h = (h_fwd + h_bwd).transpose(0, 2, 1, 3)
    h = h * lax.rsqrt(jnp.mean(h * h, axis=-1, keepdims=True) + EPS)
    h = h.reshape(B, S, D_MLSTM) * mlstm_norm_w.astype(jnp.float32)
    return h.astype(q_in.dtype)

def depthwise_conv_centred(u, w_conv, b_conv):
    C = u.shape[-1]
    y = lax.conv_general_dilated(u, w_conv[:, None, :].astype(u.dtype), window_strides=(1,),
                                 padding='SAME', dimension_numbers=('NWC', 'WIO', 'NWC'),
                                 feature_group_count=C)
    return y + b_conv

def second_inputs(seed: int = 0) -> dict:
    key = jax.random.key(seed)
    ks = jax.random.split(key, 20)
    f32 = jnp.float32
    H = N_MLSTM_HEADS
    x = jax.random.normal(ks[0], (BATCH, SEQ, D_MODEL), f32)
    c = jax.random.normal(ks[1], (BATCH, D_MODEL), f32)
    w_ada = jax.random.normal(ks[2], (D_MODEL, N_MOD * D_MODEL), f32) * (0.5 * D_MODEL ** -0.5)
    b_ada = 0.02 * jax.random.normal(ks[3], (N_MOD * D_MODEL,), f32)
    norm1_w = 1.0 + 0.02 * jax.random.normal(ks[4], (D_MODEL,), f32)
    w_in = jax.random.normal(ks[5], (D_MODEL, D_IN), f32) * (D_MODEL ** -0.5)
    bi_f = -1.0 + 0.1 * jax.random.normal(ks[6], (H,), f32)
    bf_f = jnp.linspace(3.0, 6.0, H, dtype=f32) + 0.1 * jax.random.normal(ks[7], (H,), f32)
    bi_b = -1.0 + 0.1 * jax.random.normal(ks[8], (H,), f32)
    bf_b = jnp.linspace(3.0, 6.0, H, dtype=f32) + 0.1 * jax.random.normal(ks[9], (H,), f32)
    b_gates = jnp.concatenate([bi_f, bf_f, bi_b, bf_b])
    mlstm_norm_w = 1.0 + 0.02 * jax.random.normal(ks[10], (D_MLSTM,), f32)
    w_out = jax.random.normal(ks[11], (D_MIX, D_MODEL), f32) * (D_MIX ** -0.5)
    norm2_w = 1.0 + 0.02 * jax.random.normal(ks[12], (D_MODEL,), f32)
    w_up = jax.random.normal(ks[13], (D_MODEL, 2 * D_FF), f32) * (D_MODEL ** -0.5)
    w_conv = jax.random.normal(ks[14], (CONV_W, 2 * D_FF), f32) * (CONV_W ** -0.5)
    b_conv = 0.02 * jax.random.normal(ks[15], (2 * D_FF,), f32)
    w_down = jax.random.normal(ks[16], (D_FF, D_MODEL), f32) * (D_FF ** -0.5)
    norm_f_w = 1.0 + 0.02 * jax.random.normal(ks[17], (D_MODEL,), f32)
    return {"x": x, "c": c, "w_ada": w_ada, "b_ada": b_ada, "norm1_w": norm1_w,
            "w_in": w_in, "b_gates": b_gates, "mlstm_norm_w": mlstm_norm_w, "w_out": w_out,
            "norm2_w": norm2_w, "w_up": w_up, "w_conv": w_conv, "b_conv": b_conv,
            "w_down": w_down, "norm_f_w": norm_f_w}

def second_block(x, c, w_ada, b_ada, norm1_w, w_in, b_gates, mlstm_norm_w, w_out,
              norm2_w, w_up, w_conv, b_conv, w_down, norm_f_w):
    mod = jax.nn.silu(c) @ w_ada + b_ada
    shift1, scale1, gate1, shift2, scale2, gate2 = jnp.split(mod, N_MOD, axis=-1)
    o1 = D_FOURIER
    o2 = o1 + D_QK
    o3 = o2 + D_QK
    o4 = o3 + D_MLSTM
    o5 = o4 + D_MLSTM
    for _ in range(DEPTH):
        h = modulate(rms_norm_2(x, norm1_w), shift1, scale1)
        p = h @ w_in
        u_f = p[..., :o1]
        q_in, k_in, v_in = p[..., o1:o2], p[..., o2:o3], p[..., o3:o4]
        o_gate = jax.nn.sigmoid(p[..., o4:o5])
        gates = p[..., o5:] + b_gates
        y_f = fourier_mix(u_f)
        y_m = mlstm_bidirectional(q_in, k_in, v_in, gates, mlstm_norm_w) * o_gate
        mix = jnp.concatenate([y_f, y_m], axis=-1)
        x = x + gate1[:, None, :] * (mix @ w_out)
        h2 = modulate(rms_norm_2(x, norm2_w), shift2, scale2)
        u = depthwise_conv_centred(h2 @ w_up, w_conv, b_conv)
        a, v = jnp.split(u, 2, axis=-1)
        x = x + gate2[:, None, :] * ((jax.nn.silu(a) * v) @ w_down)
    return rms_norm_2(x, norm_f_w)


def setup_inputs(seed=0):
    out = dict(first_inputs(seed))
    for name, value in second_inputs(seed + 1).items():
        if name != "x":
            out[name + "_2"] = value
    return out


def reference(
    x, c, w_in, w_out, rwkv_mu, rwkv_w0, rwkv_w_up, rwkv_a0, rwkv_a_up, rwkv_g_up, rwkv_k_k,
    rwkv_k_a, rwkv_r_k, rwkv_ln_w, rwkv_ln_b, w_ffn_up, ffn_conv_w, ffn_conv_b, w_ffn_down,
    w_ada, b_ada, norm_mix, norm_ffn, norm_final, c_2, w_ada_2, b_ada_2, norm1_w_2, w_in_2,
    b_gates_2, mlstm_norm_w_2, w_out_2, norm2_w_2, w_up_2, w_conv_2, b_conv_2, w_down_2,
    norm_f_w_2,
):
    x = first_block(
        x, c, w_in, w_out, rwkv_mu, rwkv_w0, rwkv_w_up, rwkv_a0, rwkv_a_up, rwkv_g_up, rwkv_k_k,
        rwkv_k_a, rwkv_r_k, rwkv_ln_w, rwkv_ln_b, w_ffn_up, ffn_conv_w, ffn_conv_b, w_ffn_down,
        w_ada, b_ada, norm_mix, norm_ffn, norm_final,
    )
    return second_block(
        x, c_2, w_ada_2, b_ada_2, norm1_w_2, w_in_2, b_gates_2, mlstm_norm_w_2, w_out_2,
        norm2_w_2, w_up_2, w_conv_2, b_conv_2, w_down_2, norm_f_w_2,
    )


_drawn_inputs = setup_inputs


def setup_inputs(seed=0):
    import zlib

    import numpy as np

    out = dict(_drawn_inputs(seed))
    spreads = {}
    factors = {'rwkv_w_up': 8.0,
     'rwkv_a0': 8.0,
     'rwkv_k_k': 8.0,
     'rwkv_k_a': 8.0,
     'rwkv_ln_w': 8.0,
     'rwkv_ln_b': 8.0,
     'ffn_conv_b': 8.0,
     'norm_mix': 3.687,
     'norm_ffn': 3.528,
     'norm1_w_2': 8.0,
     'mlstm_norm_w_2': 28.191,
     'norm2_w_2': 8.0,
     'b_conv_2': 8.0,
     'norm_f_w_2': 7.708}
    for name, (base, spread) in spreads.items():
        noise = np.random.default_rng([zlib.crc32(name.encode()), seed]).standard_normal(out[name].shape)
        drawn = base * np.exp(spread * noise) if base else spread * noise
        out[name] = __import__('jax').numpy.asarray(drawn.astype(out[name].dtype))
    for name, factor in factors.items():
        out[name] = (out[name] * factor).astype(out[name].dtype)
    return out
```

```python
from contextlib import ExitStack, contextmanager

import numpy as np
import concourse.bass as bass
from concourse import mybir

F32 = mybir.dt.float32
F32R = mybir.dt.float32r
ALU = mybir.AluOpType
ACT = mybir.ActivationFunctionType
AX_X = mybir.AxisListType.X

P = 128
S = 256
D = 2048
KT = D // P
DFF = 5632
NFF = DFF // 512
SLAB = 1024
RING = 4
GS = KT // 2
EPS = 1e-6
EXP_HALF = float(np.exp(-0.5))

G_RR, G_RK, G_RV, G_LORA, G_TQK, G_TV, G_TG, G_MQ0, G_MK0, G_MV0, G_MQ1, G_MK1, G_MV1 = range(13)
MIX1 = 13
MIX2 = 8
B1_OUT = MIX1 * GS
B1_UP = B1_OUT + 4 * GS
B1_DOWN = B1_UP + 2 * NFF * GS
DOWN_HALF = NFF * 4
B2 = B1_DOWN + 2 * DOWN_HALF
B2_OUT = B2 + MIX2 * GS
B2_UP = B2_OUT + 4 * GS
B2_DOWN = B2_UP + 2 * NFF * GS
N_SLABS = B2_DOWN + 2 * DOWN_HALF

COLS = {}
_at = 0
for _name, _n in [("c", 32), ("bada", 192), ("norm_mix", 16), ("norm_ffn", 16), ("norm_final", 16),
                  ("norm1", 16), ("norm2", 16), ("norm_f", 16), ("mu", 16), ("w0", 4), ("a0", 4),
                  ("k_k", 4), ("k_a", 4), ("r_k", 4), ("ln_w", 4), ("ln_b", 4), ("mlstm_norm", 8),
                  ("bgates", 16)]:
    COLS[_name] = _at
    _at += _n
NCOLS = _at

TABS = {}
_at = 0
for _name, _n in [("ident", 128), ("ones", 128), ("blk64", 128), ("strict", 128), ("incl", 128),
                  ("levels", 6 * 128), ("id64", 64), ("alibi", 256), ("retdecay", 4 * 256),
                  ("mfwd", 256), ("mbwd", 256), ("tri", 128), ("dft", 1024)]:
    TABS[_name] = (_at, _n)
    _at += _n
NTABS = _at
N_KEPT = TABS["id64"][0] + TABS["id64"][1]


UNITS1 = [0] + [2] * 8 + [1] * 8
UNITS2 = [0] + [2] * 5 + [1] * 6
START_UNITS = 16


def lo_signal(n):
    dve = sum((min(n + 1, n1) - n0) // 2 for n0, n1 in ((B1_UP, B2), (B2_UP, N_SLABS)) if n >= n0)
    if n % 2 and (B1_UP <= n < B2 or n >= B2_UP):
        return True, dve
    return False, n + 1 - dve


def lo_per(n, per):
    return per if n < B1_UP or B2 <= n < B2_UP else per // 2


def tables():
    t = np.zeros((P, NTABS), np.float32)

    def put(name, a):
        at, n = TABS[name]
        t[:, at:at + n] = np.asarray(a, np.float64).reshape(P, n)

    i = np.arange(P)
    row, col = i[:, None], i[None, :]
    same64 = row // 64 == col // 64
    put("ident", np.eye(P))
    put("ones", np.ones((P, P)))
    put("blk64", same64)
    put("strict", same64 & (row < col))
    put("incl", same64 & (row <= col))
    put("levels", np.stack([(row // (2 << l) == col // (2 << l)) & (row // (1 << l) < col // (1 << l))
                            for l in range(6)], 1))
    put("id64", np.concatenate([np.eye(64), np.eye(64)]))
    j = np.arange(S)[None, :]
    dist = (P + row) - j
    put("alibi", np.where(dist >= 0, -dist.astype(np.float64), -1e30))
    put("mfwd", np.where(dist >= 0, 0.0, -1e30))
    put("mbwd", np.where(j >= row, 0.0, -1e30))
    log_g = np.log1p(-np.exp2(-5.0 - np.arange(4)))
    q = np.arange(S)[None, :] - row
    put("retdecay", np.stack([np.where(q >= 0, np.exp(log_g[h] * np.maximum(q, 0)), 0.0) / 8.0
                              for h in range(4)], 1))
    put("tri", row <= col)
    n = np.arange(S)
    ang = 2 * np.pi * np.outer(n, n) / S
    cs = np.concatenate([np.cos(ang), np.sin(ang)], 1) / 16.0
    put("dft", cs.reshape(2, P, 512).transpose(1, 0, 2))
    return t


class Count:

    def __init__(self):
        self.n, self.i, self.per, self.last = {}, None, {}, None

    def up(self, sem):
        self.n[sem] = self.n.get(sem, 0) + 1
        v = self.n[sem]
        self.last = (sem, v if self.i is None else v + self.per.get(sem, 0) * self.i)
        return sem, 1

    @contextmanager
    def loop(self, eng, count, per):
        before = dict(self.n)
        with eng.Fori(0, count) as i:
            self.i, self.per = i, per
            yield i
        for sem in set(self.n) | set(per):
            a, b = before.get(sem, 0), self.n.get(sem, 0)
            assert b - a == per.get(sem, 0), (sem, b - a, per.get(sem, 0))
            self.n[sem] = a + (b - a) * count
        self.i, self.per, self.last = None, {}, None


class Semaphores:

    def __init__(self, nc, ctx):
        def new(name):
            return ctx.enter_context(nc.semaphore(name))

        self.w_landed = [new(f"w_landed{q}") for q in range(RING)]
        self.ada_landed = [new(f"ada_landed{q}") for q in range(2)]
        self.step = new("step")
        self.a_act = new("a_act")
        self.a_done = new("a_done")
        self.acc_ready = new("acc_ready")
        self.ada_sum = new("ada_sum")
        self.ada_used = new("ada_used")
        self.bonus_ready = new("bonus_ready")
        self.bonus_sum = new("bonus_sum")
        self.bt_ready = new("bt_ready")
        self.c_made = new("c_made")
        self.cact_ready = new("cact_ready")
        self.ccol = new("ccol")
        self.chain = new("chain")
        self.cl = new("cl")
        self.cl_used = new("cl_used")
        self.clx = new("clx")
        self.cols_landed = new("cols_landed")
        self.conv_landed = new("conv_landed")
        self.cw_ready = new("cw_ready")
        self.d_done = new("d_done")
        self.decays = new("decays")
        self.den_made = new("den_made")
        self.dft_done = new("dft_done")
        self.dft_out = new("dft_out")
        self.f_abs = new("f_abs")
        self.f_exp = new("f_exp")
        self.f_ln = new("f_ln")
        self.f_out = new("f_out")
        self.fh = new("fh")
        self.floor_made = new("floor_made")
        self.free_gate = new("free_gate")
        self.free_val = new("free_val")
        self.g_act = new("g_act")
        self.g_done = new("g_done")
        self.g_made = new("g_made")
        self.gate_act = new("gate_act")
        self.gate_tap = new("gate_tap")
        self.gates = new("gates")
        self.gn_mean = new("gn_mean")
        self.gn_ms = new("gn_ms")
        self.gn_sd = new("gn_sd")
        self.gn_var = new("gn_var")
        self.gs_hi = new("gs_hi")
        self.gs_lo = new("gs_lo")
        self.gt_ready = new("gt_ready")
        self.h_hi = new("h_hi")
        self.h_out = new("h_out")
        self.h_ready = new("h_ready")
        self.head_made = new("head_made")
        self.hi_ready = new("hi_ready")
        self.hms = new("hms")
        self.hsd = new("hsd")
        self.hsq = new("hsq")
        self.hsum = new("hsum")
        self.hval = new("hval")
        self.kept = new("kept")
        self.kh_ready = new("kh_ready")
        self.kk0 = new("kk0")
        self.kk_ms = new("kk_ms")
        self.kk_sd = new("kk_sd")
        self.kk_sq = new("kk_sq")
        self.kk_sum = new("kk_sum")
        self.kt_ready = new("kt_ready")
        self.l2v = new("l2v")
        self.lo2_ready = new("lo2_ready")
        self.lo_ready = new("lo_ready")
        self.lora_act = new("lora_act")
        self.m_out = new("m_out")
        self.m_ready = new("m_ready")
        self.masked = new("masked")
        self.mix_hi = new("mix_hi")
        self.mix_split = new("mix_split")
        self.mo_biased = new("mo_biased")
        self.mo_exp = new("mo_exp")
        self.mo_max = new("mo_max")
        self.mo_out = new("mo_out")
        self.mo_p = new("mo_p")
        self.mo_pt = new("mo_pt")
        self.mo_scores = new("mo_scores")
        self.mo_turned = new("mo_turned")
        self.mo_values = new("mo_values")
        self.ms_ready = new("ms_ready")
        self.mt = new("mt")
        self.mt_turned = new("mt_turned")
        self.mu1_ready = new("mu1_ready")
        self.out_landed = new("out_landed")
        self.p_exp = new("p_exp")
        self.p_made = new("p_made")
        self.qy = new("qy")
        self.qy_add = new("qy_add")
        self.ret_masked = new("ret_masked")
        self.ret_ms = new("ret_ms")
        self.ret_out = new("ret_out")
        self.ret_scores = new("ret_scores")
        self.ret_sd = new("ret_sd")
        self.ret_sq = new("ret_sq")
        self.ret_sum = new("ret_sum")
        self.ret_values = new("ret_values")
        self.rk_ready = new("rk_ready")
        self.rows_made = new("rows_made")
        self.rows_out = new("rows_out")
        self.rt_ready = new("rt_ready")
        self.rw_mixed = new("rw_mixed")
        self.rw_out = new("rw_out")
        self.rw_self = new("rw_self")
        self.sc1 = new("sc1")
        self.sc1_out = new("sc1_out")
        self.sc2 = new("sc2")
        self.sc2_out = new("sc2_out")
        self.sd_ready = new("sd_ready")
        self.slab_used = new("slab_used")
        self.sq_ready = new("sq_ready")
        self.sq_used = new("sq_used")
        self.t_ready = new("t_ready")
        self.tables1_landed = new("tables1_landed")
        self.tables2_landed = new("tables2_landed")
        self.tabs_landed = new("tabs_landed")
        self.turned = new("turned")
        self.turned_out = new("turned_out")
        self.tx = new("tx")
        self.u_done = new("u_done")
        self.u_out = new("u_out")
        self.u_ready = new("u_ready")
        self.val_tap = new("val_tap")
        self.wg_hi = new("wg_hi")
        self.wg_ready = new("wg_ready")
        self.wz = new("wz")
        self.x_landed = new("x_landed")
        self.x_made = new("x_made")
        self.x_ready = new("x_ready")
        self.y_full = new("y_full")
        self.y_gated = new("y_gated")
        self.y_out = new("y_out")
        self.y_ready = new("y_ready")
        self.yc = new("yc")
        self.yc_sq = new("yc_sq")
        self.z_act = new("z_act")
        self.z_done = new("z_done")


def build(nc, wstream, adastream, x_in, cols_in, conv_in, tabs_in, rw_in, wg_in, out):
    ctx = ExitStack()
    with ctx:
        sem = Semaphores(nc, ctx)
        used = [0]
        base = nc.sbuf_base if isinstance(nc.sbuf_base, int) else nc.sbuf_base()
        base = (base + 63) // 64 * 64
        total = nc.sbuf_bytes_remaining() if callable(nc.sbuf_bytes_remaining) else nc.sbuf_bytes_remaining

        def sb(name, shape, dt=F32, offset=None):
            size = (int(np.prod(shape[1:])) * 4 + 31) // 32 * 32
            if offset is None:
                offset = base + used[0]
                used[0] += size
                assert used[0] <= total - 64, (name, used[0], total)
            t = nc.alloc_sbuf_tensor_at(name, shape, dt, offset=offset)
            return t, offset

        raw, _ = sb("raw", [P, RING, SLAB])
        whi, _ = sb("whi", [P, RING, SLAB], F32R)
        wlo, _ = sb("wlo", [P, RING, SLAB], F32R)
        hhi, _ = sb("hhi", [P, KT, S], F32R)
        hlo, _ = sb("hlo", [P, KT, S], F32R)
        ada_raw, _ = sb("ada_raw", [P, 2, 2048])
        acc, _ = sb("acc", [P, 2, 2, 256])
        cols, _ = sb("cols", [P, NCOLS])
        conv, _ = sb("conv", [P, 2, NFF, 32])
        modc, _ = sb("modc", [P, 192])
        cact, _ = sb("cact", [P, 32])
        tabs, _ = sb("tabs", [P, N_KEPT])
        colA, _ = sb("colA", [P, 16])
        mu1, _ = sb("mu1", [P, 20])
        cw, _ = sb("cw", [P, 32])
        small, _ = sb("small", [P, 256])
        rstd, _ = sb("rstd", [P, S])
        pc, _ = sb("pc", [P, 16])
        gshi, gs_at = sb("gshi", [P, 2, 4, S], F32R)
        gslo, _ = sb("gslo", [P, 2, 4, S], F32R)
        xT, x_at = sb("xT", [P, KT, S])
        arena_at = base + used[0]
        arena, _ = sb("arena", [P, 15, 1024])
        gT = arena[:, 0:11, :].rearrange("p a (b s) -> p (a b) s", s=S)
        gsf, _ = sb("gs_pages", [P, 4, 1024], F32, offset=gs_at)

        psum = ctx.enter_context(nc.psum_tensor("psum", [P, 8, 512], F32))
        bank = [psum[:, b, :] for b in range(8)]

        def tab(name):
            a, n = TABS[name]
            return tabs[:, a:a + n]

        def col(name, i, n=1):
            return cols[:, COLS[name] + i:COLS[name] + i + n]

        ident, ones, blk64 = tab("ident"), tab("ones"), tab("blk64")

        def page(i):
            if i < 15:
                return arena[:, i, :]
            if i < 19:
                return xT[:, 4 * (i - 15):4 * (i - 14), :].rearrange("p a s -> p (a s)")
            return gsf[:, i - 19, :]

        def tiles(i):
            return page(i).rearrange("p (a s) -> p a s", s=S)

        def halves(i):
            return page(i).rearrange("p (a s) -> p a s", s=512)

        def pair(p):
            return psum[:, 2 * p:2 * p + 2, :].rearrange("p b (h s) -> p (b h) s", s=S)

        def flat(p):
            return psum[:, 2 * p:2 * p + 2, :].rearrange("p b s -> p (b s)")

        block = ctx.enter_context(nc.Block())

        def quarter(pg, h):
            return page(pg)[:, 512 * h:512 * h + 512].rearrange("p (m t) -> p m t", t=P)

        L1T, MT = quarter(13, 0), quarter(13, 1)
        G1T, G2T = quarter(14, 0), quarter(14, 1)
        TM, TT = quarter(11, 0), quarter(11, 1)
        UM, XM = quarter(12, 0), quarter(12, 1)
        WZ = quarter(2, 0)
        L2T = MT
        mstate = page(2)[:, 512:1024].rearrange("p (b t v) -> p b t v", b=2, v=64)
        FT = page(16).rearrange("p (t c j) -> p t c j", t=4, c=4)
        HM = page(17).rearrange("p (t c v) -> p t c v", t=4, c=4)
        scores = arena[:, 11:13, :].rearrange("p a n -> p (a n)")[:, 0:1536].rearrange("p (h n) -> p h n", n=384)
        mscores = xT[:, 4:12, :].rearrange("p a n -> p (a n)")[:, 0:1536].rearrange("p (h n) -> p h n", n=384)
        decayT = page(19).rearrange("p (h n) -> p h n", n=S)
        alibi = page(20)[:, 0:S]
        MOBA = [(7, 8, 9, 14), (10, 1, 5, 2)]
        MIXED1 = [13, 15, 14, 2]

        def rows(h):
            return slice(64 * h, 64 * h + 64)

        def pe_mix1(pe, st, mm, part, finish):
            def group(g, k0=0, k1=GS):
                part(g * GS, g % 2, k0, k1, "tok" if g in (G_TV, G_MV0, G_MV1) else None,
                     (sem.h_ready, 0) if g == 0 else None)
                if k1 == GS:
                    st["free"][g % 2] = (sem.rw_mixed, g + 1) if g < 4 else (sem.kept, g - 3)

            for g in range(4):
                group(g, 0, 4)
                if UNITS1[g] == 2:
                    finish()
                group(g, 4, 8)
                if UNITS1[g]:
                    finish()

            pe.wait_ge(sem.tables1_landed, 64)
            lo = tiles(3)
            pe.wait_ge(sem.lora_act, 1)
            for j in range(4):
                ins = mm(pair(2)[:, j, :], page(21)[:, j * P:(j + 1) * P], lo[:, 0, :], j % 2 == 0, True)
                if j == 3:
                    ins.then_inc(sem.z_done, 1)
            group(G_TQK, 0, 4)
            finish()
            pe.wait_ge(sem.z_act, 1)
            for j in range(4):
                ins = mm(pair(2)[:, j, :], page(21)[:, 512 + j * P:512 + (j + 1) * P], lo[:, 1, :], j % 2 == 0, True)
                if j == 3:
                    ins.then_inc(sem.a_done, 1)
            group(G_TQK, 4, 8)
            finish()
            pe.wait_ge(sem.a_act, 1)
            pe.wait_ge(sem.lora_act, 2)
            for j in range(4):
                for kk in range(2):
                    ins = mm(pair(2)[:, j, :], page(22)[:, kk * 512 + j * P:kk * 512 + (j + 1) * P],
                       lo[:, 2 + kk, :], j % 2 == 0 and kk == 0, kk == 1)
                    if j == 3 and kk:
                        ins.then_inc(sem.g_done, 1)
            pe.wait_ge(sem.g_act, 1)
            pe.wait_ge(sem.kk_sq, 1)
            for b in range(2):
                ins = mm(bank[4 + b], blk64, halves(11)[:, b, :], True, True)
                if b:
                    ins.then_inc(sem.kk_sum, 1)
            pe.wait_ge(sem.rk_ready, 1)
            pe.wait_ge(sem.kk_ms, 1)
            for b in range(2):
                ins = mm(bank[4 + b], blk64, halves(13)[:, b, :], True, True)
                if b:
                    ins.then_inc(sem.bonus_sum, 1)

            turned = 0
            for src, ready_ in ((2, sem.bonus_ready), (4, sem.kt_ready), (5, sem.bt_ready), (1, sem.kh_ready)):
                pe.wait_ge(ready_, 1)
                for b in range(2):
                    if turned >= 3:
                        pe.wait_ge(sem.turned_out, turned - 2)
                    o = bank[(6, 4, 5)[turned % 3]]
                    for j in range(4):
                        ins = nc.tensor.transpose(o[:, j * P:(j + 1) * P], tiles(src)[:, j, b * P:(b + 1) * P], ident)
                        if j == 3:
                            ins.then_inc(sem.turned, 1)
                    turned += 1

            fillers = [(G_TV + t // 2, 4 * (t % 2) + s) for t in range(4) for s in range(4)]

            def fill(k=1):
                for _ in range(k):
                    if fillers:
                        g, s = fillers.pop(0)
                        group(g, s, s + 1)

            pe.wait_ge(sem.rt_ready, 1)
            pe.wait_ge(sem.turned_out, 8)
            for t in range(4):
                def scores_of(src, banks, signal):
                    for h in range(2):
                        for kind, right in enumerate((4, 0)):
                            for b in range(2):
                                tok = slice(b * P, (b + 1) * P)
                                ins = mm(banks[h][:, kind * S + b * P:kind * S + (b + 1) * P],
                                   tiles(src)[rows(h), t, tok], tiles(right)[rows(h), t, tok], True, True)
                                if h and kind and b:
                                    ins.then_inc(signal, 1)

                if t:
                    pe.wait_ge(sem.qy_add, t)
                    pe.wait_ge(sem.h_out, t)
                    pe.wait_ge(sem.f_out, t)
                scores_of(5, (bank[4], bank[5]), sem.sc1)
                pe.wait_ge(sem.sc1_out, t + 1)
                scores_of(1, (bank[6], bank[4]), sem.sc2)
                fill()
                pe.wait_ge(sem.sc2_out, t + 1)
                for m in range(4):
                    b, h = divmod(m, 2)
                    ins = mm(bank[5][:, m * 64:(m + 1) * 64], L2T[:, m, :],
                       halves(7)[:, b, t * P + h * 64:t * P + h * 64 + 64], True, True)
                    if m == 3:
                        ins.then_inc(sem.l2v, 1)
                pe.wait_ge(sem.mt, 6 * t + 1)
                for m in range(4):
                    ins = nc.tensor.transpose(bank[6][:, m * P:(m + 1) * P], MT[:, m, :], ident)
                    if m == 3:
                        ins.then_inc(sem.mt_turned, 1)
                for l in range(1, 6):
                    pe.wait_ge(sem.mt, 6 * t + l + 1)
                    pe.wait_ge(sem.t_ready, 6 * t + l)
                    for m in range(4):
                        ins = mm(bank[4][:, m * P:(m + 1) * P], MT[:, m, :], TM[:, m, :], True, True)
                        if m == 3:
                            ins.then_inc(sem.u_done, 1)
                    if l in (1, 3, 5):
                        fill()
                    pe.wait_ge(sem.u_out, 5 * t + l)
                    if l < 5:
                        for m in range(4):
                            mm(bank[5][:, m * P:(m + 1) * P], TT[:, m, :], UM[:, m, :], True, True)
                    for m in range(4):
                        ins = mm(bank[6][:, m * P:(m + 1) * P], UM[:, m, :], TT[:, m, :], True, True)
                        if m == 3:
                            ins.then_inc(sem.d_done, 1)
                pe.wait_ge(sem.t_ready, 6 * t + 6)
                pe.wait_ge(sem.x_made, t + 1)
                for m in range(4):
                    ins = mm(bank[4][:, m * P:(m + 1) * P], TT[:, m, :], XM[:, m, :], True, True)
                    if m == 3:
                        ins.then_inc(sem.tx, 1)
                finish()
                pe.wait_ge(sem.wz, t + 1)
                for h in range(2):
                    for b in range(2):
                        m = 2 * b + h
                        vt = halves(7)[:, b, t * P + h * 64:t * P + h * 64 + 64]
                        mm(bank[5][rows(h), b * P:(b + 1) * P], WZ[:, m, 0:64], G1T[:, m, :], b == 0)
                        mm(bank[5][rows(h), S + b * P:S + (b + 1) * P], WZ[:, m, 64:128], G1T[:, m, :], False, False)
                        ins = mm(bank[5][rows(h), S + b * P:S + (b + 1) * P], vt, G2T[:, m, :], False, True)
                        if h and b:
                            ins.then_inc(sem.qy, 1)
                for cc in range(2):
                    o = bank[(6, 4)[cc]]
                    r = rows(cc)
                    for h in range(2):
                        for b in range(2):
                            m = 2 * b + h
                            ch = slice(t * P + h * 64, t * P + h * 64 + 64)
                            bt, kh, vt = (halves(pg)[r, b, ch] for pg in (9, 10, 7))
                            mm(o[rows(h), b * 64:b * 64 + 64], WZ[r, m, 0:64], bt, b == 0)
                            mm(o[rows(h), P + b * 64:P + b * 64 + 64], bt, WZ[r, m, 64:128], False, False)
                            ins = mm(o[rows(h), P + b * 64:P + b * 64 + 64], kh, vt, False, True)
                            if cc and h and b:
                                ins.then_inc(sem.fh, 1)

            for c in range(1, 4):
                pe.wait_ge(sem.m_ready, c)
                if c == 1:
                    pe.wait_ge(sem.qy_add, 4)
                    pe.wait_ge(sem.h_out, 4)
                    pe.wait_ge(sem.f_out, 4)
                for h in range(2):
                    for t in range(4):
                        m = mstate[rows(h), (c - 1) % 2, t, :]
                        ins = mm(bank[4 + h][rows(h), t * 64:t * 64 + 64], m,
                           tiles(0)[rows(h), t, c * 64:c * 64 + 64], True, True)
                        if c == 3 and h and t == 3:
                            ins.then_inc(sem.chain, 1)
                        if c < 3:
                            ins = mm(bank[4 + h][rows(h), S + t * 64:S + t * 64 + 64], FT[rows(h), t, c, :], m, True, True)
                            if h and t == 3:
                                ins.then_inc(sem.chain, 1)
                group(G_MQ0 + (c - 1) // 2, 4 * ((c - 1) % 2), 4 * ((c - 1) % 2) + 4)
                finish()
            pe.wait_ge(sem.y_full, 1)
            for b in range(2):
                ins = mm(bank[4 + b], blk64, halves(15)[:, b, :], True, True)
                if b:
                    ins.then_inc(sem.gn_mean, 1)
            group(G_MK0, 4, 8)
            finish()
            pe.wait_ge(sem.yc_sq, 1)
            for b in range(2):
                ins = mm(bank[4 + b], blk64, halves(4)[:, b, :], True, True)
                if b:
                    ins.then_inc(sem.gn_var, 1)
            group(G_MV0)
            finish()

            pe.wait_ge(sem.kept, 3)
            for h in range(4):
                o, r, tq = bank[(6, 4, 5, 6)[h]], rows(h % 2), h // 2
                if h == 1:
                    pe.wait_ge(sem.gn_ms, 1)
                if h == 3:
                    pe.wait_ge(sem.ret_masked, 1)
                mm(o[:, 0:S], tiles(18)[r, 2 + tq, 0:P], tiles(18)[r, tq, :], True)
                mm(o[:, S:S + P], tiles(18)[r, 2 + tq, P:S], tiles(18)[r, tq, P:S], True, True).then_inc(sem.ret_scores, 1)
            group(G_MQ1, 0, 4)
            pe.wait_ge(sem.ret_masked, 4)
            for h in range(4):
                o = bank[4 + h // 2][:, (h % 2) * S:(h % 2 + 1) * S]
                mm(o, halves(21)[:, 0, h * P:(h + 1) * P], scores[:, h, 0:S], h % 2 == 0, False)
                ins = mm(o[:, P:S], halves(21)[:, 1, h * P:(h + 1) * P], scores[:, h, S:S + P], False, True)
                if h == 3:
                    ins.then_inc(sem.ret_values, 1)
            group(G_MQ1, 4, 8)
            finish()
            pe.wait_ge(sem.ret_sq, 1)
            for b in range(2):
                ins = mm(bank[4 + b], ones, halves(14)[:, b, :], True, True)
                if b:
                    ins.then_inc(sem.ret_sum, 1)

            def moba_scores(n):
                q, k, _, _ = MOBA[n]
                for h in range(4):
                    o = bank[(6, 4, 5, 6)[h]]
                    if h == 0:
                        pe.wait_ge(sem.kept, 5 + 3 * n)
                        pe.wait_ge(sem.ret_masked if n == 0 else sem.mo_out, 4 if n == 0 else 1)
                    if h == 1 and n == 0:
                        pe.wait_ge(sem.ret_ms, 1)
                    if h == 3:
                        pe.wait_ge(sem.mo_biased, 4 * n + 1)
                    mm(o[:, 0:P], tiles(q)[:, h, 0:P], tiles(k)[:, h, 0:P], True)
                    mm(o[:, P:P + S], tiles(q)[:, h, P:S], tiles(k)[:, h, :], True, True).then_inc(sem.mo_scores, 1)

            def moba_turn(n):
                pe.wait_ge(sem.mo_p, n + 1)
                for h in range(4):
                    o = bank[(6, 4, 5, 6)[h]]
                    if h == 3:
                        pe.wait_ge(sem.mo_pt, 4 * n + 1)
                    for i in range(3):
                        ins = nc.tensor.transpose(o[:, i * P:(i + 1) * P], mscores[:, h, i * P:(i + 1) * P], ident)
                    ins.then_inc(sem.mo_turned, 1)

            def moba_values(n):
                v = halves(MOBA[n][2])
                pe.wait_ge(sem.mo_pt, 4 * n + 4)
                pe.wait_ge(sem.kept, 6 + 3 * n)
                for h in range(4):
                    o = bank[4 + h // 2][:, (h % 2) * S:(h % 2 + 1) * S]
                    mm(o, v[:, 0, h * P:(h + 1) * P], scores[:, h, 0:S], h % 2 == 0, False)
                    ins = mm(o[:, P:S], v[:, 1, h * P:(h + 1) * P], scores[:, h, S:S + P], False, True)
                    if h == 3:
                        ins.then_inc(sem.mo_values, 1)

            moba_scores(0)
            group(G_MK1)
            finish()
            moba_turn(0)
            group(G_MV1, 0, 4)
            moba_values(0)
            group(G_MV1, 4, 8)
            finish()
            moba_scores(1)
            moba_turn(1)
            moba_values(1)

        def act_mix1(act, copy, fn, his):
            def kept(g, dst, f=ACT.Copy, scale=1.0):
                act.wait_ge(sem.slab_used, (g + 1) * GS)
                nc.scalar.activation(page(dst), flat(g % 2), f, scale=scale).then_inc(sem.kept, 1)

            act.wait_ge(sem.mu1_ready, 1)
            for g in range(4):
                his(g * GS + 3, (g + 1) * GS + 3)
                act.wait_ge(sem.slab_used, (g + 1) * GS)
                for j in range(4):
                    c = 4 * g + j
                    ins = fn(tiles(g)[:, j, :], pair(g % 2)[:, j, :], ACT.Identity, scale=mu1[:, c:c + 1])
                    if j == 3:
                        ins.then_inc(sem.rw_self, 1)
            act.wait_ge(sem.rw_mixed, 4)
            fn(tiles(3)[:, 0, :], tiles(3)[:, 0, :], ACT.Tanh).then_inc(sem.lora_act, 1)
            fn(halves(3)[:, 1, :], halves(3)[:, 1, :], ACT.Sigmoid).then_inc(sem.lora_act, 1)
            act.wait_ge(sem.z_done, 1)
            for j in range(4):
                ins = fn(tiles(4)[:, j, :], pair(2)[:, j, :], ACT.Sigmoid, bias=col("w0", j))
                if j == 3:
                    ins.then_inc(sem.z_act, 1)
            his(G_TQK * GS + 3, G_TQK * GS + 7)
            act.wait_ge(sem.a_done, 1)
            for j in range(4):
                ins = fn(tiles(5)[:, j, :], pair(2)[:, j, :], ACT.Sigmoid, bias=col("a0", j))
                if j == 3:
                    ins.then_inc(sem.a_act, 1)
            act.wait_ge(sem.cl, 1)
            fn(page(8), page(7), ACT.Exp).then_inc(sem.decays, 1)
            fn(page(9), page(7), ACT.Exp, scale=-1.0).then_inc(sem.decays, 1)
            act.wait_ge(sem.clx, 1)
            fn(page(4), page(4), ACT.Exp).then_inc(sem.decays, 1)
            his(G_TQK * GS + 7, G_TQK * GS + 11)
            kept(G_TQK, 18)
            act.wait_ge(sem.g_done, 1)
            copy(page(6), flat(2)).then_inc(sem.g_act, 1)
            act.wait_ge(sem.kk0, 1)
            fn(page(11), page(10), ACT.Square).then_inc(sem.kk_sq, 1)
            act.wait_ge(sem.kk_ms, 1)
            fn(page(11), page(11), ACT.Sqrt).then_inc(sem.kk_sd, 1)
            for n in range(8):
                act.wait_ge(sem.turned, n + 1)
                if n == 2:
                    act.wait_ge(sem.cl_used, 1)
                if n == 4:
                    act.wait_ge(sem.kh_ready, 1)
                copy(halves(7 + n // 2)[:, n % 2, :], bank[(6, 4, 5)[n % 3]]).then_inc(sem.turned_out, 1)
            for t in range(4):
                n0 = G_TV * GS + 4 * t + 3
                his(n0, n0 + 1)
                for l in range(1, 6):
                    if l in (1, 3, 5):
                        his(n0 + (l + 1) // 2, n0 + (l + 1) // 2 + 1)
                    act.wait_ge(sem.u_done, 5 * t + l)
                    copy(UM, bank[4].rearrange("p (m t) -> p m t", t=P)).then_inc(sem.u_out, 1)
                if t == 2:
                    kept(G_TV, 21)
                act.wait_ge(sem.tx, t + 1)
                copy(WZ, bank[4].rearrange("p (m t) -> p m t", t=P), scale=-1.0).then_inc(sem.wz, 1)
                act.wait_ge(sem.qy, t + 1)
                copy(tiles(15)[:, t, :], bank[5][:, S:2 * S]).then_inc(sem.y_out, 1)
                act.wait_ge(sem.fh, t + 1)
                for cc in range(2):
                    ins = copy(HM[:, t, cc::2, :], bank[(6, 4)[cc]][:, P:2 * P].rearrange("p (b v) -> p b v", v=64))
                    if cc:
                        ins.then_inc(sem.h_out, 1)
            act.wait_ge(sem.slab_used, G_MQ0 * GS)
            kept(G_TG, 22, ACT.Silu)
            for c in range(1, 4):
                n0 = G_MQ0 * GS + 4 * (c - 1) + 3
                his(n0, n0 + 4)
                if c == 3:
                    kept(G_MQ0, 7, scale=P ** -0.5)
            his(G_MK0 * GS + 7, G_MK0 * GS + 11)
            act.wait_ge(sem.yc, 1)
            fn(page(4), page(15), ACT.Square).then_inc(sem.yc_sq, 1)
            kept(G_MK0, 8)
            his(G_MV0 * GS + 3, G_MV0 * GS + 11)
            act.wait_ge(sem.gn_ms, 1)
            fn(page(4), page(4), ACT.Sqrt).then_inc(sem.gn_sd, 1)
            kept(G_MV0, 9)
            his(G_MQ1 * GS + 3, G_MQ1 * GS + 7)
            act.wait_ge(sem.ret_values, 1)
            copy(page(13), flat(2))
            nc.scalar.activation(page(14), flat(2), ACT.Square).then_inc(sem.ret_sq, 1)
            his(G_MQ1 * GS + 7, G_MQ1 * GS + 11)
            kept(G_MQ1, 10, scale=P ** -0.5)
            act.wait_ge(sem.ret_ms, 1)
            fn(page(14), page(14), ACT.Sqrt).then_inc(sem.ret_sd, 1)

            def moba_exp(n):
                act.wait_ge(sem.mo_max, n + 1)
                for h in range(4):
                    for ib in range(2):
                        s = mscores[:, h, P * ib:P + S * ib]
                        c = 4 * ib + h
                        ins = nc.scalar.activation(s, s, ACT.Exp, bias=small[:, c:c + 1],
                                                  accum_out=small[:, 8 + c:9 + c])
                        if h == 3 and ib:
                            ins.then_inc(sem.mo_exp, 1)

            def moba_turned(n, h):
                act.wait_ge(sem.mo_turned, 4 * n + h + 1)
                copy(scores[:, h, :], bank[(6, 4, 5, 6)[h]][:, 0:384]).then_inc(sem.mo_pt, 1)

            def moba_out(n):
                act.wait_ge(sem.mo_values, n + 1)
                copy(page(MOBA[n][3]), flat(2)).then_inc(sem.mo_out, 1)

            his(G_MK1 * GS + 3, G_MK1 * GS + 7)
            moba_exp(0)
            his(G_MK1 * GS + 7, G_MK1 * GS + 11)
            kept(G_MK1, 1)
            for h in range(4):
                moba_turned(0, h)
            his(G_MV1 * GS + 3, G_MV1 * GS + 7)
            act.wait_ge(sem.ret_out, 1)
            moba_out(0)
            his(G_MV1 * GS + 7, G_MV1 * GS + 11)
            kept(G_MV1, 5)
            moba_exp(1)
            for h in range(4):
                moba_turned(1, h)
            moba_out(1)
            for k, pg in enumerate(MIXED1):
                act.wait_ge(*((sem.ret_out, 1), (sem.rw_out, 1), (sem.mo_out, 1), (sem.mo_out, 2))[k])
                copy(hhi[:, 4 * k:4 * k + 4, :], tiles(pg)).then_inc(sem.mix_hi, 1)

        def dve_mix1(dve, at, st, tt, ts, stt, unit, modulation):
            V = nc.vector
            ts(mu1[:, 0:16], col("mu", 0, 16), -1.0, 1.0, ALU.mult, ALU.add).then_inc(*at.up(sem.step))
            ts(mu1[:, 16:20], col("k_a", 0, 4), -1.0, 1.0, ALU.mult, ALU.add).then_inc(*at.up(sem.mu1_ready))
            for g in range(4):
                for _ in range(UNITS1[g]):
                    unit()
                dve.wait_ge(sem.rw_self, g + 1)
                for j in range(4):
                    c = 4 * g + j
                    t = tiles(g)[:, j, :]
                    stt(t[:, 1:S], pair(g % 2)[:, j, 0:S - 1], col("mu", c), t[:, 1:S], ALU.mult, ALU.add).then_inc(*at.up(sem.rw_mixed if j == 3 else sem.step))
            unit()
            V.memset(page(12), 1.0).then_inc(*at.up(sem.step))
            one = at.last
            for j in range(4):
                ts(tiles(10)[:, j, :], tiles(1)[:, j, :], col("k_k", j), None, ALU.mult).then_inc(*at.up(sem.kk0 if j == 3 else sem.step))
            dve.wait_ge(*one)
            V.memset(page(12).rearrange("p (c s) -> p c s", s=64)[:, :, 0:1], 0.0).then_inc(*at.up(sem.step))
            dve.wait_ge(sem.z_act, 1)
            ts(page(4), page(4), -EXP_HALF, None, ALU.mult).then_inc(*at.up(sem.step))
            dve.wait_ge(*at.last)
            V.tensor_tensor_scan(page(7), page(12), page(4), 0.0, ALU.mult, ALU.add).then_inc(*at.up(sem.cl))
            dve.wait_ge(*at.last)
            tt(page(4), page(7), page(4), ALU.subtract).then_inc(*at.up(sem.clx))
            unit()
            dve.wait_ge(sem.a_act, 1)
            for j in range(4):
                ts(tiles(12)[:, j, :], tiles(5)[:, j, :], col("k_a", j), mu1[:, 16 + j:17 + j], ALU.mult, ALU.add).then_inc(*at.up(sem.step))
            dve.wait_ge(*at.last)
            tt(page(1), page(1), page(12), ALU.mult).then_inc(*at.up(sem.step))
            dve.wait_ge(*at.last)
            tt(page(13), page(0), page(1), ALU.mult).then_inc(*at.up(sem.step))
            dve.wait_ge(*at.last)
            for j in range(4):
                ts(tiles(13)[:, j, :], tiles(13)[:, j, :], col("r_k", j), None, ALU.mult).then_inc(*at.up(sem.rk_ready if j == 3 else sem.step))
            dve.wait_ge(sem.kk_sum, 1)
            ts(page(11), flat(2), 1e-24, None, ALU.max).then_inc(*at.up(sem.kk_ms))
            dve.wait_ge(sem.decays, 3)
            V.tensor_copy(pc[:].rearrange("p (t c) -> p t c", c=4),
                               tiles(8).rearrange("p t (c s) -> p t c s", s=64)[:, :, :, 63]).then_inc(*at.up(sem.cl_used))
            tt(page(0), page(0), page(8), ALU.mult).then_inc(*at.up(sem.rt_ready))
            dve.wait_ge(sem.kk_sd, 1)
            V.reciprocal(page(11), page(11)).then_inc(*at.up(sem.step))
            dve.wait_ge(*at.last)
            tt(page(10), page(10), page(11), ALU.mult).then_inc(*at.up(sem.step))
            dve.wait_ge(*at.last)
            tt(page(4), page(10), page(4), ALU.mult).then_inc(*at.up(sem.kt_ready))
            dve.wait_ge(sem.bonus_sum, 1)
            tt(page(3), flat(2), page(2), ALU.mult).then_inc(*at.up(sem.bonus_ready))
            tt(page(5), page(5), page(10), ALU.mult).then_inc(*at.up(sem.step))
            dve.wait_ge(*at.last)
            tt(page(5), page(5), page(9), ALU.mult).then_inc(*at.up(sem.bt_ready))
            tt(page(1), page(1), page(9), ALU.mult).then_inc(*at.up(sem.kh_ready))

            def masked(h, o, src, mask):
                return tt(o.rearrange("p (b h) t -> p b h t", h=2)[:, :, h, :],
                          src.rearrange("p (b t) -> p b t", t=P),
                          tab(mask).unsqueeze(1).broadcast_to([P, 2, P]), ALU.mult)

            def level(l):
                return tabs[:, TABS["levels"][0] + l * P:TABS["levels"][0] + (l + 1) * P
                            ].unsqueeze(1).broadcast_to([P, 4, P])

            eye = ident.unsqueeze(1).broadcast_to([P, 4, P])
            for t in range(4):
                unit()
                dve.wait_ge(sem.sc1, t + 1)
                for h in range(2):
                    masked(h, L1T, bank[4 + h][:, 0:S], "strict").then_inc(*at.up(sem.step))
                    masked(h, G1T, bank[4 + h][:, S:2 * S], "incl").then_inc(*at.up(sem.sc1_out if h else sem.step))
                dve.wait_ge(sem.sc2, t + 1)
                for h, bk in ((0, bank[6]), (1, bank[4])):
                    masked(h, L2T, bk[:, 0:S], "strict").then_inc(*at.up(sem.step))
                    masked(h, G2T, bk[:, S:2 * S], "incl").then_inc(*at.up(sem.sc2_out if h else sem.step))
                dve.wait_ge(sem.l2v, t + 1)
                V.tensor_copy(XM[:, :, 64:128], bank[5][:, 0:S].rearrange("p (m v) -> p m v", v=64)).then_inc(*at.up(sem.step))
                V.tensor_copy(XM[:, :, 0:64].rearrange("p (b h) v -> p b h v", h=2),
                                   halves(8)[:, :, t * P:(t + 1) * P].rearrange("p b (h v) -> p b h v", h=2)).then_inc(*at.up(sem.x_made))
                tt(MT, L1T, level(0), ALU.mult).then_inc(*at.up(sem.mt))
                dve.wait_ge(*at.last)
                tt(TT, eye, MT, ALU.subtract).then_inc(*at.up(sem.step))
                dve.wait_ge(sem.mt_turned, t + 1)
                tt(TM, eye, bank[6].rearrange("p (m t) -> p m t", t=P), ALU.subtract).then_inc(*at.up(sem.t_ready))
                for l in range(1, 6):
                    if l > 1:
                        dve.wait_ge(sem.u_done, 5 * t + l - 1)
                    else:
                        dve.wait_ge(*at.last)
                    tt(MT, L1T, level(l), ALU.mult).then_inc(*at.up(sem.mt))
                    dve.wait_ge(sem.d_done, 5 * t + l)
                    if l < 5:
                        tt(TM, TM, bank[5].rearrange("p (m t) -> p m t", t=P), ALU.subtract).then_inc(*at.up(sem.step))
                    tt(TT, TT, bank[6].rearrange("p (m t) -> p m t", t=P), ALU.subtract).then_inc(*at.up(sem.t_ready))
                dve.wait_ge(sem.y_out, t + 1)
                tt(tiles(0)[:, t, :], tiles(0)[:, t, :], bank[5][:, 0:S], ALU.add).then_inc(*at.up(sem.qy_add))
                dve.wait_ge(sem.h_out, t + 1)
                for cc in range(2):
                    tt(FT[:, t, cc::2, :], bank[(6, 4)[cc]][:, 0:P].rearrange("p (b j) -> p b j", j=64),
                       tab("id64").unsqueeze(1).broadcast_to([P, 2, 64]), ALU.add).then_inc(*at.up(sem.f_out if cc else sem.step))

            pcv = pc[:].rearrange("p (t c) -> p t c", c=4)

            def decayed(c, src):
                tt(mstate[:, c % 2, :, :], src, pcv[:, :, c:c + 1].broadcast_to([P, 4, 64]), ALU.mult).then_inc(*at.up(sem.m_ready))

            dve.wait_ge(sem.h_out, 4)
            decayed(0, HM[:, :, 0, :])
            for c in range(1, 4):
                dve.wait_ge(sem.chain, c)
                for h in range(2):
                    r, ps = rows(h), bank[4 + h][rows(h), :].rearrange("p (k t v) -> p k t v", k=2, v=64)
                    y = tiles(15)[r, :, c * 64:c * 64 + 64]
                    if c == 1 and h == 0:
                        dve.wait_ge(sem.y_out, 4)
                    if c < 3:
                        tt(mstate[r, c % 2, :, :], ps[:, 1, :, :], HM[r, :, c, :], ALU.add).then_inc(*at.up(sem.step))
                    tt(y, ps[:, 0, :, :], y, ALU.add).then_inc(*at.up(sem.y_full if c == 3 and h else sem.step))
                if c < 3:
                    dve.wait_ge(*at.last)
                    decayed(c, mstate[:, c % 2, :, :])
                unit()
            dve.wait_ge(sem.gn_mean, 1)
            stt(page(15), flat(2), -1.0 / 64, page(15), ALU.mult, ALU.add).then_inc(*at.up(sem.yc))
            unit()
            dve.wait_ge(sem.gn_var, 1)
            ts(page(4), flat(2), 1.0 / 64, 64e-5, ALU.mult, ALU.add).then_inc(*at.up(sem.gn_ms))
            unit()
            dve.wait_ge(sem.gn_sd, 1)
            V.reciprocal(page(4), page(4)).then_inc(*at.up(sem.step))
            dve.wait_ge(*at.last)
            tt(page(15), page(15), page(4), ALU.mult).then_inc(*at.up(sem.step))
            dve.wait_ge(*at.last)
            for j in range(4):
                y = tiles(15)[:, j, :]
                ts(y, y, col("ln_w", j), col("ln_b", j), ALU.mult, ALU.add).then_inc(*at.up(sem.step))
            dve.wait_ge(*at.last)
            tt(page(15), page(15), page(3), ALU.add).then_inc(*at.up(sem.step))
            dve.wait_ge(*at.last)
            tt(page(15), page(15), page(6), ALU.mult).then_inc(*at.up(sem.rw_out))

            for h in range(4):
                o = bank[(6, 4, 5, 6)[h]]
                dve.wait_ge(sem.ret_scores, h + 1)
                tt(scores[:, h, 0:S], o[:, 0:S], decayT[:, h, :], ALU.mult).then_inc(*at.up(sem.step))
                tt(scores[:, h, S:S + P], o[:, S:S + P], decayT[:, h, 0:P], ALU.mult).then_inc(*at.up(sem.ret_masked))
            unit()
            dve.wait_ge(sem.ret_sum, 1)
            ts(page(14), flat(2), 1.0 / P, EPS, ALU.mult, ALU.add).then_inc(*at.up(sem.ret_ms))

            def moba_bias(n):
                for h in range(4):
                    o = bank[(6, 4, 5, 6)[h]]
                    slope = 2.0 ** -(4 * n + h + 1)
                    dve.wait_ge(sem.mo_scores, 4 * n + h + 1)
                    stt(mscores[:, h, 0:P], alibi[:, P:S], slope, o[:, 0:P], ALU.mult, ALU.add).then_inc(*at.up(sem.step))
                    stt(mscores[:, h, P:P + S], alibi, slope, o[:, P:P + S], ALU.mult, ALU.add).then_inc(*at.up(sem.mo_biased))
                dve.wait_ge(*at.last)
                V.tensor_reduce(small[:, 0:4], mscores[:, :, 0:P], AX_X, ALU.max).then_inc(*at.up(sem.step))
                V.tensor_reduce(small[:, 4:8], mscores[:, :, P:P + S], AX_X, ALU.max).then_inc(*at.up(sem.step))
                dve.wait_ge(*at.last)
                ts(small[:, 0:8], small[:, 0:8], -1.0, None, ALU.mult).then_inc(*at.up(sem.mo_max))

            def moba_norm(n):
                dve.wait_ge(sem.mo_exp, n + 1)
                V.reciprocal(small[:, 8:16], small[:, 8:16]).then_inc(*at.up(sem.step))
                dve.wait_ge(*at.last)
                for h in range(4):
                    for ib in range(2):
                        s = mscores[:, h, P * ib:P + S * ib]
                        c = 8 + 4 * ib + h
                        ts(s, s, small[:, c:c + 1], None, ALU.mult).then_inc(*at.up(sem.mo_p if h == 3 and ib else sem.step))

            moba_bias(0)
            dve.wait_ge(sem.ret_sd, 1)
            V.reciprocal(page(14), page(14)).then_inc(*at.up(sem.step))
            dve.wait_ge(*at.last)
            tt(page(13), page(13), page(14), ALU.mult).then_inc(*at.up(sem.step))
            dve.wait_ge(*at.last)
            dve.wait_ge(sem.kept, 3)
            tt(page(13), page(13), page(22), ALU.mult).then_inc(*at.up(sem.ret_out))
            moba_norm(0)
            unit()
            unit()
            dve.wait_ge(sem.mo_out, 1)
            moba_bias(1)
            moba_norm(1)
            for k, pg in enumerate(MIXED1):
                dve.wait_ge(sem.mix_hi, k + 1)
                tt(hlo[:, 4 * k:4 * k + 4, :], tiles(pg), hhi[:, 4 * k:4 * k + 4, :].bitcast(F32),
                   ALU.subtract).then_inc(*at.up(sem.mix_split))

        MQ, MK, MV, MU, MG, MY, MF = 0, 1, (2, 3), (4, 5), (6, 7), (8, 9), (10, 11)
        ORDER2 = ("q", "k", "v0", "u0", "v1", "u1", "g0", "g1")
        KEPT2 = {"q": MQ, "k": MK, "v0": MV[0], "v1": MV[1], "u0": MU[0], "u1": MU[1], "g0": MG[0], "g1": MG[1]}
        MIXED2 = (MF[0], MF[1], MY[0], MY[1])

        def kept2(name):
            return 9 + ORDER2.index(name) + 1

        wg_hi, wg_lo = gslo[:, 0, 0, :], gslo[:, 0, 1, :]
        dft = halves(19)
        gate_tok = page(22)[:, 0:256].rearrange("p (k b c) -> p k b c", k=2, b=2)
        gate_in = page(22)[:, 512:544].rearrange("p (b c) -> p b c", c=16)
        f_min = page(22)[:, 544:560].rearrange("p (b c) -> p b c", c=8)
        f_abs = page(22)[:, 560:576].rearrange("p (b c) -> p b c", c=8)
        row_c, row_m, row_b, row_s = (tiles(14)[:, k, :] for k in range(4))
        FWD, BWD, BOTH = slice(0, 32), slice(32, 64), slice(0, 64)
        ccol = pc[:].rearrange("p (b r) -> p b r", r=8)
        pf0, pf1 = page(21)[:, 0:256], page(21)[:, 256:384]
        pb0, pb1 = page(21)[:, 384:512], page(21)[:, 512:768]
        PARTS = ((pf0, 0, slice(0, S), 0), (pf1, 1, slice(P, S), 0), (pb1, 1, slice(0, S), 1), (pb0, 0, slice(0, P), 1))
        inv = page(22)[:, 0:512]
        floor_ = page(22)[:, 512:1024]
        hsq, hrms = page(13)[:, 0:512], page(13)[:, 512:768]
        mask_f, mask_b = page(20)[:, S:2 * S], page(20)[:, 0:S]

        def pe_mix2(pe, st, mm, part, finish):
            def slot(g, s):
                part(B2 + g * GS, g % 2, 2 * s, 2 * s + 2, "tok" if ORDER2[g][0] in "vu" else None,
                     (sem.h_ready, 8) if g == 0 else None)
                if s == 3:
                    st["free"][g % 2] = (sem.kept, 10 + g)
                if UNITS2[g] and (s == 3 or s == 1 and UNITS2[g] == 2):
                    finish()

            def head_scores(h):
                if h == 0:
                    pe.wait_ge(sem.kept, kept2("k"))
                    pe.wait_ge(sem.rows_out, 3)
                else:
                    pe.wait_ge(sem.m_out, h)
                for jb in range(2):
                    mm(bank[4][:, jb * S:(jb + 1) * S], tiles(MK)[:, h, jb * P:(jb + 1) * P], tiles(MQ)[:, h, :],
                       jb == 0)
                for bk, row in ((5, row_m), (6, row_s)):
                    for d in range(2):
                        r = 32 * d + h
                        ins = mm(bank[bk][:, d * S:(d + 1) * S], ident[BOTH, r:r + 1].broadcast_to([64, P]), row[BOTH, :],
                           d == 0, True)
                        if bk == 6 and d:
                            ins.then_inc(sem.head_made, 1)

            def head_den(h):
                pe.wait_ge(sem.p_made, h + 1)
                for n, (pp, jb, q, d) in enumerate(PARTS):
                    ins = mm(bank[5][:, d * S + q.start:d * S + q.stop], ones, pp, n == 0, True)
                    if n == 3:
                        ins.then_inc(sem.den_made, 1)

            def head_values(h):
                pe.wait_ge(sem.c_made, h + 1)
                pe.wait_ge(sem.kept, kept2("v0" if h < 2 else "v1"))
                v = halves(MV[h // 2])
                for t in range(2):
                    ch = slice((h % 2) * S + t * P, (h % 2) * S + (t + 1) * P)
                    mm(bank[4][:, t * S:(t + 1) * S], v[:, 0, ch], pf0, t == 0, False)
                    ins = mm(bank[4][:, t * S:(t + 1) * S], v[:, 1, ch], pb1, False, True)
                    if t:
                        ins.then_inc(sem.hval, 1)

            def head_rms(h):
                pe.wait_ge(sem.hsq, h + 1)
                for t in range(2):
                    ins = mm(bank[5][:, 0:S], ones, hsq[:, t * S:(t + 1) * S], t == 0, t == 1)
                    if t:
                        ins.then_inc(sem.hsum, 1)

            def fourier_tokens(n):
                pe.wait_ge(sem.kept, kept2(("u0", "u1")[n // 2]))
                if n:
                    pe.wait_ge(sem.dft_out, 3 * n)
                else:
                    pe.wait_ge(sem.m_out, 3)
                for dt in range(2):
                    for tb in range(2):
                        c = (n % 2) * S + dt * P
                        ins = mm(bank[(4, 5)[dt]], halves(MU[n // 2])[:, tb, c:c + P], dft[:, tb, :], tb == 0, tb == 1)
                        if tb:
                            ins.then_inc(sem.dft_done, 1)

            def fourier_channels(n):
                pe.wait_ge(sem.dft_out, 3 * n + 2)
                a = halves(12)
                for o in range(2):
                    for dt in range(2):
                        for cs in range(2):
                            ins = mm(bank[6][:, o * S:(o + 1) * S], dft[:, dt, cs * S + o * P:cs * S + (o + 1) * P],
                               a[:, dt, cs * S:(cs + 1) * S], o == 0 and dt == 0 and cs == 0, dt == 1 and cs == 1)
                            if o and dt and cs:
                                ins.then_inc(sem.dft_done, 1)

            for s in range(4):
                slot(0, s)
            pe.wait_ge(sem.wg_ready, 1)
            for tb in range(2):
                o = bank[6][:, tb * 16:(tb + 1) * 16]
                t = slice(tb * P, (tb + 1) * P)
                for kt in range(KT):
                    w = slice(kt * 16, kt * 16 + 16)
                    mm(o, hhi[:, kt, t], wg_hi[:, w], tb == 0 and kt == 0, False)
                    mm(o, hlo[:, kt, t], wg_hi[:, w], False, False)
                    ins = mm(o, hhi[:, kt, t], wg_lo[:, w], False, kt == KT - 1)
                    if tb and kt == KT - 1:
                        ins.then_inc(sem.gates, 1)
            slot(1, 0)
            slot(1, 1)
            pe.wait_ge(sem.gt_ready, 1)
            for k in range(2):
                for tb in range(2):
                    ins = mm(bank[4][BOTH, k * S + tb * P:k * S + (tb + 1) * P], gate_tok[:, k, tb, :], ident,
                       k == 0 and tb == 0, True)
                    if k and tb:
                        ins.then_inc(sem.rows_made, 1)
            slot(1, 2)
            slot(1, 3)
            slot(2, 0)
            pe.wait_ge(sem.rows_out, 1)
            for tb in range(2):
                ins = mm(bank[5][:, tb * 64:(tb + 1) * 64], row_c[BOTH, tb * P:(tb + 1) * P], ident[BOTH, 0:64],
                   tb == 0, True)
                if tb:
                    ins.then_inc(sem.ccol, 1)
            for s in range(1, 4):
                slot(2, s)
            for h, g in enumerate((3, 4, 5)):
                for s, step in enumerate((head_scores, head_den, head_values, head_rms)):
                    slot(g, s)
                    step(h)
            fourier_tokens(0)
            slot(6, 0)
            fourier_channels(0)
            pe.wait_ge(sem.dft_out, 3)
            head_scores(3)
            slot(6, 1)
            head_den(3)
            slot(6, 2)
            head_values(3)
            slot(6, 3)
            head_rms(3)
            pe.wait_ge(sem.m_out, 4)
            for n in range(1, 4):
                fourier_tokens(n)
                slot(7, n - 1)
                fourier_channels(n)
            slot(7, 3)

        def act_mix2(act, copy, fn, his):
            def kept(name):
                g = ORDER2.index(name)
                act.wait_ge(sem.slab_used, B2 + (g + 1) * GS)
                f, scale = (ACT.Sigmoid, 1.0) if name[0] == "g" else (ACT.Copy, P ** -0.5 if name == "q" else 1.0)
                nc.scalar.activation(page(KEPT2[name]), flat(g % 2), f, scale=scale).then_inc(sem.kept, 1)

            def ahead(g, s, n=2):
                n0 = B2 + g * GS + 2 * s + 3
                his(n0, n0 + n)

            def head(h, s):
                if s == 0:
                    act.wait_ge(sem.head_made, h + 1)
                    fn(floor_, bank[6], ACT.Exp).then_inc(sem.floor_made, 1)
                    act.wait_ge(sem.masked, h + 1)
                    for n, (pp, jb, q, d) in enumerate(PARTS):
                        ins = fn(pp, pp, ACT.Exp, bias=ccol[:, jb, 4 * d + h:4 * d + h + 1])
                        if n == 3:
                            ins.then_inc(sem.p_exp, 1)
                if s == 2:
                    act.wait_ge(sem.hval, h + 1)
                    fn(hsq, bank[4], ACT.Square).then_inc(sem.hsq, 1)
                if s == 3:
                    act.wait_ge(sem.hms, h + 1)
                    fn(hrms, hrms, ACT.Sqrt).then_inc(sem.hsd, 1)

            def fourier_a(n):
                for dt in range(2):
                    act.wait_ge(sem.dft_done, 3 * n + dt + 1)
                    a = halves(12)[:, dt, :]
                    copy(a[:, 0:S], bank[4 + dt][:, 0:S])
                    copy(a[:, S:2 * S], bank[4 + dt][:, S:2 * S], scale=-1.0).then_inc(sem.dft_out, 1)

            def fourier_y(n):
                act.wait_ge(sem.dft_done, 3 * n + 3)
                copy(halves(MF[n // 2])[:, n % 2, :], bank[6]).then_inc(sem.dft_out, 1)

            act.wait_ge(sem.tables2_landed, 48)
            copy(wg_hi, small[:]).then_inc(sem.wg_hi, 1)
            for s in range(4):
                ahead(0, s)
            kept("q")
            ahead(1, 0)
            act.wait_ge(sem.f_abs, 1)
            fn(f_abs, f_abs, ACT.Exp).then_inc(sem.f_exp, 1)
            act.wait_ge(sem.f_exp, 1)
            fn(f_abs, f_abs, ACT.Ln, bias=1.0).then_inc(sem.f_ln, 1)
            for s in range(1, 4):
                ahead(1, s)
            kept("k")
            for s in range(4):
                ahead(2, s)
            kept("v0")
            for h, g in enumerate((3, 4, 5)):
                for s in range(4):
                    ahead(g, s)
                    head(h, s)
                kept(ORDER2[g])
            fourier_a(0)
            ahead(6, 0)
            fourier_y(0)
            head(3, 0)
            ahead(6, 1)
            ahead(6, 2)
            head(3, 2)
            ahead(6, 3)
            kept("g0")
            head(3, 3)
            for n in range(1, 4):
                fourier_a(n)
                ahead(7, n - 1)
                fourier_y(n)
            ahead(7, 3)
            kept("g1")
            for k, pg in enumerate(MIXED2):
                act.wait_ge(*((sem.dft_out, 12) if k < 2 else (sem.y_gated, k - 1)))
                copy(hhi[:, 4 * k:4 * k + 4, :], tiles(pg)).then_inc(sem.mix_hi, 1)

        def dve_mix2(dve, at, st, tt, ts, stt, unit, modulation):
            V = nc.vector
            dve.wait_ge(sem.wg_hi, 1)
            tt(wg_lo, small[:], wg_hi.bitcast(F32), ALU.subtract).then_inc(*at.up(sem.wg_ready))
            V.memset(page(22)[:, 0:256], 0.0).then_inc(*at.up(sem.step))
            V.memset(page(21)[:, 512:768], 1.0).then_inc(*at.up(sem.step))
            V.memset(page(21)[:, 768:1024], 0.0).then_inc(*at.up(sem.step))
            unit()
            one, zero = page(21)[BOTH, 512:768], page(21)[FWD, 768:1024]
            dve.wait_ge(sem.gates, 1)
            tt(gate_in, bank[6][:, 0:32].rearrange("p (b c) -> p b c", c=16),
               col("bgates", 0, 16).unsqueeze(1).broadcast_to([P, 2, 16]), ALU.add).then_inc(*at.up(sem.step))
            dve.wait_ge(*at.last)
            ts(f_min, gate_in[:, :, 8:16], 0.0, None, ALU.min).then_inc(*at.up(sem.step))
            V.tensor_copy(gate_tok[:, 0].rearrange("p b (d x) -> p b d x", d=2)[:, :, :, 0:4],
                               gate_in[:, :, 0:8].rearrange("p b (d x) -> p b d x", d=2)).then_inc(*at.up(sem.step))
            dve.wait_ge(*at.last)
            stt(f_abs, f_min, 2.0, gate_in[:, :, 8:16], ALU.mult, ALU.subtract).then_inc(*at.up(sem.f_abs))
            dve.wait_ge(sem.f_ln, 1)
            tt(gate_tok[:, 1].rearrange("p b (d x) -> p b d x", d=2)[:, :, :, 0:4],
               f_min.rearrange("p b (d x) -> p b d x", d=2), f_abs.rearrange("p b (d x) -> p b d x", d=2),
               ALU.subtract).then_inc(*at.up(sem.gt_ready))
            unit()
            dve.wait_ge(sem.rows_made, 1)
            gi, gf = bank[4][:, 0:S], bank[4][:, S:2 * S]
            V.tensor_tensor_scan(row_b[BOTH], one, gf[BOTH], 0.0, ALU.mult, ALU.add).then_inc(*at.up(sem.step))
            dve.wait_ge(*at.last)
            tt(row_b[BWD], row_b[BWD], gf[BWD], ALU.subtract).then_inc(*at.up(sem.step))
            tt(row_c[FWD], gi[FWD], row_b[FWD], ALU.subtract).then_inc(*at.up(sem.step))
            dve.wait_ge(*at.last)
            tt(row_c[BWD], gi[BWD], row_b[BWD], ALU.add).then_inc(*at.up(sem.rows_out))
            dve.wait_ge(*at.last)
            V.tensor_tensor_scan(row_m[FWD], zero, row_c[FWD], -3e38, ALU.add, ALU.max).then_inc(*at.up(sem.step))
            V.tensor_copy(row_m[BWD], row_c[BWD]).then_inc(*at.up(sem.step))
            for k in range(8):
                n = 1 << k
                dve.wait_ge(*at.last)
                tt(row_m[BWD, 0:S - n], row_m[BWD, 0:S - n], row_m[BWD, n:S], ALU.max).then_inc(*at.up(sem.step))
            dve.wait_ge(*at.last)
            stt(row_s[FWD], row_b[FWD], -1.0, row_m[FWD], ALU.mult, ALU.subtract).then_inc(*at.up(sem.step))
            tt(row_s[BWD], row_b[BWD], row_m[BWD], ALU.subtract).then_inc(*at.up(sem.step))
            dve.wait_ge(*at.last)
            ts(row_m[BOTH], row_m[BOTH], -1.0, None, ALU.mult).then_inc(*at.up(sem.rows_out))
            dve.wait_ge(sem.ccol, 1)
            V.tensor_copy(ccol.rearrange("p b (d x) -> p b d x", d=2),
                               bank[5][:, 0:P].rearrange("p (b d x) -> p b d x", b=2, d=2)[:, :, :, 0:4]).then_inc(*at.up(sem.rows_out))
            unit()
            unit()

            def head(h, s):
                if s == 0:
                    dve.wait_ge(sem.head_made, h + 1)
                    m = bank[5]
                    tt(pf0[:, 0:P], m[:, 0:P], mask_f[:, 0:P], ALU.add).then_inc(*at.up(sem.step))
                    V.tensor_copy(pf0[:, P:S], m[:, P:S]).then_inc(*at.up(sem.step))
                    tt(pf1, m[:, P:S], mask_f[:, 0:P], ALU.add).then_inc(*at.up(sem.step))
                    tt(pb0, m[:, S:S + P], mask_b[:, P:S], ALU.add).then_inc(*at.up(sem.step))
                    tt(pb1, m[:, S:2 * S], mask_b, ALU.add).then_inc(*at.up(sem.masked))
                    dve.wait_ge(sem.p_exp, h + 1)
                    for n, (pp, jb, q, d) in enumerate(PARTS):
                        tt(pp, pp, bank[4][:, jb * S + q.start:jb * S + q.stop], ALU.mult).then_inc(*at.up(sem.p_made if n == 3 else sem.step))
                if s == 1:
                    dve.wait_ge(sem.den_made, h + 1)
                    dve.wait_ge(sem.floor_made, h + 1)
                    stt(inv, bank[5], -1.0, floor_, ALU.mult, ALU.max).then_inc(*at.up(sem.step))
                    dve.wait_ge(*at.last)
                    tt(inv, inv, bank[5], ALU.max).then_inc(*at.up(sem.step))
                    dve.wait_ge(*at.last)
                    V.reciprocal(inv, inv).then_inc(*at.up(sem.step))
                    dve.wait_ge(*at.last)
                    for n, (pp, jb, q, d) in enumerate(PARTS):
                        tt(pp, pp, inv[:, d * S + q.start:d * S + q.stop], ALU.mult).then_inc(*at.up(sem.step))
                    dve.wait_ge(*at.last)
                    tt(pf0[:, 0:P], pf0[:, 0:P], pb0, ALU.add).then_inc(*at.up(sem.step))
                    tt(pb1[:, P:S], pb1[:, P:S], pf1, ALU.add).then_inc(*at.up(sem.c_made))
                if s == 3:
                    dve.wait_ge(sem.hsum, h + 1)
                    ts(hrms, bank[5][:, 0:S], 1.0 / S, EPS, ALU.mult, ALU.add).then_inc(*at.up(sem.hms))
                    dve.wait_ge(sem.hsd, h + 1)
                    V.reciprocal(hrms, hrms).then_inc(*at.up(sem.step))
                    dve.wait_ge(*at.last)
                    for t in range(2):
                        stt(tiles(MY[h // 2])[:, 2 * (h % 2) + t, :], bank[4][:, t * S:(t + 1) * S],
                            col("mlstm_norm", 2 * h + t), hrms, ALU.mult, ALU.mult).then_inc(*at.up(sem.m_out if t else sem.step))

            for h in range(3):
                unit()
                head(h, 0)
                head(h, 1)
                unit()
                head(h, 3)
            unit()
            head(3, 0)
            head(3, 1)
            head(3, 3)
            unit()
            for n in range(2):
                dve.wait_ge(sem.kept, kept2(("g0", "g1")[n]))
                if n == 0:
                    dve.wait_ge(*at.last)
                tt(page(MY[n]), page(MY[n]), page(MG[n]), ALU.mult).then_inc(*at.up(sem.y_gated))
            for k, pg in enumerate(MIXED2):
                dve.wait_ge(sem.mix_hi, 4 + k + 1)
                tt(hlo[:, 4 * k:4 * k + 4, :], tiles(pg), hhi[:, 4 * k:4 * k + 4, :].bitcast(F32),
                   ALU.subtract).then_inc(*at.up(sem.mix_split))

        @block.sync
        def _(sp):
            st = {"unit": 0}

            def slab(n, per=0, i=0):
                if n >= RING:
                    by_dve, v = lo_signal(n - RING)
                    sp.wait_ge(sem.lo2_ready if by_dve else sem.lo_ready, v + lo_per(n - RING, per) * i)
                sp.dma_start(raw[:, n % RING, :],
                             wstream[bass.ds(n + per * i, 1), :, :].rearrange("a p n -> (a p) n")
                             ).then_inc(sem.w_landed[n % RING], 16)

            def ada(s, per=0, i=0):
                u = st["unit"]
                m = 2 * u + s + 2 * per * i
                if u > 0:
                    sp.wait_ge((sem.ada_used, sem.acc_ready)[s], u + per * i)
                sp.dma_start(ada_raw[:, s, :], adastream[bass.ds(m, 1), :, :].rearrange("a p n -> (a p) n")
                             ).then_inc(sem.ada_landed[s], 16)
                st["unit"] += s

            def unit(per=0, i=0):
                ada(0, per, i)
                ada(1, per, i)

            MIX_TWO = {1: 0, 2: 1, 5: 0, 6: 1}

            def groups(n0, count, units, size=GS):
                per_turn = sum(units.values())

                def body(n, i=0, per=0):
                    for k in range(size):
                        if k in units:
                            ada(units[k], per_turn if per else 0, i)
                        slab(n + k, per, i)

                body(n0)
                if count > 1:
                    u0 = st["unit"]
                    with sp.Fori(0, count - 1) as i:
                        body(n0 + size, i, size)
                    st["unit"] = u0 + per_turn * (count - 1)

            def down(n0, units):
                for half in range(2):
                    n = n0 + half * DOWN_HALF
                    for k in range(4):
                        slab(n + k)
                    groups(n + 4, 5, {1: 0, 4: 1} if units else {})

            sp.dma_start(cols[:], cols_in).then_inc(sem.cols_landed, 16)
            unit()
            sp.dma_start(tabs[:], tabs_in[:, 0:N_KEPT]).then_inc(sem.tabs_landed, 16)
            for n in range(RING):
                slab(n)
            for k in range(4):
                sp.dma_start(xT[:, 4 * k:4 * k + 4, :], x_in[:, 4 * k:4 * k + 4, :]).then_inc(sem.x_landed, 16)
            sp.dma_start(conv[:], conv_in).then_inc(sem.conv_landed, 16)
            for dst, name in ((page(19), "retdecay"), (page(20)[:, 0:S], "alibi")):
                a, n = TABS[name]
                sp.dma_start(dst, tabs_in[:, a:a + n]).then_inc(sem.tables1_landed, 16)
            sp.dma_start(page(21), rw_in[:, 0, :]).then_inc(sem.tables1_landed, 16)
            sp.dma_start(page(22), rw_in[:, 1, :]).then_inc(sem.tables1_landed, 16)
            with sp.Fori(0, START_UNITS - 1) as i:
                unit(1, i)
            st["unit"] = START_UNITS
            for n in range(RING, GS):
                slab(n)
            groups(GS, 8, MIX_TWO)
            groups(9 * GS, MIX1 - 9, {1: 0, 3: 1})
            groups(B1_OUT, 1, {1: 0, 3: 1})
            sp.wait_ge(sem.mix_split, 4)
            for k in range(4):
                sp.dma_start(xT[:, 4 * k:4 * k + 4, :], x_in[:, 4 * k:4 * k + 4, :]
                             ).then_inc(sem.x_landed, 16)
            groups(B1_OUT + GS, 3, {1: 0, 3: 1})
            groups(B1_UP, NFF, {2: 0, 5: 1, GS + 2: 0, GS + 5: 1}, 2 * GS)
            down(B1_DOWN, True)
            sp.wait_ge(sem.slab_used, B2)
            a, n = TABS["dft"]
            sp.dma_start(page(19), tabs_in[:, a:a + n]).then_inc(sem.tables2_landed, 16)
            a = TABS["mfwd"][0]
            sp.dma_start(page(20)[:, 0:640], tabs_in[:, a:a + 640]).then_inc(sem.tables2_landed, 16)
            sp.dma_start(small[:], wg_in).then_inc(sem.tables2_landed, 16)
            groups(B2, 1, {})
            groups(B2 + GS, 5, MIX_TWO)
            groups(B2 + 6 * GS, MIX2 - 6, {1: 0, 3: 1})
            groups(B2_OUT, 4, {1: 0, 3: 1})
            groups(B2_UP, 8, {2: 0, 5: 1}, 2 * GS)
            groups(B2_UP + 16 * GS, NFF - 8, {}, 2 * GS)
            down(B2_DOWN, False)
            for k in range(4):
                sp.wait_ge(sem.y_ready, k + 1)
                sp.dma_start(out[:, 4 * k:4 * k + 4, :], xT[:, 4 * k:4 * k + 4, :]
                             ).then_inc(sem.out_landed, 16)
            sp.wait_ge(sem.out_landed, 64)

        @block.gpsimd
        def _(pool):

            def stretch(n0, n1, step):
                with pool.Fori(0, (n1 - n0) // RING) as i:
                    for q in range(0, RING, step):
                        pool.wait_ge(sem.hi_ready, n0 + q + 1 + RING * i)
                        nc.gpsimd.tensor_tensor(wlo[:, q, :], raw[:, q, :], whi[:, q, :].bitcast(F32),
                                                     ALU.subtract).then_inc(sem.lo_ready, 1)

            for n0, n1, step in ((0, B1_UP, 1), (B1_UP, B2, 2), (B2, B2_UP, 1), (B2_UP, N_SLABS, 2)):
                stretch(n0, n1, step)

        @block.scalar
        def _(act):

            def copy(out_, in_, scale=1.0):
                return nc.scalar.activation(out_, in_, ACT.Copy, scale=scale)

            def fn(out_, in_, f, **kw):
                return nc.scalar.activation(out_, in_, f, **kw)

            def hi(n, per=0, i=0):
                if n >= N_SLABS:
                    return
                q = n % RING
                act.wait_ge(sem.w_landed[q], 16 * (n // RING + 1) + 16 * (per // RING) * i)
                if n >= RING:
                    act.wait_ge(sem.slab_used, n - RING + 1 + per * i)
                copy(whi[:, q, :], raw[:, q, :]).then_inc(sem.hi_ready, 1)


            def his(n0, n1):
                for n in range(n0, n1):
                    hi(n)

            def square(N, k):
                if N == 0:
                    act.wait_ge(sem.x_landed, 64)
                else:
                    act.wait_ge(sem.x_ready, 4 * (N - 1) + k + 1)
                if k >= 2:
                    act.wait_ge(sem.sq_used, 4 * N + k - 1)
                fn(page(13 + k % 2), page(15 + k), ACT.Square).then_inc(sem.sq_ready, 1)

            def norm(N, hN=None, squared=0):
                for k in range(squared, 4):
                    square(N, k)
                act.wait_ge(sem.ms_ready, N + 1)
                fn(rstd[:], rstd[:], ACT.Sqrt).then_inc(sem.sd_ready, 1)
                if hN is not None:
                    for k in range(4):
                        act.wait_ge(sem.u_ready, 4 * hN + k + 1)
                        copy(hhi[:, 4 * k:4 * k + 4, :], tiles(13 + k % 2)).then_inc(sem.h_hi, 1)

            def output(n0, N, hN):
                for g in range(4):
                    his(n0 + g * GS + 3, n0 + (g + 1) * GS + 3)
                    if g > 0:
                        square(N, g - 1)
                norm(N, hN, 3)

            def ffn(n0, b):
                gb = NFF * b
                with act.Fori(0, NFF) as i:
                    for half in range(2):
                        for k in range(GS):
                            hi(n0 + half * GS + 3 + k, 2 * GS, i)
                        act.wait_ge(sem.slab_used, n0 + (half + 1) * GS + 2 * GS * i)
                        if half == 0:
                            act.wait_ge(sem.cw_ready, gb + 1 + i)
                        u = pair(1 - half)
                        for j in range(4):
                            c = 16 * half + 4 * j
                            ins = fn(tiles(11 + half)[:, j, :], u[:, j, :], ACT.Identity,
                               scale=cw[:, c:c + 1], bias=cw[:, c + 3:c + 4])
                            if j == 3:
                                ins.then_inc((sem.gate_tap if half else sem.val_tap), 1)
                    act.wait_ge(sem.free_gate, gb + 1 + i)
                    fn(page(12), page(12), ACT.Silu).then_inc(sem.gate_act, 1)

            def down(n0, b, more):
                def gs(kk, kk_reg=None):
                    kc = kk % NFF if kk_reg is None else kk_reg
                    act.wait_ge(sem.g_made, NFF * b + (kk % NFF + 1 if kk < NFF else NFF))
                    if kk >= 2:
                        act.wait_ge(sem.slab_used, n0 + 4 * (kk - 1))
                    copy(gshi[:, kk % 2, :, :], gT[:, 4 * kc:4 * kc + 4, :]).then_inc(sem.gs_hi, 1)

                gs(0)
                for half in range(2):
                    kk0 = NFF * half
                    gs(kk0 + 1)
                    his(n0 + 4 * kk0 + 3, n0 + 4 * kk0 + 7)
                    with act.Fori(0, 4) as i:
                        for s in range(2):
                            kk = kk0 + 2 + s
                            act.wait_ge(sem.slab_used, n0 + 4 * (kk - 1) + 8 * i)
                            if half == 0:
                                act.wait_ge(sem.g_made, NFF * b + kk + 1 + 2 * i)
                            copy(gshi[:, kk % 2, :, :], gT[:, bass.ds(4 * (kk % NFF) + 8 * i, 4), :]).then_inc(sem.gs_hi, 1)
                            for c in range(4):
                                hi(n0 + 4 * (kk - 1) + 3 + c, 8, i)
                    for kk in (kk0 + 9, kk0 + 10):
                        if kk + 1 < 2 * NFF:
                            gs(kk + 1)
                        his(n0 + 4 * kk + 3, n0 + 4 * kk + 7)

            act.wait_ge(sem.cols_landed, 16)
            fn(cact[:], col("c", 0, 32), ACT.Silu).then_inc(sem.cact_ready, 1)
            his(0, 3)
            norm(0, 0)
            act_mix1(act, copy, fn, his)
            output(B1_OUT, 1, 1)
            ffn(B1_UP, 0)
            down(B1_DOWN, 0, True)
            norm(2)
            norm(3, 2)
            act_mix2(act, copy, fn, his)
            output(B2_OUT, 4, 3)
            ffn(B2_UP, 1)
            down(B2_DOWN, 1, False)
            norm(5)

        @block.tensor
        def _(pe):
            st = {"free": {0: None, 1: None}, "finished": 0}

            def mm(o, lhsT, rhs, start, stop=True):
                return nc.tensor.matmul(o, lhsT, rhs, start=start, stop=stop, skip_group_check=True)

            def product(o, lh, ll, rh, rl, start, stop):
                mm(o, lh, rh, start, False)
                mm(o, ll, rh, False, False)
                return mm(o, lh, rl, False, stop)

            def ready(n, per=0, i=0):
                by_dve, v = lo_signal(n)
                pe.wait_ge(sem.lo2_ready if by_dve else sem.lo_ready, v + lo_per(n, per) * i)

            def slab(n, p, rh, rl, first, last, per=0, i=0):
                ready(n, per, i)
                q = n % RING
                for kk in range(2):
                    for j in range(4):
                        w = slice(kk * 512 + j * P, kk * 512 + (j + 1) * P)
                        ins = product(pair(p)[:, j, :], whi[:, q, w], wlo[:, q, w], rh[:, kk, :], rl[:, kk, :],
                                      first and kk == 0 and j % 2 == 0, last and kk == 1)
                        if kk == 1 and j == 3:
                            ins.then_inc(sem.slab_used, 1)

            def slab_tok(n, p, k, first, last):
                ready(n)
                q = n % RING
                for kk in range(2):
                    w = slice(kk * 512, (kk + 1) * 512)
                    for tb in range(2):
                        t = slice(tb * P, (tb + 1) * P)
                        o = bank[2 * p + tb]
                        mm(o, hhi[:, 2 * k + kk, t], whi[:, q, w], first and kk == 0, False)
                        mm(o, hlo[:, 2 * k + kk, t], whi[:, q, w], False, False)
                        ins = mm(o, hhi[:, 2 * k + kk, t], wlo[:, q, w], False, last and kk == 1)
                        if kk == 1 and tb == 1:
                            ins.then_inc(sem.slab_used, 1)

            def finish(b=0, per=0, i=0):
                pe.wait_ge(sem.acc_ready, st["finished"] + 1 + per * i)
                st["finished"] += 1
                for j in range(2):
                    for h in range(2):
                        ins = mm(bank[7][:, j:j + 1], acc[:, b, h, j * P:(j + 1) * P], ones[:, 0:1],
                           j == 0 and h == 0, h == 1)
                        if j and h:
                            ins.then_inc(sem.ada_sum, 1)

            def part(n0, p, k0, k1, form=None, h_at=None):
                if k0 == 0 and st["free"][p]:
                    pe.wait_ge(*st["free"][p])
                for k in range(k0, k1):
                    if h_at and k % 2 == 0:
                        pe.wait_ge(h_at[0], h_at[1] + k // 2 + 1)
                    if form == "tok":
                        slab_tok(n0 + k, p, k, k == 0, k == GS - 1)
                    else:
                        slab(n0 + k, p, hhi[:, 2 * k:2 * k + 2, :], hlo[:, 2 * k:2 * k + 2, :],
                             k == 0, k == GS - 1)

            def sums(N, k):
                pe.wait_ge(sem.sq_ready, 4 * N + k + 1)
                for j in range(4):
                    ins = mm(bank[6][:, 0:S], ones, tiles(13 + k % 2)[:, j, :], k == 0 and j == 0,
                       k == 3 and j == 3)
                    if j == 3:
                        ins.then_inc(sem.sq_used, 1)

            def output(n0, g0, N, x0, h_at, units):
                for g in range(4):
                    p = (g0 + g) % 2
                    part(n0 + g * GS, p, 0, 4, h_at=h_at if g == 0 else None)
                    if g >= 2:
                        sums(N, g - 2)
                    part(n0 + g * GS, p, 4, GS, h_at=h_at if g == 0 else None)
                    st["free"][p] = (sem.x_ready, x0 + g + 1)
                    if units:
                        finish()
                sums(N, 2)
                sums(N, 3)

            def up(n0, b, h0, segments):
                done = 0
                gb = NFF * b

                def body(t, i, per, units):
                    for half in range(2):
                        p = 1 - half
                        free = (sem.free_val, sem.free_gate)[half]
                        if i is None and t == 0:
                            pe.wait_ge(*st["free"][p])
                        else:
                            pe.wait_ge(free, gb + t + (0 if i is None else i))
                        for k in range(GS):
                            if i is None and t == 0 and half == 0 and k % 2 == 0:
                                pe.wait_ge(sem.h_ready, h0 + k // 2 + 1)
                            slab(n0 + 2 * GS * t + half * GS + k, p, hhi[:, 2 * k:2 * k + 2, :],
                                 hlo[:, 2 * k:2 * k + 2, :], k == 0, k == GS - 1, 2 * GS * per, 0 if i is None else i)
                        if half < units:
                            finish(0, units * per, 0 if i is None else i)

                for turns, units in segments:
                    if done == 0:
                        body(0, None, 0, units)
                        done, turns = 1, turns - 1
                    before = st["finished"]
                    with pe.Fori(0, turns) as i:
                        body(done, i, 1, units)
                    st["finished"] = before + units * turns
                    done += turns

            def down(n0, b, N, x0, units):
                for half in range(2):
                    pa, pb = ((1, 0), (2, 1))[half]
                    kk0 = NFF * half

                    def chunk(kk, per=0, i=0, first=False, last=False):
                        pe.wait_ge(sem.gs_lo, 2 * NFF * b + kk + 1 + (per // 4) * i)
                        for g, p in enumerate((pa, pb)):
                            if first and half == 0:
                                pe.wait_ge((sem.free_gate, sem.free_val)[p], NFF * (b + 1))
                            if first and half == 1 and p == 1:
                                pe.wait_ge(sem.x_ready, x0 + 1)
                            for k in range(2):
                                slab(n0 + 4 * kk + 2 * g + k, p, gshi[:, kk % 2, 2 * k:2 * k + 2, :],
                                     gslo[:, kk % 2, 2 * k:2 * k + 2, :], first and k == 0, last and k == 1,
                                     per, i)

                    chunk(kk0, first=True)
                    before = st["finished"]
                    with pe.Fori(0, 4) as i:
                        for s in range(2):
                            chunk(kk0 + 1 + s, 8, i)
                        if units:
                            finish(0, 1, i)
                    if units:
                        st["finished"] = before + 4
                    chunk(kk0 + 9)
                    chunk(kk0 + 10, last=True)
                    if units:
                        finish()
                    if half == 1:
                        for k in range(4):
                            sums(N, k)

            def final(N):
                for k in range(4):
                    sums(N, k)

            pe.wait_ge(sem.tabs_landed, 16)
            with pe.Fori(0, START_UNITS // 2) as i:
                for b in range(2):
                    st["finished"] = b
                    finish(b, 2, i)
            st["finished"] = START_UNITS
            for k in range(4):
                sums(0, k)
            pe_mix1(pe, st, mm, part, finish)
            output(B1_OUT, MIX1, 1, 0, (sem.mix_split, 0), True)
            up(B1_UP, 0, 4, [(NFF, 2)])
            down(B1_DOWN, 0, 2, 4, True)
            final(3)
            st["free"] = {0: (sem.x_ready, 8), 1: (sem.x_ready, 8)}
            pe_mix2(pe, st, mm, part, finish)
            output(B2_OUT, MIX2, 4, 12, (sem.mix_split, 4), True)
            up(B2_UP, 1, 12, [(8, 1), (3, 0)])
            down(B2_DOWN, 1, 5, 16, False)

        @block.vector
        def _(dve):
            at = Count()
            V = nc.vector
            st = {"unit": 0}

            def tt(o, a, b, op_):
                return V.tensor_tensor(o, a, b, op_)

            def ts(o, a, s1, s2, op0, op1=ALU.bypass):
                if s2 is None:
                    return V.tensor_scalar(o, a, s1, None, op0)
                return V.tensor_scalar(o, a, s1, s2, op0, op1)

            def stt(o, a, s, b, op0, op1):
                return V.scalar_tensor_tensor(out=o, in0=a, scalar=s, in1=b, op0=op0, op1=op1)

            def modulation(u, static=True, per=0, i=0):
                dve.wait_ge(sem.ada_sum, u + 1 + per * i)
                s = bass.ds(2 * u + 2 * per * i, 2) if per else slice(2 * u, 2 * u + 2)
                b = bass.ds(COLS["bada"] + 2 * u + 2 * per * i, 2) if per else \
                    slice(COLS["bada"] + 2 * u, COLS["bada"] + 2 * u + 2)
                tt(modc[:, s], bank[7][:, 0:2], cols[:, b], ALU.add).then_inc(*at.up(sem.step))

            def chunk(s, buf, u, per=0, i=0):
                blk = u // 48
                dve.wait_ge(sem.ada_landed[s], 16 * (u + 1) + 16 * per * i)
                marks = st["marks"]
                c0 = 16 * (1 if (u >= 48) else 0)
                for k in range(8):
                    kt = 8 * s + k
                    w = ada_raw[:, s, k * 256:(k + 1) * 256]
                    o = acc[:, buf, kt % 2, :]
                    c = cact[:, c0 + kt:c0 + kt + 1]
                    if kt >= 2:
                        dve.wait_ge(*marks[kt % 2])
                    signal = sem.acc_ready if kt == 15 else (sem.ada_used if k == 7 else sem.step)
                    if kt < 2:
                        ts(o, w, c, None, ALU.mult).then_inc(*at.up(signal))
                    else:
                        stt(o, w, c, o, ALU.mult, ALU.add).then_inc(*at.up(signal))
                    marks[kt % 2] = at.last

            def unit(buf=0, fill=None):
                u = st["unit"]
                st["unit"] += 1
                st["marks"] = {}
                if u > 0:
                    modulation(u - 1)
                chunk(0, buf, u)
                if fill:
                    fill()
                chunk(1, buf, u)

            def norm(N):
                dve.wait_ge(sem.sq_used, 4 * (N + 1))
                ts(rstd[:], bank[6][:, 0:S], 1.0 / D, EPS, ALU.mult, ALU.add).then_inc(*at.up(sem.ms_ready))
                dve.wait_ge(sem.sd_ready, N + 1)
                V.reciprocal(rstd[:], rstd[:]).then_inc(*at.up(sem.step))
                dve.wait_ge(*at.last)

            def rstd4():
                return rstd[:].unsqueeze(1).broadcast_to([P, 4, S])

            def modulated(N, hN, gain, u0):
                shift, scale = u0, u0 + 16
                norm(N)
                stt(colA[:], modc[:, scale:scale + 16], 1.0, col(gain, 0, 16), ALU.add, ALU.mult).then_inc(*at.up(sem.step))
                dve.wait_ge(*at.last)
                split = []
                for k in range(4):
                    u = tiles(13 + k % 2)
                    if k >= 2:
                        dve.wait_ge(*split[k - 2])
                    tt(u, xT[:, 4 * k:4 * k + 4, :], rstd4(), ALU.mult).then_inc(*at.up(sem.step))
                    dve.wait_ge(*at.last)
                    for j in range(4):
                        c = 4 * k + j
                        ts(u[:, j, :], u[:, j, :], colA[:, c:c + 1], modc[:, shift + c:shift + c + 1],
                           ALU.mult, ALU.add).then_inc(*at.up(sem.u_ready if j == 3 else sem.step))
                    dve.wait_ge(sem.h_hi, 4 * hN + k + 1)
                    h = hhi[:, 4 * k:4 * k + 4, :]
                    tt(hlo[:, 4 * k:4 * k + 4, :], u, h.bitcast(F32), ALU.subtract).then_inc(*at.up(sem.h_ready))
                    split.append(at.last)

            def scaled(N, gain, signal):
                norm(N)
                for k in range(4):
                    xk = xT[:, 4 * k:4 * k + 4, :]
                    tt(xk, xk, rstd4(), ALU.mult).then_inc(*at.up(sem.step))
                    dve.wait_ge(*at.last)
                    for j in range(4):
                        c = 4 * k + j
                        ts(xT[:, c, :], xT[:, c, :], col(gain, c), None, ALU.mult).then_inc(*at.up(signal if j == 3 else sem.step))

            def residual(n_used, p, k, gate, signal=sem.x_ready):
                dve.wait_ge(sem.slab_used, n_used)
                for j in range(4):
                    c = 4 * k + j
                    stt(xT[:, c, :], pair(p)[:, j, :], modc[:, gate + c:gate + c + 1], xT[:, c, :],
                        ALU.mult, ALU.add).then_inc(*at.up(signal if j == 3 else sem.step))

            def lo2(n, per=0, i=0):
                if n % 2 == 0:
                    return
                q = n % RING
                dve.wait_ge(sem.hi_ready, n + 1 + per * i)
                tt(wlo[:, q, :], raw[:, q, :], whi[:, q, :].bitcast(F32), ALU.subtract).then_inc(*at.up(sem.lo2_ready))

            def los(n0, n1):
                for n in range(n0, n1):
                    if n < N_SLABS:
                        lo2(n)

            def ffn(n0, b, segments):
                done = 0
                for turns, units, own in segments:
                    u0 = st["unit"]
                    with at.loop(dve, turns, {sem.lo2_ready: GS, sem.cw_ready: 1, sem.free_val: 1, sem.free_gate: 1,
                                                sem.g_made: 1, sem.acc_ready: units, sem.ada_used: units,
                                                sem.step: own}) as i:
                        n1 = n0 + 2 * GS * done
                        for half in range(2):
                            if half == 0:
                                V.tensor_copy(cw[:].rearrange("p (a c) -> p a c", a=1),
                                                   conv[:, b, bass.ds(done + i, 1), :]).then_inc(*at.up(sem.cw_ready))
                            has = half < units
                            uu = u0 + half
                            lo_at = n1 + half * GS + 3
                            lo2(lo_at, 2 * GS, i)
                            lo2(lo_at + 1, 2 * GS, i)
                            if has:
                                st["marks"] = {}
                                modulation(uu - 1, per=units, i=i)
                                chunk(0, 0, uu, units, i)
                            for k in range(2, 5):
                                lo2(lo_at + k, 2 * GS, i)
                            if has:
                                chunk(1, 0, uu, units, i)
                            for k in range(5, GS):
                                lo2(lo_at + k, 2 * GS, i)
                            dve.wait_ge((sem.val_tap, sem.gate_tap)[half], NFF * b + done + 1 + i)
                            u, t = pair(1 - half), tiles(11 + half)
                            marks = []
                            for j in range(4):
                                c = 16 * half + 4 * j
                                stt(t[:, j, 1:S], u[:, j, 0:S - 1], cw[:, c + 1:c + 2],
                                                 t[:, j, 1:S], ALU.mult, ALU.add).then_inc(*at.up(sem.step))
                                marks.append(at.last)
                            for j in range(4):
                                c = 16 * half + 4 * j
                                dve.wait_ge(*marks[j])
                                o, f = (slice(2, S), slice(0, S - 2)) if b == 0 else (slice(0, S - 1), slice(1, S))
                                stt(t[:, j, o], u[:, j, f], cw[:, c + 2:c + 3], t[:, j, o], ALU.mult, ALU.add).then_inc(*at.up((sem.free_val, sem.free_gate)[half] if j == 3 else sem.step))
                        dve.wait_ge(sem.gate_act, NFF * b + done + 1 + i)
                        tt(gT[:, bass.ds(4 * (done + i), 4), :], tiles(11), tiles(12), ALU.mult).then_inc(*at.up(sem.g_made))
                        dve.wait_ge(*at.last)
                    st["unit"] = u0 + units * turns
                    done += turns

            def down(n0, b, gate, x0, units, own):
                def gs(kk, per=0, i=0):
                    kc = kk % NFF
                    dve.wait_ge(sem.gs_hi, 2 * NFF * b + kk + 1 + per * i)
                    src = gT[:, 4 * kc:4 * kc + 4, :] if not per else gT[:, bass.ds(4 * kc + 8 * i, 4), :]
                    tt(gslo[:, kk % 2, :, :], src, gshi[:, kk % 2, :, :].bitcast(F32), ALU.subtract).then_inc(*at.up(sem.gs_lo))

                gs(0)
                for half in range(2):
                    kk0 = NFF * half
                    gs(kk0 + 1)
                    los(n0 + 4 * kk0 + 3, n0 + 4 * kk0 + 7)
                    if half == 1:
                        for k, p in enumerate((1, 0)):
                            residual(n0 + 4 * NFF, p, k, gate)
                    u0 = st["unit"]
                    with at.loop(dve, 4, {sem.gs_lo: 2, sem.lo2_ready: 4, sem.acc_ready: units, sem.ada_used: units,
                                              sem.step: own}) as i:
                        n1 = n0 + 4 * kk0
                        gs(kk0 + 2, 2, i)
                        for c in range(4):
                            lo2(n1 + 4 + 3 + c, 8, i)
                        if units:
                            st["marks"] = {}
                            modulation(u0 - 1, per=1, i=i)
                            chunk(0, 0, u0, 1, i)
                        gs(kk0 + 3, 2, i)
                        for c in range(2):
                            lo2(n1 + 8 + 3 + c, 8, i)
                        if units:
                            chunk(1, 0, u0, 1, i)
                        for c in range(2, 4):
                            lo2(n1 + 8 + 3 + c, 8, i)
                    st["unit"] = u0 + 4 * units
                    gs(kk0 + 10)
                    los(n0 + 4 * (kk0 + 9) + 3, n0 + 4 * (kk0 + 9) + 7)
                    if units:
                        unit()
                    if half == 0:
                        gs(kk0 + 11)
                    los2 = min(n0 + 4 * (kk0 + 10) + 7, n0 + 8 * NFF)
                    los(n0 + 4 * (kk0 + 10) + 3, los2)
                for k, p in enumerate((2, 1)):
                    residual(n0 + 8 * NFF, p, 2 + k, gate)


            dve.wait_ge(sem.cact_ready, 1)
            st["marks"] = {}
            dve.wait_ge(sem.cols_landed, 16)
            for u in range(2):
                chunk(0, u, u)
                if u:
                    modulation(u - 1)
                chunk(1, u, u)
            with at.loop(dve, START_UNITS // 2 - 1, {sem.acc_ready: 2, sem.ada_used: 2, sem.step: 30}) as i:
                for b in range(2):
                    st["marks"] = {}
                    chunk(0, b, 2 + b, 2, i)
                    modulation(1 + b, per=2, i=i)
                    chunk(1, b, 2 + b, 2, i)
            st["unit"] = START_UNITS
            modulation(START_UNITS - 1)
            dve.wait_ge(*at.last)
            modulated(0, 0, "norm_mix", 0)
            dve_mix1(dve, at, st, tt, ts, stt, unit, modulation)
            for g in range(4):
                unit()
                if g == 0:
                    dve.wait_ge(sem.x_landed, 128)
                residual(B1_OUT + (g + 1) * GS, (MIX1 + g) % 2, g, 32)
            los(B1_UP, B1_UP + 3)
            modulation(st["unit"] - 1)
            dve.wait_ge(*at.last)
            modulated(1, 1, "norm_ffn", 48)
            ffn(B1_UP, 0, [(4, 2, 44), (NFF - 4, 2, 44)])
            down(B1_DOWN, 0, 80, 4, 1, 15)
            scaled(2, "norm_final", sem.x_ready)
            dve.wait_ge(*at.last)
            modulated(3, 2, "norm1", 96)
            dve_mix2(dve, at, st, tt, ts, stt, unit, modulation)
            for g in range(4):
                unit()
                residual(B2_OUT + (g + 1) * GS, (MIX2 + g) % 2, g, 96 + 32)
            los(B2_UP, B2_UP + 3)
            modulation(st["unit"] - 1)
            dve.wait_ge(*at.last)
            modulated(4, 3, "norm2", 96 + 48)
            ffn(B2_UP, 1, [(8, 1, 29), (3, 0, 14)])
            modulation(st["unit"] - 1)
            dve.wait_ge(*at.last)
            down(B2_DOWN, 1, 96 + 80, 16, 0, 0)
            dve.wait_ge(*at.last)
            scaled(5, "norm_f", sem.y_ready)


def _slabs(w):
    k, n = w.shape
    return w.reshape(k // 256, 2, P, n // 512, 512).transpose(3, 0, 2, 1, 4).reshape(-1, P, SLAB)


def _down_slabs(w):
    return w.reshape(NFF, 2, 2, P, 2, 2, 512).transpose(4, 0, 5, 1, 3, 2, 6).reshape(-1, P, SLAB)


def _value_first(a):
    return np.concatenate([a[..., DFF:], a[..., :DFF]], -1)


def _up_slabs(w):
    v, g = _slabs(w[:, :DFF]), _slabs(w[:, DFF:])
    return np.concatenate([v.reshape(NFF, GS, P, SLAB), g.reshape(NFF, GS, P, SLAB)], 1).reshape(-1, P, SLAB)


def _ada(w):
    return w.reshape(2, 8, P, 48, 256).transpose(3, 0, 2, 1, 4).reshape(-1, P, 2048)


def _columns(v):
    return np.asarray(v).reshape(-1, P).T


def _padded_lora(w, axis):
    a = np.moveaxis(np.asarray(w), axis, 0)
    z = np.zeros((32,) + a.shape[1:], a.dtype)
    return np.moveaxis(np.concatenate([a[:96], z, a[96:192], z, a[192:]]), 0, axis)


def lay_out(inp):
    g = {k: np.asarray(v) for k, v in inp.items()}
    w = g["w_in"][0]
    ret, rw, mo = w[:, :1536], w[:, 1536:3520], w[:, 3520:]
    lora = _padded_lora(rw[:, 1536:], 1)
    w1 = np.concatenate([rw[:, :1536], lora, ret] + [mo[:, 1024 * c + 512 * h:1024 * c + 512 * h + 512]
                                                     for h in range(2) for c in range(3)], 1)
    w2 = g["w_in_2"]
    in2 = np.concatenate([w2[:, a:a + 512] for a in (1024, 1536, 2048, 0, 2560, 512, 3072, 3584)], 1)
    gate_order = [4 * k + h for k in (0, 2, 1, 3) for h in range(4)]
    wstream = np.concatenate([
        _slabs(w1), _slabs(g["w_out"][0]), _up_slabs(g["w_ffn_up"][0]), _down_slabs(g["w_ffn_down"][0]),
        _slabs(in2), _slabs(g["w_out_2"]), _up_slabs(_value_first(g["w_up_2"])), _down_slabs(g["w_down_2"])])
    assert wstream.shape[0] == N_SLABS
    ada = np.concatenate([_ada(g["w_ada"][0]), _ada(g["w_ada_2"])])
    mu = g["rwkv_mu"][0]
    mu = np.concatenate([mu[:1536], _padded_lora(mu[1536:], 0)])
    cols = np.concatenate([_columns(v) for v in (
        g["c"], g["c_2"], g["b_ada"], g["b_ada_2"], g["norm_mix"], g["norm_ffn"], g["norm_final"], g["norm1_w_2"],
        g["norm2_w_2"], g["norm_f_w_2"], mu, g["rwkv_w0"], g["rwkv_a0"], g["rwkv_k_k"], g["rwkv_k_a"],
        g["rwkv_r_k"], g["rwkv_ln_w"], g["rwkv_ln_b"], g["mlstm_norm_w_2"])]
        + [np.broadcast_to(g["b_gates_2"][None, gate_order], (P, 16))], 1)

    def conv(cw, cb, order):
        rows = np.stack([cw[order[0]], cw[order[1]], cw[order[2]], cb])
        return rows.reshape(4, 2, NFF, 4, P).transpose(4, 2, 1, 3, 0).reshape(P, NFF, 32)

    convs = np.stack([conv(g["ffn_conv_w"][0], g["ffn_conv_b"][0], (2, 1, 0)),
                      conv(_value_first(g["w_conv_2"]), _value_first(g["b_conv_2"]), (1, 0, 2))], 1)
    z = np.zeros((32, 512), np.float32)
    gup = g["rwkv_g_up"][0]
    rw_up = np.stack([np.concatenate([np.concatenate([g["rwkv_w_up"][0], z]), np.concatenate([g["rwkv_a_up"][0], z])], 1),
                      np.concatenate([gup[:P], gup[P:]], 1)], 1)
    wg = w2[:, 4096:][:, gate_order].reshape(KT, P, 16).transpose(1, 0, 2).reshape(P, 256)
    x = g["x"][0].T.reshape(KT, P, S).transpose(1, 0, 2)
    arrays = {"wstream": wstream, "adastream": ada, "x_in": x, "cols_in": cols, "conv_in": convs,
              "tabs_in": tables(), "rw_in": rw_up, "wg_in": wg}
    return {k: np.ascontiguousarray(v, dtype=np.float32) for k, v in arrays.items()}


def kernel(**inputs):
    import concourse.bacc as bacc
    from concourse.bass_utils import run_bass_kernel_spmd

    nc = bacc.Bacc("TRN2", target_bir_lowering=False, num_devices=1)
    arrays = lay_out(inputs)
    args = [nc.dram_tensor(k, v.shape, F32, kind="ExternalInput").ap() for k, v in arrays.items()]
    out = nc.dram_tensor("y_out", (P, KT, S), F32, kind="ExternalOutput").ap()
    build(nc, *args, out)
    r = run_bass_kernel_spmd(nc, [arrays], core_ids=[0])
    y = r.results[0]["y_out"]
    return np.asarray(y).transpose(2, 1, 0).reshape(1, S, D)
```

```python
from contextlib import ExitStack, contextmanager

import numpy as np
import concourse.bass as bass
from concourse import mybir

F32 = mybir.dt.float32
F32R = mybir.dt.float32r
ALU = mybir.AluOpType
ACT = mybir.ActivationFunctionType
AX_X = mybir.AxisListType.X

P = 128
S = 256
D = 2048
KT = D // P
DFF = 5632
NFF = DFF // 512
SLAB = 1024
RING = 4
GS = KT // 2
EPS = 1e-6
EXP_HALF = float(np.exp(-0.5))

G_RR, G_RK, G_RV, G_LORA, G_TQK, G_TV, G_TG, G_MQ0, G_MK0, G_MV0, G_MQ1, G_MK1, G_MV1 = range(13)
MIX1 = 13
MIX2 = 8
B1_OUT = MIX1 * GS
B1_UP = B1_OUT + 4 * GS
B1_DOWN = B1_UP + 2 * NFF * GS
DOWN_HALF = NFF * 4
B2 = B1_DOWN + 2 * DOWN_HALF
B2_OUT = B2 + MIX2 * GS
B2_UP = B2_OUT + 4 * GS
B2_DOWN = B2_UP + 2 * NFF * GS
N_SLABS = B2_DOWN + 2 * DOWN_HALF

COLS = {}
_at = 0
for _name, _n in [("c", 32), ("bada", 192), ("norm_mix", 16), ("norm_ffn", 16), ("norm_final", 16),
                  ("norm1", 16), ("norm2", 16), ("norm_f", 16), ("mu", 16), ("w0", 4), ("a0", 4),
                  ("k_k", 4), ("k_a", 4), ("r_k", 4), ("ln_w", 4), ("ln_b", 4), ("mlstm_norm", 8),
                  ("bgates", 16)]:
    COLS[_name] = _at
    _at += _n
NCOLS = _at

TABS = {}
_at = 0
for _name, _n in [("ident", 128), ("ones", 128), ("blk64", 128), ("strict", 128), ("incl", 128),
                  ("levels", 6 * 128), ("id64", 64), ("alibi", 256), ("retdecay", 4 * 256),
                  ("mfwd", 256), ("mbwd", 256), ("tri", 128), ("dft", 1024)]:
    TABS[_name] = (_at, _n)
    _at += _n
NTABS = _at
N_KEPT = TABS["id64"][0] + TABS["id64"][1]


UNITS1 = [0] + [2] * 4 + [1] * 4 + [2] * 4 + [1] * 4
UNITS2 = [0] + [2] * 5 + [1] * 6
START_UNITS = 16
START_PAIRS = 4
START_DVE = 12


def lo_signal(n):
    dve = sum((min(n + 1, n1) - n0) // 2 for n0, n1 in ((B1_UP, B2), (B2_UP, N_SLABS)) if n >= n0)
    if n % 2 and (B1_UP <= n < B2 or n >= B2_UP):
        return True, dve
    return False, n + 1 - dve


def lo_per(n, per):
    return per if n < B1_UP or B2 <= n < B2_UP else per // 2


def tables():
    t = np.zeros((P, NTABS), np.float32)

    def put(name, a):
        at, n = TABS[name]
        t[:, at:at + n] = np.asarray(a, np.float64).reshape(P, n)

    i = np.arange(P)
    row, col = i[:, None], i[None, :]
    same64 = row // 64 == col // 64
    put("ident", np.eye(P))
    put("ones", np.ones((P, P)))
    put("blk64", same64)
    put("strict", same64 & (row < col))
    put("incl", same64 & (row <= col))
    put("levels", np.stack([(row // (2 << l) == col // (2 << l)) & (row // (1 << l) < col // (1 << l))
                            for l in range(6)], 1))
    put("id64", np.concatenate([np.eye(64), np.eye(64)]))
    j = np.arange(S)[None, :]
    dist = (P + row) - j
    put("alibi", np.where(dist >= 0, -dist.astype(np.float64), -1e30))
    put("mfwd", np.where(dist >= 0, 0.0, -1e30))
    put("mbwd", np.where(j >= row, 0.0, -1e30))
    log_g = np.log1p(-np.exp2(-5.0 - np.arange(4)))
    q = np.arange(S)[None, :] - row
    put("retdecay", np.stack([np.where(q >= 0, np.exp(log_g[h] * np.maximum(q, 0)), 0.0) / 8.0
                              for h in range(4)], 1))
    put("tri", row <= col)
    n = np.arange(S)
    ang = 2 * np.pi * np.outer(n, n) / S
    cs = np.concatenate([np.cos(ang), np.sin(ang)], 1) / 16.0
    put("dft", cs.reshape(2, P, 512).transpose(1, 0, 2))
    return t


class Count:

    def __init__(self):
        self.n, self.i, self.per, self.last = {}, None, {}, None

    def up(self, sem):
        self.n[sem] = self.n.get(sem, 0) + 1
        v = self.n[sem]
        self.last = (sem, v if self.i is None else v + self.per.get(sem, 0) * self.i)
        return sem, 1

    @contextmanager
    def loop(self, eng, count, per):
        before = dict(self.n)
        with eng.Fori(0, count) as i:
            self.i, self.per = i, per
            yield i
        for sem in set(self.n) | set(per):
            a, b = before.get(sem, 0), self.n.get(sem, 0)
            assert b - a == per.get(sem, 0), (sem, b - a, per.get(sem, 0))
            self.n[sem] = a + (b - a) * count
        self.i, self.per, self.last = None, {}, None


class Semaphores:

    def __init__(self, nc, ctx):
        def new(name):
            return ctx.enter_context(nc.semaphore(name))

        self.w_landed = [new(f"w_landed{q}") for q in range(RING)]
        self.ada_landed = [new(f"ada_landed{q}") for q in range(2)]
        self.start_landed = [new(f"start_landed{q}") for q in range(2 * START_PAIRS)]
        self.step = new("step")
        self.a_act = new("a_act")
        self.a_done = new("a_done")
        self.acc_ready = new("acc_ready")
        self.ada_sum = new("ada_sum")
        self.ada_used = new("ada_used")
        self.bonus_ready = new("bonus_ready")
        self.bonus_sum = new("bonus_sum")
        self.bt_ready = new("bt_ready")
        self.c_made = new("c_made")
        self.cact_ready = new("cact_ready")
        self.ccol = new("ccol")
        self.chain = new("chain")
        self.cl = new("cl")
        self.cl_used = new("cl_used")
        self.clx = new("clx")
        self.cols_landed = new("cols_landed")
        self.conv_landed = new("conv_landed")
        self.cw_ready = new("cw_ready")
        self.d_done = new("d_done")
        self.decays = new("decays")
        self.den_made = new("den_made")
        self.dft_done = new("dft_done")
        self.dft_out = new("dft_out")
        self.f_abs = new("f_abs")
        self.f_exp = new("f_exp")
        self.f_ln = new("f_ln")
        self.f_out = new("f_out")
        self.fh = new("fh")
        self.floor_made = new("floor_made")
        self.free_gate = new("free_gate")
        self.free_val = new("free_val")
        self.g_act = new("g_act")
        self.g_done = new("g_done")
        self.g_made = new("g_made")
        self.gate_act = new("gate_act")
        self.gate_tap = new("gate_tap")
        self.gates = new("gates")
        self.gn_mean = new("gn_mean")
        self.gn_ms = new("gn_ms")
        self.gn_sd = new("gn_sd")
        self.gn_var = new("gn_var")
        self.gs_hi = new("gs_hi")
        self.gs_lo = new("gs_lo")
        self.gt_ready = new("gt_ready")
        self.h_hi = new("h_hi")
        self.h_out = new("h_out")
        self.h_ready = new("h_ready")
        self.head_made = new("head_made")
        self.hi_ready = new("hi_ready")
        self.hms = new("hms")
        self.hsd = new("hsd")
        self.hsq = new("hsq")
        self.hsum = new("hsum")
        self.hval = new("hval")
        self.kept = new("kept")
        self.kh_ready = new("kh_ready")
        self.kk0 = new("kk0")
        self.kk_ms = new("kk_ms")
        self.kk_sd = new("kk_sd")
        self.kk_sq = new("kk_sq")
        self.kk_sum = new("kk_sum")
        self.kt_ready = new("kt_ready")
        self.l2v = new("l2v")
        self.lo2_ready = new("lo2_ready")
        self.lo_ready = new("lo_ready")
        self.lora_act = new("lora_act")
        self.m_out = new("m_out")
        self.m_ready = new("m_ready")
        self.masked = new("masked")
        self.mix_hi = new("mix_hi")
        self.mix_split = new("mix_split")
        self.mo_biased = new("mo_biased")
        self.mo_exp = new("mo_exp")
        self.mo_max = new("mo_max")
        self.mo_out = new("mo_out")
        self.mo_p = new("mo_p")
        self.mo_pt = new("mo_pt")
        self.mo_scores = new("mo_scores")
        self.mo_turned = new("mo_turned")
        self.mo_values = new("mo_values")
        self.ms_ready = new("ms_ready")
        self.mt = new("mt")
        self.mt_turned = new("mt_turned")
        self.mu1_ready = new("mu1_ready")
        self.out_landed = new("out_landed")
        self.p_exp = new("p_exp")
        self.p_made = new("p_made")
        self.qy = new("qy")
        self.qy_add = new("qy_add")
        self.ret_masked = new("ret_masked")
        self.ret_ms = new("ret_ms")
        self.ret_out = new("ret_out")
        self.ret_scores = new("ret_scores")
        self.ret_sd = new("ret_sd")
        self.ret_sq = new("ret_sq")
        self.ret_sum = new("ret_sum")
        self.ret_values = new("ret_values")
        self.rk_ready = new("rk_ready")
        self.rows_made = new("rows_made")
        self.rows_out = new("rows_out")
        self.rt_ready = new("rt_ready")
        self.rw_mixed = new("rw_mixed")
        self.rw_out = new("rw_out")
        self.rw_self = new("rw_self")
        self.sc1 = new("sc1")
        self.sc1_out = new("sc1_out")
        self.sc2 = new("sc2")
        self.sc2_out = new("sc2_out")
        self.sd_ready = new("sd_ready")
        self.slab_used = new("slab_used")
        self.sq_ready = new("sq_ready")
        self.sq_used = new("sq_used")
        self.t_ready = new("t_ready")
        self.tables1_landed = new("tables1_landed")
        self.tables2_landed = new("tables2_landed")
        self.tabs_landed = new("tabs_landed")
        self.turned = new("turned")
        self.turned_out = new("turned_out")
        self.tx = new("tx")
        self.u_done = new("u_done")
        self.u_out = new("u_out")
        self.u_ready = new("u_ready")
        self.val_tap = new("val_tap")
        self.wg_hi = new("wg_hi")
        self.wg_ready = new("wg_ready")
        self.wz = new("wz")
        self.x_landed = new("x_landed")
        self.x_made = new("x_made")
        self.x_ready = new("x_ready")
        self.y_full = new("y_full")
        self.y_gated = new("y_gated")
        self.y_out = new("y_out")
        self.y_ready = new("y_ready")
        self.yc = new("yc")
        self.yc_sq = new("yc_sq")
        self.z_act = new("z_act")
        self.z_done = new("z_done")


def build(nc, wstream, adastream, x_in, cols_in, conv_in, tabs_in, rw_in, wg_in, out):
    ctx = ExitStack()
    with ctx:
        sem = Semaphores(nc, ctx)
        used = [0]
        base = nc.sbuf_base if isinstance(nc.sbuf_base, int) else nc.sbuf_base()
        base = (base + 63) // 64 * 64
        total = nc.sbuf_bytes_remaining() if callable(nc.sbuf_bytes_remaining) else nc.sbuf_bytes_remaining

        def sb(name, shape, dt=F32, offset=None):
            size = (int(np.prod(shape[1:])) * 4 + 31) // 32 * 32
            if offset is None:
                offset = base + used[0]
                used[0] += size
                assert used[0] <= total - 64, (name, used[0], total)
            t = nc.alloc_sbuf_tensor_at(name, shape, dt, offset=offset)
            return t, offset

        raw, _ = sb("raw", [P, RING, SLAB])
        whi, _ = sb("whi", [P, RING, SLAB], F32R)
        wlo, _ = sb("wlo", [P, RING, SLAB], F32R)
        hhi, _ = sb("hhi", [P, KT, S], F32R)
        hlo, _ = sb("hlo", [P, KT, S], F32R)
        ada_raw, _ = sb("ada_raw", [P, 2, 2048])
        acc, _ = sb("acc", [P, 2, 2, 256])
        cols, _ = sb("cols", [P, NCOLS])
        conv, _ = sb("conv", [P, 2, NFF, 32])
        modc, _ = sb("modc", [P, 192])
        cact, _ = sb("cact", [P, 32])
        tabs, _ = sb("tabs", [P, N_KEPT])
        colA, _ = sb("colA", [P, 16])
        mu1, _ = sb("mu1", [P, 20])
        cw, _ = sb("cw", [P, 32])
        small, _ = sb("small", [P, 256])
        rstd, _ = sb("rstd", [P, S])
        pc, _ = sb("pc", [P, 16])
        gshi, gs_at = sb("gshi", [P, 2, 4, S], F32R)
        gslo, _ = sb("gslo", [P, 2, 4, S], F32R)
        xT, _ = sb("xT", [P, KT, S])
        arena, _ = sb("arena", [P, 15, 1024])
        gT = arena[:, 0:11, :].rearrange("p a (b s) -> p (a b) s", s=S)
        gsf, _ = sb("gs_pages", [P, 4, 1024], F32, offset=gs_at)

        psum = ctx.enter_context(nc.psum_tensor("psum", [P, 8, 512], F32))
        bank = [psum[:, b, :] for b in range(8)]

        def tab(name):
            a, n = TABS[name]
            return tabs[:, a:a + n]

        def col(name, i, n=1):
            return cols[:, COLS[name] + i:COLS[name] + i + n]

        ident, ones, blk64 = tab("ident"), tab("ones"), tab("blk64")

        def page(i):
            if i < 15:
                return arena[:, i, :]
            if i < 19:
                return xT[:, 4 * (i - 15):4 * (i - 14), :].rearrange("p a s -> p (a s)")
            return gsf[:, i - 19, :]

        def tiles(i):
            return page(i).rearrange("p (a s) -> p a s", s=S)

        def halves(i):
            return page(i).rearrange("p (a s) -> p a s", s=512)

        def start_place(k, s):
            if k == 0:
                return ada_raw[:, s, :]
            return arena[:, 4 * k - 4 + 2 * s:4 * k - 2 + 2 * s, :].rearrange("p a n -> p (a n)")

        rstd2 = page(12)[:, 0:S]

        def pair(p):
            return psum[:, 2 * p:2 * p + 2, :].rearrange("p b (h s) -> p (b h) s", s=S)

        def flat(p):
            return psum[:, 2 * p:2 * p + 2, :].rearrange("p b s -> p (b s)")

        block = ctx.enter_context(nc.Block())

        def quarter(pg, h):
            return page(pg)[:, 512 * h:512 * h + 512].rearrange("p (m t) -> p m t", t=P)

        L1T, MT = quarter(13, 0), quarter(13, 1)
        G1T, G2T = quarter(14, 0), quarter(14, 1)
        TM, TT = quarter(11, 0), quarter(11, 1)
        UM, XM = quarter(12, 0), quarter(12, 1)
        WZ = quarter(2, 0)
        L2T = MT
        mstate = page(2)[:, 512:1024].rearrange("p (b t v) -> p b t v", b=2, v=64)
        FT = page(16).rearrange("p (t c j) -> p t c j", t=4, c=4)
        HM = page(17).rearrange("p (t c v) -> p t c v", t=4, c=4)
        scores = arena[:, 11:13, :].rearrange("p a n -> p (a n)")[:, 0:1536].rearrange("p (h n) -> p h n", n=384)
        mscores = xT[:, 4:12, :].rearrange("p a n -> p (a n)")[:, 0:1536].rearrange("p (h n) -> p h n", n=384)
        decayT = page(19).rearrange("p (h n) -> p h n", n=S)
        alibi = page(20)[:, 0:S]
        MOBA = [(7, 8, 9, 14), (10, 1, 5, 2)]
        MIXED1 = [13, 15, 14, 2]

        def rows(h):
            return slice(64 * h, 64 * h + 64)

        def pe_mix1(pe, st, mm, part, finish):
            def group(g, k0=0, k1=GS, kks=(0, 1)):
                part(g * GS, g % 2, k0, k1, "tok" if g in (G_TV, G_MV0, G_MV1) else None,
                     (sem.h_ready, 0) if g == 0 else None, kks)
                if k1 == GS and kks[-1] == 1:
                    st["free"][g % 2] = (sem.rw_mixed, g + 1) if g < 4 else (sem.kept, g - 3)

            halves_done = [0]

            def fill(n):
                for _ in range(n):
                    g, k = divmod(halves_done[0], 2 * GS)
                    group(G_TV + g, k // 2, k // 2 + 1, (k % 2,))
                    halves_done[0] += 1

            for g in range(4):
                group(g, 0, 4)
                if UNITS1[g] == 2:
                    finish()
                group(g, 4, 8)
                if UNITS1[g]:
                    finish()

            pe.wait_ge(sem.tables1_landed, 64)
            lo = tiles(3)
            group(G_TQK, 0, 2)
            pe.wait_ge(sem.lora_act, 1)
            for j in range(4):
                ins = mm(pair(2)[:, j, :], page(21)[:, j * P:(j + 1) * P], lo[:, 0, :], j % 2 == 0, True)
                if j == 3:
                    ins.then_inc(sem.z_done, 1)
            group(G_TQK, 2, 4)
            finish()
            pe.wait_ge(sem.z_act, 1)
            for j in range(4):
                ins = mm(pair(2)[:, j, :], page(21)[:, 512 + j * P:512 + (j + 1) * P], lo[:, 1, :], j % 2 == 0, True)
                if j == 3:
                    ins.then_inc(sem.a_done, 1)
            group(G_TQK, 4, 5)
            pe.wait_ge(sem.a_act, 1)
            pe.wait_ge(sem.lora_act, 2)
            for j in range(4):
                for kk in range(2):
                    ins = mm(pair(2)[:, j, :], page(22)[:, kk * 512 + j * P:kk * 512 + (j + 1) * P],
                       lo[:, 2 + kk, :], j % 2 == 0 and kk == 0, kk == 1)
                    if j == 3 and kk:
                        ins.then_inc(sem.g_done, 1)
            group(G_TQK, 5, 6)
            finish()
            pe.wait_ge(sem.g_act, 1)
            pe.wait_ge(sem.kk_sq, 1)
            for b in range(2):
                ins = mm(bank[4 + b], blk64, halves(11)[:, b, :], True, True)
                if b:
                    ins.then_inc(sem.kk_sum, 1)
            group(G_TQK, 6, 7)
            pe.wait_ge(sem.rk_ready, 1)
            pe.wait_ge(sem.kk_ms, 1)
            for b in range(2):
                ins = mm(bank[4 + b], blk64, halves(13)[:, b, :], True, True)
                if b:
                    ins.then_inc(sem.bonus_sum, 1)
            group(G_TQK, 7, 8)

            turned = 0
            for src, ready_ in ((2, sem.bonus_ready), (4, sem.kt_ready), (5, sem.bt_ready), (1, sem.kh_ready)):
                pe.wait_ge(ready_, 1)
                for b in range(2):
                    if turned >= 3:
                        pe.wait_ge(sem.turned_out, turned - 2)
                    o = bank[(6, 4, 5)[turned % 3]]
                    for j in range(4):
                        ins = nc.tensor.transpose(o[:, j * P:(j + 1) * P], tiles(src)[:, j, b * P:(b + 1) * P], ident)
                        if j == 3:
                            ins.then_inc(sem.turned, 1)
                    turned += 1

            pe.wait_ge(sem.rt_ready, 1)
            pe.wait_ge(sem.turned_out, 8)
            for t in range(4):
                def scores_of(src, banks, signal):
                    for h in range(2):
                        for kind, right in enumerate((4, 0)):
                            for b in range(2):
                                tok = slice(b * P, (b + 1) * P)
                                ins = mm(banks[h][:, kind * S + b * P:kind * S + (b + 1) * P],
                                   tiles(src)[rows(h), t, tok], tiles(right)[rows(h), t, tok], True, True)
                                if h and kind and b:
                                    ins.then_inc(signal, 1)

                if t:
                    pe.wait_ge(sem.qy_add, t)
                    pe.wait_ge(sem.h_out, t)
                    pe.wait_ge(sem.f_out, t)
                scores_of(5, (bank[4], bank[5]), sem.sc1)
                fill(1)
                pe.wait_ge(sem.sc1_out, t + 1)
                scores_of(1, (bank[6], bank[4]), sem.sc2)
                fill(1)
                pe.wait_ge(sem.sc2_out, t + 1)
                for m in range(4):
                    b, h = divmod(m, 2)
                    ins = mm(bank[5][:, m * 64:(m + 1) * 64], L2T[:, m, :],
                       halves(7)[:, b, t * P + h * 64:t * P + h * 64 + 64], True, True)
                    if m == 3:
                        ins.then_inc(sem.l2v, 1)
                fill(1)
                pe.wait_ge(sem.mt, 6 * t + 1)
                for m in range(4):
                    ins = nc.tensor.transpose(bank[6][:, m * P:(m + 1) * P], MT[:, m, :], ident)
                    if m == 3:
                        ins.then_inc(sem.mt_turned, 1)
                fill(1)
                for l in range(1, 6):
                    pe.wait_ge(sem.mt, 6 * t + l + 1)
                    pe.wait_ge(sem.t_ready, 6 * t + l)
                    for m in range(4):
                        ins = mm(bank[4][:, m * P:(m + 1) * P], MT[:, m, :], TM[:, m, :], True, True)
                        if m == 3:
                            ins.then_inc(sem.u_done, 1)
                    fill(1)
                    pe.wait_ge(sem.u_out, 5 * t + l)
                    if l < 5:
                        for m in range(4):
                            mm(bank[5][:, m * P:(m + 1) * P], TT[:, m, :], UM[:, m, :], True, True)
                    for m in range(4):
                        ins = mm(bank[6][:, m * P:(m + 1) * P], UM[:, m, :], TT[:, m, :], True, True)
                        if m == 3:
                            ins.then_inc(sem.d_done, 1)
                    fill(1)
                fill(1)
                pe.wait_ge(sem.t_ready, 6 * t + 6)
                pe.wait_ge(sem.x_made, t + 1)
                for m in range(4):
                    ins = mm(bank[4][:, m * P:(m + 1) * P], TT[:, m, :], XM[:, m, :], True, True)
                    if m == 3:
                        ins.then_inc(sem.tx, 1)
                fill(1)
                pe.wait_ge(sem.wz, t + 1)
                for h in range(2):
                    for b in range(2):
                        m = 2 * b + h
                        vt = halves(7)[:, b, t * P + h * 64:t * P + h * 64 + 64]
                        mm(bank[5][rows(h), b * P:(b + 1) * P], WZ[:, m, 0:64], G1T[:, m, :], b == 0)
                        mm(bank[5][rows(h), S + b * P:S + (b + 1) * P], WZ[:, m, 64:128], G1T[:, m, :], False, False)
                        ins = mm(bank[5][rows(h), S + b * P:S + (b + 1) * P], vt, G2T[:, m, :], False, True)
                        if h and b:
                            ins.then_inc(sem.qy, 1)
                for cc in range(2):
                    o = bank[(6, 4)[cc]]
                    r = rows(cc)
                    for h in range(2):
                        for b in range(2):
                            m = 2 * b + h
                            ch = slice(t * P + h * 64, t * P + h * 64 + 64)
                            bt, kh, vt = (halves(pg)[r, b, ch] for pg in (9, 10, 7))
                            mm(o[rows(h), b * 64:b * 64 + 64], WZ[r, m, 0:64], bt, b == 0)
                            mm(o[rows(h), P + b * 64:P + b * 64 + 64], bt, WZ[r, m, 64:128], False, False)
                            ins = mm(o[rows(h), P + b * 64:P + b * 64 + 64], kh, vt, False, True)
                            if cc and h and b:
                                ins.then_inc(sem.fh, 1)
                finish()

            for c in range(1, 4):
                pe.wait_ge(sem.m_ready, c)
                if c == 1:
                    pe.wait_ge(sem.qy_add, 4)
                    pe.wait_ge(sem.h_out, 4)
                    pe.wait_ge(sem.f_out, 4)
                for h in range(2):
                    for t in range(4):
                        m = mstate[rows(h), (c - 1) % 2, t, :]
                        ins = mm(bank[4 + h][rows(h), t * 64:t * 64 + 64], m,
                           tiles(0)[rows(h), t, c * 64:c * 64 + 64], True, True)
                        if c == 3 and h and t == 3:
                            ins.then_inc(sem.chain, 1)
                        if c < 3:
                            ins = mm(bank[4 + h][rows(h), S + t * 64:S + t * 64 + 64], FT[rows(h), t, c, :], m, True, True)
                            if h and t == 3:
                                ins.then_inc(sem.chain, 1)
                if c > 1:
                    finish()
                fill((6, 6, 4)[c - 1])
            pe.wait_ge(sem.y_full, 1)
            for b in range(2):
                ins = mm(bank[4 + b], blk64, halves(15)[:, b, :], True, True)
                if b:
                    ins.then_inc(sem.gn_mean, 1)
            finish()
            fill(6)
            pe.wait_ge(sem.yc_sq, 1)
            for b in range(2):
                ins = mm(bank[4 + b], blk64, halves(4)[:, b, :], True, True)
                if b:
                    ins.then_inc(sem.gn_var, 1)
            finish()
            fill(6)

            pe.wait_ge(sem.kept, 3)
            for h in range(4):
                o, r, tq = bank[(6, 4, 5, 6)[h]], rows(h % 2), h // 2
                if h == 1:
                    pe.wait_ge(sem.gn_ms, 1)
                if h == 3:
                    finish()
                    fill(6)
                    pe.wait_ge(sem.ret_masked, 1)
                mm(o[:, 0:S], tiles(18)[r, 2 + tq, 0:P], tiles(18)[r, tq, :], True)
                mm(o[:, S:S + P], tiles(18)[r, 2 + tq, P:S], tiles(18)[r, tq, P:S], True, True).then_inc(sem.ret_scores, 1)
            fill(2)
            pe.wait_ge(sem.ret_masked, 4)
            for h in range(4):
                o = bank[4 + h // 2][:, (h % 2) * S:(h % 2 + 1) * S]
                mm(o, halves(21)[:, 0, h * P:(h + 1) * P], scores[:, h, 0:S], h % 2 == 0, False)
                ins = mm(o[:, P:S], halves(21)[:, 1, h * P:(h + 1) * P], scores[:, h, S:S + P], False, True)
                if h == 3:
                    ins.then_inc(sem.ret_values, 1)
            fill(6)
            finish()
            pe.wait_ge(sem.ret_sq, 1)
            for b in range(2):
                ins = mm(bank[4 + b], ones, halves(14)[:, b, :], True, True)
                if b:
                    ins.then_inc(sem.ret_sum, 1)

            def moba_scores(n):
                q, k, _, _ = MOBA[n]
                for h in range(4):
                    o = bank[(6, 4, 5, 6)[h]]
                    if h == 0:
                        pe.wait_ge(sem.kept, 5 + 3 * n)
                        pe.wait_ge(sem.ret_masked if n == 0 else sem.mo_out, 4 if n == 0 else 1)
                    if h == 1 and n == 0:
                        pe.wait_ge(sem.ret_ms, 1)
                    if h == 3:
                        pe.wait_ge(sem.mo_biased, 4 * n + 1)
                    mm(o[:, 0:P], tiles(q)[:, h, 0:P], tiles(k)[:, h, 0:P], True)
                    mm(o[:, P:P + S], tiles(q)[:, h, P:S], tiles(k)[:, h, :], True, True).then_inc(sem.mo_scores, 1)

            def moba_turn(n):
                pe.wait_ge(sem.mo_p, n + 1)
                for h in range(4):
                    o = bank[(6, 4, 5, 6)[h]]
                    if h == 3:
                        pe.wait_ge(sem.mo_pt, 4 * n + 1)
                    for i in range(3):
                        ins = nc.tensor.transpose(o[:, i * P:(i + 1) * P], mscores[:, h, i * P:(i + 1) * P], ident)
                    ins.then_inc(sem.mo_turned, 1)

            def moba_values(n):
                v = halves(MOBA[n][2])
                pe.wait_ge(sem.mo_pt, 4 * n + 4)
                pe.wait_ge(sem.kept, 6 + 3 * n)
                for h in range(4):
                    o = bank[4 + h // 2][:, (h % 2) * S:(h % 2 + 1) * S]
                    mm(o, v[:, 0, h * P:(h + 1) * P], scores[:, h, 0:S], h % 2 == 0, False)
                    ins = mm(o[:, P:S], v[:, 1, h * P:(h + 1) * P], scores[:, h, S:S + P], False, True)
                    if h == 3:
                        ins.then_inc(sem.mo_values, 1)

            moba_scores(0)
            fill(8)
            moba_turn(0)
            fill(2)
            finish()
            moba_values(0)
            fill(4)
            moba_scores(1)
            finish()
            fill(4)
            moba_turn(1)
            fill(4)
            moba_values(1)

        def act_mix1(act, copy, fn, his):
            def kept(g, dst, f=ACT.Copy, scale=1.0):
                act.wait_ge(sem.slab_used, (g + 1) * GS)
                nc.scalar.activation(page(dst), flat(g % 2), f, scale=scale).then_inc(sem.kept, 1)

            act.wait_ge(sem.mu1_ready, 1)
            for g in range(4):
                his(g * GS + 3, (g + 1) * GS + 3)
                act.wait_ge(sem.slab_used, (g + 1) * GS)
                for j in range(4):
                    c = 4 * g + j
                    ins = fn(tiles(g)[:, j, :], pair(g % 2)[:, j, :], ACT.Identity, scale=mu1[:, c:c + 1])
                    if j == 3:
                        ins.then_inc(sem.rw_self, 1)
            act.wait_ge(sem.rw_mixed, 4)
            fn(tiles(3)[:, 0, :], tiles(3)[:, 0, :], ACT.Tanh).then_inc(sem.lora_act, 1)
            fn(halves(3)[:, 1, :], halves(3)[:, 1, :], ACT.Sigmoid).then_inc(sem.lora_act, 1)
            act.wait_ge(sem.z_done, 1)
            for j in range(4):
                ins = fn(tiles(4)[:, j, :], pair(2)[:, j, :], ACT.Sigmoid, bias=col("w0", j))
                if j == 3:
                    ins.then_inc(sem.z_act, 1)
            his(G_TQK * GS + 3, G_TQK * GS + 7)
            act.wait_ge(sem.a_done, 1)
            for j in range(4):
                ins = fn(tiles(5)[:, j, :], pair(2)[:, j, :], ACT.Sigmoid, bias=col("a0", j))
                if j == 3:
                    ins.then_inc(sem.a_act, 1)
            his(G_TQK * GS + 7, G_TQK * GS + 8)
            act.wait_ge(sem.cl, 1)
            fn(page(8), page(7), ACT.Exp).then_inc(sem.decays, 1)
            fn(page(9), page(7), ACT.Exp, scale=-1.0).then_inc(sem.decays, 1)
            act.wait_ge(sem.clx, 1)
            fn(page(4), page(4), ACT.Exp).then_inc(sem.decays, 1)
            his(G_TQK * GS + 8, G_TQK * GS + 9)
            act.wait_ge(sem.g_done, 1)
            copy(page(6), flat(2)).then_inc(sem.g_act, 1)
            act.wait_ge(sem.kk0, 1)
            fn(page(11), page(10), ACT.Square).then_inc(sem.kk_sq, 1)
            his(G_TQK * GS + 9, G_TQK * GS + 10)
            act.wait_ge(sem.kk_ms, 1)
            fn(page(11), page(11), ACT.Sqrt).then_inc(sem.kk_sd, 1)
            his(G_TQK * GS + 10, G_TQK * GS + 11)
            kept(G_TQK, 18)
            for n in range(8):
                act.wait_ge(sem.turned, n + 1)
                if n == 2:
                    act.wait_ge(sem.cl_used, 1)
                if n == 4:
                    act.wait_ge(sem.kh_ready, 1)
                copy(halves(7 + n // 2)[:, n % 2, :], bank[(6, 4, 5)[n % 3]]).then_inc(sem.turned_out, 1)
            ahead = [G_TV * GS + 3]

            def upto(f):
                his(ahead[0], G_TV * GS + f + 3)
                ahead[0] = G_TV * GS + f + 3

            for t in range(4):
                f = 8 * t
                upto(f + 2)
                if t in (1, 2):
                    kept(*((G_TV, 21), (G_TG, 22, ACT.Silu))[t - 1])
                for l in range(1, 6):
                    act.wait_ge(sem.u_done, 5 * t + l)
                    copy(UM, bank[4].rearrange("p (m t) -> p m t", t=P)).then_inc(sem.u_out, 1)
                    upto(f + 2 + l)
                act.wait_ge(sem.tx, t + 1)
                copy(WZ, bank[4].rearrange("p (m t) -> p m t", t=P), scale=-1.0).then_inc(sem.wz, 1)
                upto(f + 8)
                act.wait_ge(sem.qy, t + 1)
                copy(tiles(15)[:, t, :], bank[5][:, S:2 * S]).then_inc(sem.y_out, 1)
                act.wait_ge(sem.fh, t + 1)
                for cc in range(2):
                    ins = copy(HM[:, t, cc::2, :], bank[(6, 4)[cc]][:, P:2 * P].rearrange("p (b v) -> p b v", v=64))
                    if cc:
                        ins.then_inc(sem.h_out, 1)
            kept(G_MQ0, 7, scale=P ** -0.5)
            kept(G_MK0, 8)
            upto(32 + 8)
            act.wait_ge(sem.yc, 1)
            fn(page(4), page(15), ACT.Square).then_inc(sem.yc_sq, 1)
            upto(32 + 10)
            kept(G_MV0, 9)
            upto(32 + 11)
            act.wait_ge(sem.gn_ms, 1)
            fn(page(4), page(4), ACT.Sqrt).then_inc(sem.gn_sd, 1)
            upto(32 + 18)
            kept(G_MQ1, 10, scale=P ** -0.5)
            act.wait_ge(sem.ret_values, 1)
            copy(page(13), flat(2))
            nc.scalar.activation(page(14), flat(2), ACT.Square).then_inc(sem.ret_sq, 1)
            upto(32 + 21)
            act.wait_ge(sem.ret_ms, 1)
            fn(page(14), page(14), ACT.Sqrt).then_inc(sem.ret_sd, 1)

            def moba_exp(n):
                act.wait_ge(sem.mo_max, n + 1)
                for h in range(4):
                    for ib in range(2):
                        s = mscores[:, h, P * ib:P + S * ib]
                        c = 4 * ib + h
                        ins = nc.scalar.activation(s, s, ACT.Exp, bias=small[:, c:c + 1],
                                                   accum_out=small[:, 8 + c:9 + c])
                        if h == 3 and ib:
                            ins.then_inc(sem.mo_exp, 1)

            def moba_turned(n, h):
                act.wait_ge(sem.mo_turned, 4 * n + h + 1)
                copy(scores[:, h, :], bank[(6, 4, 5, 6)[h]][:, 0:384]).then_inc(sem.mo_pt, 1)

            def moba_out(n):
                act.wait_ge(sem.mo_values, n + 1)
                copy(page(MOBA[n][3]), flat(2)).then_inc(sem.mo_out, 1)

            upto(32 + 22)
            moba_exp(0)
            upto(32 + 25)
            kept(G_MK1, 1)
            for h in range(4):
                moba_turned(0, h)
            upto(32 + 26)
            act.wait_ge(sem.ret_out, 1)
            moba_out(0)
            upto(32 + 28)
            moba_exp(1)
            upto(32 + 30)
            for h in range(4):
                moba_turned(1, h)
            upto(32 + 32)
            kept(G_MV1, 5)
            moba_out(1)
            for k, pg in enumerate(MIXED1):
                act.wait_ge(*((sem.ret_out, 1), (sem.rw_out, 1), (sem.mo_out, 1), (sem.mo_out, 2))[k])
                copy(hhi[:, 4 * k:4 * k + 4, :], tiles(pg)).then_inc(sem.mix_hi, 1)

        def dve_mix1(dve, at, st, tt, ts, stt, unit, unit_pieces):
            V = nc.vector
            ts(mu1[:, 0:16], col("mu", 0, 16), -1.0, 1.0, ALU.mult, ALU.add).then_inc(*at.up(sem.step))
            ts(mu1[:, 16:20], col("k_a", 0, 4), -1.0, 1.0, ALU.mult, ALU.add).then_inc(*at.up(sem.mu1_ready))
            for g in range(4):
                for _ in range(UNITS1[g]):
                    unit()
                dve.wait_ge(sem.rw_self, g + 1)
                for j in range(4):
                    c = 4 * g + j
                    t = tiles(g)[:, j, :]
                    stt(t[:, 1:S], pair(g % 2)[:, j, 0:S - 1], col("mu", c), t[:, 1:S], ALU.mult, ALU.add).then_inc(*at.up(sem.rw_mixed if j == 3 else sem.step))
            unit()
            V.memset(page(12), 1.0).then_inc(*at.up(sem.step))
            one = at.last
            for j in range(4):
                ts(tiles(10)[:, j, :], tiles(1)[:, j, :], col("k_k", j), None, ALU.mult).then_inc(*at.up(sem.kk0 if j == 3 else sem.step))
            dve.wait_ge(*one)
            V.memset(page(12).rearrange("p (c s) -> p c s", s=64)[:, :, 0:1], 0.0).then_inc(*at.up(sem.step))
            dve.wait_ge(sem.z_act, 1)
            ts(page(4), page(4), -EXP_HALF, None, ALU.mult).then_inc(*at.up(sem.step))
            dve.wait_ge(*at.last)
            V.tensor_tensor_scan(page(7), page(12), page(4), 0.0, ALU.mult, ALU.add).then_inc(*at.up(sem.cl))
            dve.wait_ge(*at.last)
            tt(page(4), page(7), page(4), ALU.subtract).then_inc(*at.up(sem.clx))
            unit()
            dve.wait_ge(sem.a_act, 1)
            for j in range(4):
                ts(tiles(12)[:, j, :], tiles(5)[:, j, :], col("k_a", j), mu1[:, 16 + j:17 + j], ALU.mult, ALU.add).then_inc(*at.up(sem.step))
            dve.wait_ge(*at.last)
            tt(page(1), page(1), page(12), ALU.mult).then_inc(*at.up(sem.step))
            dve.wait_ge(*at.last)
            tt(page(13), page(0), page(1), ALU.mult).then_inc(*at.up(sem.step))
            dve.wait_ge(*at.last)
            for j in range(4):
                ts(tiles(13)[:, j, :], tiles(13)[:, j, :], col("r_k", j), None, ALU.mult).then_inc(*at.up(sem.rk_ready if j == 3 else sem.step))
            dve.wait_ge(sem.kk_sum, 1)
            ts(page(11), flat(2), 1e-24, None, ALU.max).then_inc(*at.up(sem.kk_ms))
            dve.wait_ge(sem.decays, 3)
            V.tensor_copy(pc[:].rearrange("p (t c) -> p t c", c=4),
                               tiles(8).rearrange("p t (c s) -> p t c s", s=64)[:, :, :, 63]).then_inc(*at.up(sem.cl_used))
            tt(page(0), page(0), page(8), ALU.mult).then_inc(*at.up(sem.rt_ready))
            dve.wait_ge(sem.kk_sd, 1)
            V.reciprocal(page(11), page(11)).then_inc(*at.up(sem.step))
            dve.wait_ge(*at.last)
            tt(page(10), page(10), page(11), ALU.mult).then_inc(*at.up(sem.step))
            dve.wait_ge(*at.last)
            tt(page(4), page(10), page(4), ALU.mult).then_inc(*at.up(sem.kt_ready))
            dve.wait_ge(sem.bonus_sum, 1)
            tt(page(3), flat(2), page(2), ALU.mult).then_inc(*at.up(sem.bonus_ready))
            tt(page(5), page(5), page(10), ALU.mult).then_inc(*at.up(sem.step))
            dve.wait_ge(*at.last)
            tt(page(5), page(5), page(9), ALU.mult).then_inc(*at.up(sem.bt_ready))
            tt(page(1), page(1), page(9), ALU.mult).then_inc(*at.up(sem.kh_ready))

            def masked(h, o, src, mask):
                return tt(o.rearrange("p (b h) t -> p b h t", h=2)[:, :, h, :],
                          src.rearrange("p (b t) -> p b t", t=P),
                          tab(mask).unsqueeze(1).broadcast_to([P, 2, P]), ALU.mult)

            def level(l):
                return tabs[:, TABS["levels"][0] + l * P:TABS["levels"][0] + (l + 1) * P
                            ].unsqueeze(1).broadcast_to([P, 4, P])

            eye = ident.unsqueeze(1).broadcast_to([P, 4, P])
            for t in range(4):
                dve.wait_ge(sem.sc1, t + 1)
                for h in range(2):
                    masked(h, L1T, bank[4 + h][:, 0:S], "strict").then_inc(*at.up(sem.step))
                    masked(h, G1T, bank[4 + h][:, S:2 * S], "incl").then_inc(*at.up(sem.sc1_out if h else sem.step))
                dve.wait_ge(sem.sc2, t + 1)
                for h, bk in ((0, bank[6]), (1, bank[4])):
                    masked(h, L2T, bk[:, 0:S], "strict").then_inc(*at.up(sem.step))
                    masked(h, G2T, bk[:, S:2 * S], "incl").then_inc(*at.up(sem.sc2_out if h else sem.step))
                dve.wait_ge(sem.l2v, t + 1)
                V.tensor_copy(XM[:, :, 64:128], bank[5][:, 0:S].rearrange("p (m v) -> p m v", v=64)).then_inc(*at.up(sem.step))
                V.tensor_copy(XM[:, :, 0:64].rearrange("p (b h) v -> p b h v", h=2),
                                   halves(8)[:, :, t * P:(t + 1) * P].rearrange("p b (h v) -> p b h v", h=2)).then_inc(*at.up(sem.x_made))
                tt(MT, L1T, level(0), ALU.mult).then_inc(*at.up(sem.mt))
                dve.wait_ge(*at.last)
                tt(TT, eye, MT, ALU.subtract).then_inc(*at.up(sem.step))
                dve.wait_ge(sem.mt_turned, t + 1)
                tt(TM, eye, bank[6].rearrange("p (m t) -> p m t", t=P), ALU.subtract).then_inc(*at.up(sem.t_ready))
                dve.wait_ge(*at.last)
                tt(MT, L1T, level(1), ALU.mult).then_inc(*at.up(sem.mt))
                pieces = unit_pieces()
                for l in range(1, 6):
                    dve.wait_ge(sem.u_done, 5 * t + l)
                    if l < 5:
                        tt(MT, L1T, level(l + 1), ALU.mult).then_inc(*at.up(sem.mt))
                    next(pieces)
                    dve.wait_ge(sem.d_done, 5 * t + l)
                    if l < 5:
                        tt(TM, TM, bank[5].rearrange("p (m t) -> p m t", t=P), ALU.subtract).then_inc(*at.up(sem.step))
                    tt(TT, TT, bank[6].rearrange("p (m t) -> p m t", t=P), ALU.subtract).then_inc(*at.up(sem.t_ready))
                dve.wait_ge(sem.y_out, t + 1)
                tt(tiles(0)[:, t, :], tiles(0)[:, t, :], bank[5][:, 0:S], ALU.add).then_inc(*at.up(sem.qy_add))
                dve.wait_ge(sem.h_out, t + 1)
                for cc in range(2):
                    tt(FT[:, t, cc::2, :], bank[(6, 4)[cc]][:, 0:P].rearrange("p (b j) -> p b j", j=64),
                       tab("id64").unsqueeze(1).broadcast_to([P, 2, 64]), ALU.add).then_inc(*at.up(sem.f_out if cc else sem.step))

            pcv = pc[:].rearrange("p (t c) -> p t c", c=4)

            def decayed(c, src):
                tt(mstate[:, c % 2, :, :], src, pcv[:, :, c:c + 1].broadcast_to([P, 4, 64]), ALU.mult).then_inc(*at.up(sem.m_ready))

            dve.wait_ge(sem.h_out, 4)
            decayed(0, HM[:, :, 0, :])
            for c in range(1, 4):
                dve.wait_ge(sem.chain, c)
                for h in range(2):
                    r, ps = rows(h), bank[4 + h][rows(h), :].rearrange("p (k t v) -> p k t v", k=2, v=64)
                    y = tiles(15)[r, :, c * 64:c * 64 + 64]
                    if c == 1 and h == 0:
                        dve.wait_ge(sem.y_out, 4)
                    if c < 3:
                        tt(mstate[r, c % 2, :, :], ps[:, 1, :, :], HM[r, :, c, :], ALU.add).then_inc(*at.up(sem.step))
                    tt(y, ps[:, 0, :, :], y, ALU.add).then_inc(*at.up(sem.y_full if c == 3 and h else sem.step))
                if c < 3:
                    dve.wait_ge(*at.last)
                    decayed(c, mstate[:, c % 2, :, :])
                unit()
            dve.wait_ge(sem.gn_mean, 1)
            stt(page(15), flat(2), -1.0 / 64, page(15), ALU.mult, ALU.add).then_inc(*at.up(sem.yc))
            unit()
            dve.wait_ge(sem.gn_var, 1)
            ts(page(4), flat(2), 1.0 / 64, 64e-5, ALU.mult, ALU.add).then_inc(*at.up(sem.gn_ms))
            unit()
            dve.wait_ge(sem.gn_sd, 1)
            V.reciprocal(page(4), page(4)).then_inc(*at.up(sem.step))
            dve.wait_ge(*at.last)
            tt(page(15), page(15), page(4), ALU.mult).then_inc(*at.up(sem.step))
            dve.wait_ge(*at.last)
            for j in range(4):
                y = tiles(15)[:, j, :]
                ts(y, y, col("ln_w", j), col("ln_b", j), ALU.mult, ALU.add).then_inc(*at.up(sem.step))
            dve.wait_ge(*at.last)
            tt(page(15), page(15), page(3), ALU.add).then_inc(*at.up(sem.step))
            dve.wait_ge(*at.last)
            tt(page(15), page(15), page(6), ALU.mult).then_inc(*at.up(sem.rw_out))

            for h in range(4):
                o = bank[(6, 4, 5, 6)[h]]
                dve.wait_ge(sem.ret_scores, h + 1)
                tt(scores[:, h, 0:S], o[:, 0:S], decayT[:, h, :], ALU.mult).then_inc(*at.up(sem.step))
                tt(scores[:, h, S:S + P], o[:, S:S + P], decayT[:, h, 0:P], ALU.mult).then_inc(*at.up(sem.ret_masked))
            unit()
            dve.wait_ge(sem.ret_sum, 1)
            ts(page(14), flat(2), 1.0 / P, EPS, ALU.mult, ALU.add).then_inc(*at.up(sem.ret_ms))

            def moba_bias(n):
                for h in range(4):
                    o = bank[(6, 4, 5, 6)[h]]
                    slope = 2.0 ** -(4 * n + h + 1)
                    dve.wait_ge(sem.mo_scores, 4 * n + h + 1)
                    stt(mscores[:, h, 0:P], alibi[:, P:S], slope, o[:, 0:P], ALU.mult, ALU.add).then_inc(*at.up(sem.step))
                    stt(mscores[:, h, P:P + S], alibi, slope, o[:, P:P + S], ALU.mult, ALU.add).then_inc(*at.up(sem.mo_biased))
                dve.wait_ge(*at.last)
                V.tensor_reduce(small[:, 0:4], mscores[:, :, 0:P], AX_X, ALU.max).then_inc(*at.up(sem.step))
                V.tensor_reduce(small[:, 4:8], mscores[:, :, P:P + S], AX_X, ALU.max).then_inc(*at.up(sem.step))
                dve.wait_ge(*at.last)
                ts(small[:, 0:8], small[:, 0:8], -1.0, None, ALU.mult).then_inc(*at.up(sem.mo_max))

            def moba_norm(n):
                dve.wait_ge(sem.mo_exp, n + 1)
                V.reciprocal(small[:, 8:16], small[:, 8:16]).then_inc(*at.up(sem.step))
                dve.wait_ge(*at.last)
                for h in range(4):
                    for ib in range(2):
                        s = mscores[:, h, P * ib:P + S * ib]
                        c = 8 + 4 * ib + h
                        ts(s, s, small[:, c:c + 1], None, ALU.mult).then_inc(*at.up(sem.mo_p if h == 3 and ib else sem.step))

            moba_bias(0)
            dve.wait_ge(sem.ret_sd, 1)
            V.reciprocal(page(14), page(14)).then_inc(*at.up(sem.step))
            dve.wait_ge(*at.last)
            tt(page(13), page(13), page(14), ALU.mult).then_inc(*at.up(sem.step))
            dve.wait_ge(*at.last)
            dve.wait_ge(sem.kept, 3)
            tt(page(13), page(13), page(22), ALU.mult).then_inc(*at.up(sem.ret_out))
            moba_norm(0)
            unit()
            unit()
            dve.wait_ge(sem.mo_out, 1)
            moba_bias(1)
            moba_norm(1)
            for k, pg in enumerate(MIXED1):
                dve.wait_ge(sem.mix_hi, k + 1)
                tt(hlo[:, 4 * k:4 * k + 4, :], tiles(pg), hhi[:, 4 * k:4 * k + 4, :].bitcast(F32),
                   ALU.subtract).then_inc(*at.up(sem.mix_split))

        MQ, MK, MV, MU, MG, MY, MF = 0, 1, (2, 3), (4, 5), (6, 7), (8, 9), (10, 11)
        ORDER2 = ("q", "k", "v0", "u0", "v1", "u1", "g0", "g1")
        KEPT2 = {"q": MQ, "k": MK, "v0": MV[0], "v1": MV[1], "u0": MU[0], "u1": MU[1], "g0": MG[0], "g1": MG[1]}
        MIXED2 = (MF[0], MF[1], MY[0], MY[1])

        def kept2(name):
            return 9 + ORDER2.index(name) + 1

        wg_hi, wg_lo = gslo[:, 0, 0, :], gslo[:, 0, 1, :]
        dft = halves(19)
        gate_tok = page(22)[:, 0:256].rearrange("p (k b c) -> p k b c", k=2, b=2)
        gate_in = page(22)[:, 512:544].rearrange("p (b c) -> p b c", c=16)
        f_min = page(22)[:, 544:560].rearrange("p (b c) -> p b c", c=8)
        f_abs = page(22)[:, 560:576].rearrange("p (b c) -> p b c", c=8)
        row_c, row_m, row_b, row_s = (tiles(14)[:, k, :] for k in range(4))
        FWD, BWD, BOTH = slice(0, 32), slice(32, 64), slice(0, 64)
        ccol = pc[:].rearrange("p (b r) -> p b r", r=8)
        pf0, pf1 = page(21)[:, 0:256], page(21)[:, 256:384]
        pb0, pb1 = page(21)[:, 384:512], page(21)[:, 512:768]
        PARTS = ((pf0, 0, slice(0, S), 0), (pf1, 1, slice(P, S), 0), (pb1, 1, slice(0, S), 1), (pb0, 0, slice(0, P), 1))
        inv = page(22)[:, 0:512]
        floor_ = page(22)[:, 512:1024]
        hsq, hrms = page(13)[:, 0:512], page(13)[:, 512:768]
        mask_f, mask_b = page(20)[:, S:2 * S], page(20)[:, 0:S]

        def pe_mix2(pe, st, mm, part, finish):
            def slot(g, s):
                part(B2 + g * GS, g % 2, 2 * s, 2 * s + 2, "tok" if ORDER2[g][0] in "vu" else None,
                     (sem.h_ready, 8) if g == 0 else None)
                if s == 3:
                    st["free"][g % 2] = (sem.kept, 10 + g)
                if UNITS2[g] and (s == 3 or s == 1 and UNITS2[g] == 2):
                    finish()

            def head_scores(h):
                if h == 0:
                    pe.wait_ge(sem.kept, kept2("k"))
                    pe.wait_ge(sem.rows_out, 3)
                else:
                    pe.wait_ge(sem.m_out, h)
                for jb in range(2):
                    mm(bank[4][:, jb * S:(jb + 1) * S], tiles(MK)[:, h, jb * P:(jb + 1) * P], tiles(MQ)[:, h, :],
                       jb == 0)
                for bk, row in ((5, row_m), (6, row_s)):
                    for d in range(2):
                        r = 32 * d + h
                        ins = mm(bank[bk][:, d * S:(d + 1) * S], ident[BOTH, r:r + 1].broadcast_to([64, P]), row[BOTH, :],
                           d == 0, True)
                        if bk == 6 and d:
                            ins.then_inc(sem.head_made, 1)

            def head_den(h):
                pe.wait_ge(sem.p_made, h + 1)
                for n, (pp, jb, q, d) in enumerate(PARTS):
                    ins = mm(bank[5][:, d * S + q.start:d * S + q.stop], ones, pp, n == 0, True)
                    if n == 3:
                        ins.then_inc(sem.den_made, 1)

            def head_values(h):
                pe.wait_ge(sem.c_made, h + 1)
                pe.wait_ge(sem.kept, kept2("v0" if h < 2 else "v1"))
                v = halves(MV[h // 2])
                for t in range(2):
                    ch = slice((h % 2) * S + t * P, (h % 2) * S + (t + 1) * P)
                    mm(bank[4][:, t * S:(t + 1) * S], v[:, 0, ch], pf0, t == 0, False)
                    ins = mm(bank[4][:, t * S:(t + 1) * S], v[:, 1, ch], pb1, False, True)
                    if t:
                        ins.then_inc(sem.hval, 1)

            def head_rms(h):
                pe.wait_ge(sem.hsq, h + 1)
                for t in range(2):
                    ins = mm(bank[5][:, 0:S], ones, hsq[:, t * S:(t + 1) * S], t == 0, t == 1)
                    if t:
                        ins.then_inc(sem.hsum, 1)

            def fourier_tokens(n):
                pe.wait_ge(sem.kept, kept2(("u0", "u1")[n // 2]))
                if n:
                    pe.wait_ge(sem.dft_out, 3 * n)
                else:
                    pe.wait_ge(sem.m_out, 3)
                for dt in range(2):
                    for tb in range(2):
                        c = (n % 2) * S + dt * P
                        ins = mm(bank[(4, 5)[dt]], halves(MU[n // 2])[:, tb, c:c + P], dft[:, tb, :], tb == 0, tb == 1)
                        if tb:
                            ins.then_inc(sem.dft_done, 1)

            def fourier_channels(n):
                pe.wait_ge(sem.dft_out, 3 * n + 2)
                a = halves(12)
                for o in range(2):
                    for dt in range(2):
                        for cs in range(2):
                            ins = mm(bank[6][:, o * S:(o + 1) * S], dft[:, dt, cs * S + o * P:cs * S + (o + 1) * P],
                               a[:, dt, cs * S:(cs + 1) * S], o == 0 and dt == 0 and cs == 0, dt == 1 and cs == 1)
                            if o and dt and cs:
                                ins.then_inc(sem.dft_done, 1)

            for s in range(4):
                slot(0, s)
            pe.wait_ge(sem.wg_ready, 1)
            for tb in range(2):
                o = bank[6][:, tb * 16:(tb + 1) * 16]
                t = slice(tb * P, (tb + 1) * P)
                for kt in range(KT):
                    w = slice(kt * 16, kt * 16 + 16)
                    mm(o, hhi[:, kt, t], wg_hi[:, w], tb == 0 and kt == 0, False)
                    mm(o, hlo[:, kt, t], wg_hi[:, w], False, False)
                    ins = mm(o, hhi[:, kt, t], wg_lo[:, w], False, kt == KT - 1)
                    if tb and kt == KT - 1:
                        ins.then_inc(sem.gates, 1)
            slot(1, 0)
            slot(1, 1)
            pe.wait_ge(sem.gt_ready, 1)
            for k in range(2):
                for tb in range(2):
                    ins = mm(bank[4][BOTH, k * S + tb * P:k * S + (tb + 1) * P], gate_tok[:, k, tb, :], ident,
                       k == 0 and tb == 0, True)
                    if k and tb:
                        ins.then_inc(sem.rows_made, 1)
            slot(1, 2)
            slot(1, 3)
            slot(2, 0)
            pe.wait_ge(sem.rows_out, 1)
            for tb in range(2):
                ins = mm(bank[5][:, tb * 64:(tb + 1) * 64], row_c[BOTH, tb * P:(tb + 1) * P], ident[BOTH, 0:64],
                   tb == 0, True)
                if tb:
                    ins.then_inc(sem.ccol, 1)
            for s in range(1, 4):
                slot(2, s)
            for h, g in enumerate((3, 4, 5)):
                for s, step in enumerate((head_scores, head_den, head_values, head_rms)):
                    slot(g, s)
                    step(h)
            slot(6, 0)
            fourier_tokens(0)
            slot(6, 1)
            fourier_channels(0)
            pe.wait_ge(sem.dft_out, 3)
            head_scores(3)
            slot(6, 2)
            head_den(3)
            slot(6, 3)
            head_values(3)
            slot(7, 0)
            head_rms(3)
            slot(7, 1)
            pe.wait_ge(sem.m_out, 4)
            fourier_tokens(1)
            slot(7, 2)
            fourier_channels(1)
            fourier_tokens(2)
            slot(7, 3)
            fourier_channels(2)
            fourier_tokens(3)
            fourier_channels(3)

        def act_mix2(act, copy, fn, his):
            def kept(name):
                g = ORDER2.index(name)
                act.wait_ge(sem.slab_used, B2 + (g + 1) * GS)
                f, scale = (ACT.Sigmoid, 1.0) if name[0] == "g" else (ACT.Copy, P ** -0.5 if name == "q" else 1.0)
                nc.scalar.activation(page(KEPT2[name]), flat(g % 2), f, scale=scale).then_inc(sem.kept, 1)

            def ahead(g, s, n=2):
                n0 = B2 + g * GS + 2 * s + 3
                his(n0, n0 + n)

            def head(h, s):
                if s == 0:
                    act.wait_ge(sem.head_made, h + 1)
                    fn(floor_, bank[6], ACT.Exp).then_inc(sem.floor_made, 1)
                    act.wait_ge(sem.masked, h + 1)
                    for n, (pp, jb, q, d) in enumerate(PARTS):
                        ins = fn(pp, pp, ACT.Exp, bias=ccol[:, jb, 4 * d + h:4 * d + h + 1])
                        if n == 3:
                            ins.then_inc(sem.p_exp, 1)
                if s == 2:
                    act.wait_ge(sem.hval, h + 1)
                    fn(hsq, bank[4], ACT.Square).then_inc(sem.hsq, 1)
                if s == 3:
                    act.wait_ge(sem.hms, h + 1)
                    fn(hrms, hrms, ACT.Sqrt).then_inc(sem.hsd, 1)

            def fourier_a(n):
                for dt in range(2):
                    act.wait_ge(sem.dft_done, 3 * n + dt + 1)
                    a = halves(12)[:, dt, :]
                    copy(a[:, 0:S], bank[4 + dt][:, 0:S])
                    copy(a[:, S:2 * S], bank[4 + dt][:, S:2 * S], scale=-1.0).then_inc(sem.dft_out, 1)

            def fourier_y(n):
                act.wait_ge(sem.dft_done, 3 * n + 3)
                copy(halves(MF[n // 2])[:, n % 2, :], bank[6]).then_inc(sem.dft_out, 1)

            act.wait_ge(sem.tables2_landed, 48)
            copy(wg_hi, small[:]).then_inc(sem.wg_hi, 1)
            for s in range(4):
                ahead(0, s)
            kept("q")
            ahead(1, 0)
            act.wait_ge(sem.f_abs, 1)
            fn(f_abs, f_abs, ACT.Exp).then_inc(sem.f_exp, 1)
            act.wait_ge(sem.f_exp, 1)
            fn(f_abs, f_abs, ACT.Ln, bias=1.0).then_inc(sem.f_ln, 1)
            for s in range(1, 4):
                ahead(1, s)
            kept("k")
            for s in range(4):
                ahead(2, s)
            kept("v0")
            for h, g in enumerate((3, 4, 5)):
                for s in range(4):
                    ahead(g, s)
                    head(h, s)
                kept(ORDER2[g])
            ahead(6, 0)
            fourier_a(0)
            ahead(6, 1)
            fourier_y(0)
            head(3, 0)
            ahead(6, 2)
            ahead(6, 3)
            head(3, 2)
            kept("g0")
            ahead(7, 0)
            head(3, 3)
            ahead(7, 1)
            fourier_a(1)
            ahead(7, 2)
            fourier_y(1)
            fourier_a(2)
            ahead(7, 3)
            fourier_y(2)
            kept("g1")
            fourier_a(3)
            fourier_y(3)
            for k, pg in enumerate(MIXED2):
                act.wait_ge(*((sem.dft_out, 12) if k < 2 else (sem.y_gated, k - 1)))
                copy(hhi[:, 4 * k:4 * k + 4, :], tiles(pg)).then_inc(sem.mix_hi, 1)

        def dve_mix2(dve, at, st, tt, ts, stt, unit, modulation):
            V = nc.vector
            dve.wait_ge(sem.wg_hi, 1)
            tt(wg_lo, small[:], wg_hi.bitcast(F32), ALU.subtract).then_inc(*at.up(sem.wg_ready))
            V.memset(page(22)[:, 0:256], 0.0).then_inc(*at.up(sem.step))
            V.memset(page(21)[:, 512:768], 1.0).then_inc(*at.up(sem.step))
            V.memset(page(21)[:, 768:1024], 0.0).then_inc(*at.up(sem.step))
            unit()
            one, zero = page(21)[BOTH, 512:768], page(21)[FWD, 768:1024]
            dve.wait_ge(sem.gates, 1)
            tt(gate_in, bank[6][:, 0:32].rearrange("p (b c) -> p b c", c=16),
               col("bgates", 0, 16).unsqueeze(1).broadcast_to([P, 2, 16]), ALU.add).then_inc(*at.up(sem.step))
            dve.wait_ge(*at.last)
            ts(f_min, gate_in[:, :, 8:16], 0.0, None, ALU.min).then_inc(*at.up(sem.step))
            V.tensor_copy(gate_tok[:, 0].rearrange("p b (d x) -> p b d x", d=2)[:, :, :, 0:4],
                               gate_in[:, :, 0:8].rearrange("p b (d x) -> p b d x", d=2)).then_inc(*at.up(sem.step))
            dve.wait_ge(*at.last)
            stt(f_abs, f_min, 2.0, gate_in[:, :, 8:16], ALU.mult, ALU.subtract).then_inc(*at.up(sem.f_abs))
            dve.wait_ge(sem.f_ln, 1)
            tt(gate_tok[:, 1].rearrange("p b (d x) -> p b d x", d=2)[:, :, :, 0:4],
               f_min.rearrange("p b (d x) -> p b d x", d=2), f_abs.rearrange("p b (d x) -> p b d x", d=2),
               ALU.subtract).then_inc(*at.up(sem.gt_ready))
            unit()
            dve.wait_ge(sem.rows_made, 1)
            gi, gf = bank[4][:, 0:S], bank[4][:, S:2 * S]
            V.tensor_tensor_scan(row_b[BOTH], one, gf[BOTH], 0.0, ALU.mult, ALU.add).then_inc(*at.up(sem.step))
            dve.wait_ge(*at.last)
            tt(row_b[BWD], row_b[BWD], gf[BWD], ALU.subtract).then_inc(*at.up(sem.step))
            tt(row_c[FWD], gi[FWD], row_b[FWD], ALU.subtract).then_inc(*at.up(sem.step))
            dve.wait_ge(*at.last)
            tt(row_c[BWD], gi[BWD], row_b[BWD], ALU.add).then_inc(*at.up(sem.rows_out))
            dve.wait_ge(*at.last)
            V.tensor_tensor_scan(row_m[FWD], zero, row_c[FWD], -3e38, ALU.add, ALU.max).then_inc(*at.up(sem.step))
            V.tensor_copy(row_m[BWD], row_c[BWD]).then_inc(*at.up(sem.step))
            for k in range(8):
                n = 1 << k
                dve.wait_ge(*at.last)
                tt(row_m[BWD, 0:S - n], row_m[BWD, 0:S - n], row_m[BWD, n:S], ALU.max).then_inc(*at.up(sem.step))
            dve.wait_ge(*at.last)
            stt(row_s[FWD], row_b[FWD], -1.0, row_m[FWD], ALU.mult, ALU.subtract).then_inc(*at.up(sem.step))
            tt(row_s[BWD], row_b[BWD], row_m[BWD], ALU.subtract).then_inc(*at.up(sem.step))
            dve.wait_ge(*at.last)
            ts(row_m[BOTH], row_m[BOTH], -1.0, None, ALU.mult).then_inc(*at.up(sem.rows_out))
            dve.wait_ge(sem.ccol, 1)
            V.tensor_copy(ccol.rearrange("p b (d x) -> p b d x", d=2),
                               bank[5][:, 0:P].rearrange("p (b d x) -> p b d x", b=2, d=2)[:, :, :, 0:4]).then_inc(*at.up(sem.rows_out))
            unit()
            unit()

            def head(h, s):
                if s == 0:
                    dve.wait_ge(sem.head_made, h + 1)
                    m = bank[5]
                    tt(pf0[:, 0:P], m[:, 0:P], mask_f[:, 0:P], ALU.add).then_inc(*at.up(sem.step))
                    V.tensor_copy(pf0[:, P:S], m[:, P:S]).then_inc(*at.up(sem.step))
                    tt(pf1, m[:, P:S], mask_f[:, 0:P], ALU.add).then_inc(*at.up(sem.step))
                    tt(pb0, m[:, S:S + P], mask_b[:, P:S], ALU.add).then_inc(*at.up(sem.step))
                    tt(pb1, m[:, S:2 * S], mask_b, ALU.add).then_inc(*at.up(sem.masked))
                    dve.wait_ge(sem.p_exp, h + 1)
                    for n, (pp, jb, q, d) in enumerate(PARTS):
                        tt(pp, pp, bank[4][:, jb * S + q.start:jb * S + q.stop], ALU.mult).then_inc(*at.up(sem.p_made if n == 3 else sem.step))
                if s == 1:
                    dve.wait_ge(sem.den_made, h + 1)
                    dve.wait_ge(sem.floor_made, h + 1)
                    stt(inv, bank[5], -1.0, floor_, ALU.mult, ALU.max).then_inc(*at.up(sem.step))
                    dve.wait_ge(*at.last)
                    tt(inv, inv, bank[5], ALU.max).then_inc(*at.up(sem.step))
                    dve.wait_ge(*at.last)
                    V.reciprocal(inv, inv).then_inc(*at.up(sem.step))
                    dve.wait_ge(*at.last)
                    for n, (pp, jb, q, d) in enumerate(PARTS):
                        tt(pp, pp, inv[:, d * S + q.start:d * S + q.stop], ALU.mult).then_inc(*at.up(sem.step))
                    dve.wait_ge(*at.last)
                    tt(pf0[:, 0:P], pf0[:, 0:P], pb0, ALU.add).then_inc(*at.up(sem.step))
                    tt(pb1[:, P:S], pb1[:, P:S], pf1, ALU.add).then_inc(*at.up(sem.c_made))
                if s == 3:
                    dve.wait_ge(sem.hsum, h + 1)
                    ts(hrms, bank[5][:, 0:S], 1.0 / S, EPS, ALU.mult, ALU.add).then_inc(*at.up(sem.hms))
                    dve.wait_ge(sem.hsd, h + 1)
                    V.reciprocal(hrms, hrms).then_inc(*at.up(sem.step))
                    dve.wait_ge(*at.last)
                    for t in range(2):
                        stt(tiles(MY[h // 2])[:, 2 * (h % 2) + t, :], bank[4][:, t * S:(t + 1) * S],
                            col("mlstm_norm", 2 * h + t), hrms, ALU.mult, ALU.mult).then_inc(*at.up(sem.m_out if t else sem.step))

            for h in range(3):
                unit()
                head(h, 0)
                head(h, 1)
                unit()
                head(h, 3)
            unit()
            head(3, 0)
            head(3, 1)
            head(3, 3)
            unit()
            for n in range(2):
                dve.wait_ge(sem.kept, kept2(("g0", "g1")[n]))
                if n == 0:
                    dve.wait_ge(*at.last)
                tt(page(MY[n]), page(MY[n]), page(MG[n]), ALU.mult).then_inc(*at.up(sem.y_gated))
            for k, pg in enumerate(MIXED2):
                dve.wait_ge(sem.mix_hi, 4 + k + 1)
                tt(hlo[:, 4 * k:4 * k + 4, :], tiles(pg), hhi[:, 4 * k:4 * k + 4, :].bitcast(F32),
                   ALU.subtract).then_inc(*at.up(sem.mix_split))

        @block.sync
        def _(sp):
            st = {"unit": 0}

            def slab(n, per=0, i=0):
                if n >= RING:
                    by_dve, v = lo_signal(n - RING)
                    sp.wait_ge(sem.lo2_ready if by_dve else sem.lo_ready, v + lo_per(n - RING, per) * i)
                sp.dma_start(raw[:, n % RING, :],
                             wstream[bass.ds(n + per * i, 1), :, :].rearrange("a p n -> (a p) n")
                             ).then_inc(sem.w_landed[n % RING], 16)

            def ada(s, per=0, i=0):
                u = st["unit"]
                m = 2 * u + s + 2 * per * i
                sp.wait_ge((sem.ada_used, sem.acc_ready)[s], u + per * i)
                sp.dma_start(ada_raw[:, s, :], adastream[bass.ds(m, 1), :, :].rearrange("a p n -> (a p) n")
                             ).then_inc(sem.ada_landed[s], 16)
                st["unit"] += s

            MIX_TWO = {3: 0, 4: 1, 6: 0, 7: 1}

            def groups(n0, count, units, size=GS):
                per_turn = sum(units.values())

                def body(n, i=0, per=0):
                    for k in range(size):
                        if k in units:
                            ada(units[k], per_turn if per else 0, i)
                        slab(n + k, per, i)

                body(n0)
                if count > 1:
                    u0 = st["unit"]
                    with sp.Fori(0, count - 1) as i:
                        body(n0 + size, i, size)
                    st["unit"] = u0 + per_turn * (count - 1)

            def down(n0, units):
                for half in range(2):
                    n = n0 + half * DOWN_HALF
                    for k in range(4):
                        slab(n + k)
                    groups(n + 4, 5, {1: 0, 4: 1} if units else {})

            def start_unit(k, i=None):
                for s in range(2):
                    m = 2 * k + s
                    if i is not None:
                        sp.wait_ge((sem.ada_used, sem.ada_sum)[s], k + 1 + START_PAIRS * i)
                        m = m + 2 * START_PAIRS * (i + 1)
                    src = adastream[m:m + 1] if i is None else adastream[bass.ds(m, 1), :, :]
                    sp.dma_start(start_place(k, s), src.rearrange("a p n -> (a p) n")
                                 ).then_inc(sem.start_landed[2 * k + s], 16)

            sp.dma_start(cols[:], cols_in).then_inc(sem.cols_landed, 16)
            start_unit(0)
            sp.dma_start(tabs[:], tabs_in[:, 0:N_KEPT]).then_inc(sem.tabs_landed, 16)
            for k in range(1, START_PAIRS):
                start_unit(k)
            for k in range(4):
                sp.dma_start(xT[:, 4 * k:4 * k + 4, :], x_in[:, 4 * k:4 * k + 4, :]).then_inc(sem.x_landed, 16)
            with sp.Fori(0, START_UNITS // START_PAIRS - 1) as i:
                for k in range(START_PAIRS):
                    start_unit(k, i)
            st["unit"] = START_UNITS
            for n in range(RING):
                slab(n)
            sp.dma_start(conv[:], conv_in).then_inc(sem.conv_landed, 16)
            for dst, name in ((page(19), "retdecay"), (page(20)[:, 0:S], "alibi")):
                a, n = TABS[name]
                sp.dma_start(dst, tabs_in[:, a:a + n]).then_inc(sem.tables1_landed, 16)
            sp.dma_start(page(21), rw_in[:, 0, :]).then_inc(sem.tables1_landed, 16)
            sp.dma_start(page(22), rw_in[:, 1, :]).then_inc(sem.tables1_landed, 16)
            for n in range(RING, GS):
                slab(n)
            groups(GS, 4, MIX_TWO)
            groups(5 * GS, 4, {3: 0, 5: 1})
            groups(9 * GS, 4, MIX_TWO)
            groups(B1_OUT, 1, {3: 0, 5: 1})
            sp.wait_ge(sem.mix_split, 4)
            for k in range(4):
                sp.dma_start(xT[:, 4 * k:4 * k + 4, :], x_in[:, 4 * k:4 * k + 4, :]
                             ).then_inc(sem.x_landed, 16)
            groups(B1_OUT + GS, 3, {3: 0, 5: 1})
            groups(B1_UP, NFF, {3: 0, 6: 1, GS + 3: 0, GS + 6: 1}, 2 * GS)
            down(B1_DOWN, True)
            for n in range(RING):
                slab(B2 + n)
            sp.wait_ge(sem.slab_used, B2)
            a, n = TABS["dft"]
            sp.dma_start(page(19), tabs_in[:, a:a + n]).then_inc(sem.tables2_landed, 16)
            a = TABS["mfwd"][0]
            sp.dma_start(page(20)[:, 0:640], tabs_in[:, a:a + 640]).then_inc(sem.tables2_landed, 16)
            sp.dma_start(small[:], wg_in).then_inc(sem.tables2_landed, 16)
            for n in range(RING, GS):
                slab(B2 + n)
            groups(B2 + GS, 5, MIX_TWO)
            groups(B2 + 6 * GS, MIX2 - 6, {3: 0, 5: 1})
            groups(B2_OUT, 4, {3: 0, 5: 1})
            groups(B2_UP, 8, {2: 0, 5: 1}, 2 * GS)
            groups(B2_UP + 16 * GS, NFF - 8, {}, 2 * GS)
            down(B2_DOWN, False)
            for k in range(4):
                sp.wait_ge(sem.y_ready, k + 1)
                sp.dma_start(out[:, 4 * k:4 * k + 4, :], xT[:, 4 * k:4 * k + 4, :]
                             ).then_inc(sem.out_landed, 16)
            sp.wait_ge(sem.out_landed, 64)

        @block.gpsimd
        def _(pool):

            def stretch(n0, n1, step):
                with pool.Fori(0, (n1 - n0) // RING) as i:
                    for q in range(0, RING, step):
                        pool.wait_ge(sem.hi_ready, n0 + q + 1 + RING * i)
                        nc.gpsimd.tensor_tensor(wlo[:, q, :], raw[:, q, :], whi[:, q, :].bitcast(F32),
                                                     ALU.subtract).then_inc(sem.lo_ready, 1)

            for n0, n1, step in ((0, B1_UP, 1), (B1_UP, B2, 2), (B2, B2_UP, 1), (B2_UP, N_SLABS, 2)):
                stretch(n0, n1, step)

        @block.scalar
        def _(act):

            def copy(out_, in_, scale=1.0):
                return nc.scalar.activation(out_, in_, ACT.Copy, scale=scale)

            def fn(out_, in_, f, **kw):
                return nc.scalar.activation(out_, in_, f, **kw)

            def hi(n, per=0, i=0):
                if n >= N_SLABS:
                    return
                q = n % RING
                act.wait_ge(sem.w_landed[q], 16 * (n // RING + 1) + 16 * (per // RING) * i)
                if n >= RING:
                    act.wait_ge(sem.slab_used, n - RING + 1 + per * i)
                copy(whi[:, q, :], raw[:, q, :]).then_inc(sem.hi_ready, 1)


            next_hi = [0]

            def his(n0, n1):
                for n in range(max(n0, next_hi[0]), n1):
                    hi(n)
                next_hi[0] = max(n1, next_hi[0])

            def square(N, k):
                if N == 0:
                    act.wait_ge(sem.x_landed, 64)
                else:
                    act.wait_ge(sem.x_ready, 4 * (N - 1) + k + 1)
                if k >= 2:
                    act.wait_ge(sem.sq_used, 4 * N + k - 1)
                fn(page(13 + k % 2), page(15 + k), ACT.Square).then_inc(sem.sq_ready, 1)

            def square2(k):
                act.wait_ge(sem.x_ready, 4 + k + 1)
                if k >= 2:
                    act.wait_ge(sem.sq_used, 8 + 2 * (k - 1))
                fn(page(13 + k % 2), page(15 + k), ACT.Square).then_inc(sem.sq_ready, 1)
                for j in range(4):
                    ins = fn(tiles(11 + k % 2)[:, j, :], xT[:, 4 * k + j, :], ACT.Square,
                             scale=col("norm_final", 4 * k + j))
                    if j == 3:
                        ins.then_inc(sem.sq_ready, 1)

            def norm(N, hN=None, squared=0, n0=0):
                for k in range(squared, 4):
                    square(N, k)
                act.wait_ge(sem.ms_ready, N + 1)
                fn(rstd[:], rstd[:], ACT.Sqrt).then_inc(sem.sd_ready, 1)
                if N == 2:
                    act.wait_ge(sem.ms_ready, 4)
                    fn(rstd2, rstd2, ACT.Sqrt).then_inc(sem.sd_ready, 1)
                if hN is not None:
                    for k in range(4):
                        act.wait_ge(sem.u_ready, 4 * hN + k + 1)
                        copy(hhi[:, 4 * k:4 * k + 4, :], tiles(13 + k % 2)).then_inc(sem.h_hi, 1)
                        if k:
                            his(n0 + 2 + k, n0 + 3 + k)

            def output(n0, N, hN):
                for g in range(4):
                    his(n0 + g * GS + 3, n0 + (g + 1) * GS + 3)
                    if g > 0:
                        square(N, g - 1)
                norm(N, hN, 3, n0 + 4 * GS)

            def gs_hi(n0, b, kk):
                kc = kk % NFF
                act.wait_ge(sem.g_made, NFF * b + (kk % NFF + 1 if kk < NFF else NFF))
                if kk >= 2:
                    act.wait_ge(sem.slab_used, n0 + 4 * (kk - 1))
                copy(gshi[:, kk % 2, :, :], gT[:, 4 * kc:4 * kc + 4, :]).then_inc(sem.gs_hi, 1)

            def ffn(n0, b):
                gb = NFF * b
                more = 2 * GS

                def turn(t, i=None):
                    n1 = n0 + more * t
                    step = 0 if i is None else i
                    for half in range(2):
                        a, z = n1 + half * GS + 3 + (half == 0), n1 + half * GS + 3 + GS
                        if i is None:
                            his(a, z)
                        else:
                            for n in range(a, z):
                                hi(n, more, i)
                        if t == NFF - 1 and half == 1:
                            for kk in range(2):
                                gs_hi(n0 + more * NFF, b, kk)
                        act.wait_ge(sem.slab_used, n1 + (half + 1) * GS + more * step)
                        if half == 0:
                            act.wait_ge(sem.cw_ready, gb + 1 + t + step)
                        u = pair(1 - half)
                        for j in range(4):
                            c = 16 * half + 4 * j
                            ins = fn(tiles(11 + half)[:, j, :], u[:, j, :], ACT.Identity,
                                     scale=cw[:, c:c + 1], bias=cw[:, c + 3:c + 4])
                            if j == 3:
                                ins.then_inc(sem.gate_tap if half else sem.val_tap, 1)
                    if i is None:
                        his(n1 + more + 3, n1 + more + 4)
                    else:
                        hi(n1 + more + 3, more, i)
                    act.wait_ge(sem.free_gate, gb + 1 + t + step)
                    fn(page(12), page(12), ACT.Silu).then_inc(sem.gate_act, 1)

                turn(0)
                with act.Fori(0, NFF - 2) as i:
                    turn(1, i)
                next_hi[0] = n0 + more * (NFF - 1) + 4
                turn(NFF - 1)

            def down(n0, b, more):
                def gs(kk):
                    gs_hi(n0, b, kk)

                for half in range(2):
                    kk0 = NFF * half
                    if half == 1:
                        gs(kk0 + 1)
                    his(n0 + 4 * kk0 + 3, n0 + 4 * kk0 + 7)
                    with act.Fori(0, 4) as i:
                        for s in range(2):
                            kk = kk0 + 2 + s
                            act.wait_ge(sem.slab_used, n0 + 4 * (kk - 1) + 8 * i)
                            if half == 0:
                                act.wait_ge(sem.g_made, NFF * b + kk + 1 + 2 * i)
                            copy(gshi[:, kk % 2, :, :], gT[:, bass.ds(4 * (kk % NFF) + 8 * i, 4), :]).then_inc(sem.gs_hi, 1)
                            for c in range(4):
                                hi(n0 + 4 * (kk - 1) + 3 + c, 8, i)
                    if half == 1:
                        for k in range(2):
                            if b == 0:
                                square2(k)
                            else:
                                square(5, k)
                    for kk in (kk0 + 9, kk0 + 10):
                        if kk + 1 < 2 * NFF:
                            gs(kk + 1)
                        his(n0 + 4 * kk + 3, n0 + 4 * kk + 7)

            act.wait_ge(sem.cols_landed, 16)
            fn(cact[:], col("c", 0, 32), ACT.Silu).then_inc(sem.cact_ready, 1)
            for k in range(4):
                square(0, k)
            his(0, 3)
            norm(0, 0, 4)
            act_mix1(act, copy, fn, his)
            output(B1_OUT, 1, 1)
            ffn(B1_UP, 0)
            down(B1_DOWN, 0, True)
            for k in (2, 3):
                square2(k)
            norm(2, 2, 4, B2)
            act_mix2(act, copy, fn, his)
            output(B2_OUT, 4, 3)
            ffn(B2_UP, 1)
            down(B2_DOWN, 1, False)
            norm(5, None, 2)

        @block.tensor
        def _(pe):
            st = {"free": {0: None, 1: None}, "finished": 0}

            def mm(o, lhsT, rhs, start, stop=True):
                return nc.tensor.matmul(o, lhsT, rhs, start=start, stop=stop, skip_group_check=True)

            def product(o, lh, ll, rh, rl, start, stop):
                mm(o, lh, rh, start, False)
                mm(o, ll, rh, False, False)
                return mm(o, lh, rl, False, stop)

            def ready(n, per=0, i=0):
                by_dve, v = lo_signal(n)
                pe.wait_ge(sem.lo2_ready if by_dve else sem.lo_ready, v + lo_per(n, per) * i)

            def slab(n, p, rh, rl, first, last, per=0, i=0, kks=(0, 1)):
                ready(n, per, i)
                q = n % RING
                for kk in kks:
                    for j in range(4):
                        w = slice(kk * 512 + j * P, kk * 512 + (j + 1) * P)
                        ins = product(pair(p)[:, j, :], whi[:, q, w], wlo[:, q, w], rh[:, kk, :], rl[:, kk, :],
                                      first and kk == 0 and j % 2 == 0, last and kk == 1)
                        if kk == 1 and j == 3:
                            ins.then_inc(sem.slab_used, 1)

            def slab_tok(n, p, k, first, last, kks=(0, 1)):
                ready(n)
                q = n % RING
                for kk in kks:
                    w = slice(kk * 512, (kk + 1) * 512)
                    for tb in range(2):
                        t = slice(tb * P, (tb + 1) * P)
                        o = bank[2 * p + tb]
                        mm(o, hhi[:, 2 * k + kk, t], whi[:, q, w], first and kk == 0, False)
                        mm(o, hlo[:, 2 * k + kk, t], whi[:, q, w], False, False)
                        ins = mm(o, hhi[:, 2 * k + kk, t], wlo[:, q, w], False, last and kk == 1)
                        if kk == 1 and tb == 1:
                            ins.then_inc(sem.slab_used, 1)

            def finish(b=0, per=0, i=0):
                pe.wait_ge(sem.acc_ready, st["finished"] + 1 + per * i)
                st["finished"] += 1
                for j in range(2):
                    ins = mm(bank[7][:, j:j + 1], acc[:, b, 0, j * P:(j + 1) * P], ones[:, 0:1], j == 0)
                    if j:
                        ins.then_inc(sem.ada_sum, 1)

            def part(n0, p, k0, k1, form=None, h_at=None, kks=(0, 1)):
                if k0 == 0 and kks[0] == 0 and st["free"][p]:
                    pe.wait_ge(*st["free"][p])
                for k in range(k0, k1):
                    if h_at and k % 2 == 0:
                        pe.wait_ge(h_at[0], h_at[1] + k // 2 + 1)
                    if form == "tok":
                        slab_tok(n0 + k, p, k, k == 0, k == GS - 1, kks)
                    else:
                        slab(n0 + k, p, hhi[:, 2 * k:2 * k + 2, :], hlo[:, 2 * k:2 * k + 2, :],
                             k == 0, k == GS - 1, kks=kks)

            def sums(N, k):
                pe.wait_ge(sem.sq_ready, 4 * N + k + 1)
                for j in range(4):
                    ins = mm(bank[6][:, 0:S], ones, tiles(13 + k % 2)[:, j, :], k == 0 and j == 0,
                       k == 3 and j == 3)
                    if j == 3:
                        ins.then_inc(sem.sq_used, 1)

            def sums2(k):
                for n in range(2):
                    pe.wait_ge(sem.sq_ready, 8 + 2 * k + n + 1)
                    for j in range(4):
                        ins = mm(bank[6][:, n * S:(n + 1) * S], ones, tiles((13, 11)[n] + k % 2)[:, j, :],
                                 k == 0 and j == 0 and n == 0, k == 3 and j == 3)
                        if j == 3:
                            ins.then_inc(sem.sq_used, 1)

            def output(n0, g0, N, x0, h_at, units):
                for g in range(4):
                    p = (g0 + g) % 2
                    part(n0 + g * GS, p, 0, 4, h_at=h_at if g == 0 else None)
                    if g >= 2:
                        sums(N, g - 2)
                    part(n0 + g * GS, p, 4, GS, h_at=h_at if g == 0 else None)
                    st["free"][p] = (sem.x_ready, x0 + g + 1)
                    if units:
                        finish()
                sums(N, 2)
                sums(N, 3)

            def up(n0, b, h0, segments):
                done = 0
                gb = NFF * b

                def body(t, i, per, units):
                    for half in range(2):
                        p = 1 - half
                        free = (sem.free_val, sem.free_gate)[half]
                        if i is None and t == 0:
                            pe.wait_ge(*st["free"][p])
                        else:
                            pe.wait_ge(free, gb + t + (0 if i is None else i))
                        for k in range(GS):
                            if i is None and t == 0 and half == 0 and k % 2 == 0:
                                pe.wait_ge(sem.h_ready, h0 + k // 2 + 1)
                            slab(n0 + 2 * GS * t + half * GS + k, p, hhi[:, 2 * k:2 * k + 2, :],
                                 hlo[:, 2 * k:2 * k + 2, :], k == 0, k == GS - 1, 2 * GS * per, 0 if i is None else i)
                        if half < units:
                            finish(0, units * per, 0 if i is None else i)

                for turns, units in segments:
                    if done == 0:
                        body(0, None, 0, units)
                        done, turns = 1, turns - 1
                    before = st["finished"]
                    with pe.Fori(0, turns) as i:
                        body(done, i, 1, units)
                    st["finished"] = before + units * turns
                    done += turns

            def down(n0, b, N, x0, units):
                def sums_of(k):
                    if b == 0:
                        sums2(k)
                    else:
                        sums(N, k)

                for half in range(2):
                    pa, pb = ((1, 0), (2, 1))[half]
                    kk0 = NFF * half

                    def chunk(kk, per=0, i=0, first=False, last=False):
                        pe.wait_ge(sem.gs_lo, 2 * NFF * b + kk + 1 + (per // 4) * i)
                        for g, p in enumerate((pa, pb)):
                            if first and half == 0:
                                pe.wait_ge((sem.free_gate, sem.free_val)[p], NFF * (b + 1))
                            if first and half == 1 and p == 1:
                                pe.wait_ge(sem.x_ready, x0 + 1)
                            for k in range(2):
                                slab(n0 + 4 * kk + 2 * g + k, p, gshi[:, kk % 2, 2 * k:2 * k + 2, :],
                                     gslo[:, kk % 2, 2 * k:2 * k + 2, :], first and k == 0, last and k == 1,
                                     per, i)

                    chunk(kk0, first=True)
                    before = st["finished"]
                    with pe.Fori(0, 4) as i:
                        for s in range(2):
                            chunk(kk0 + 1 + s, 8, i)
                        if units:
                            finish(0, 1, i)
                    if units:
                        st["finished"] = before + 4
                    chunk(kk0 + 9)
                    if half == 1:
                        for k in range(2):
                            sums_of(k)
                    chunk(kk0 + 10, last=True)
                    if units:
                        finish()
                    if half == 1:
                        for k in range(2, 4):
                            sums_of(k)

            pe.wait_ge(sem.tabs_landed, 16)
            def start_unit(k, i=None):
                pe.wait_ge(sem.acc_ready, k + 1 if i is None else k + 1 + START_PAIRS * (i + 1))
                for j in range(2):
                    for kt in range(START_DVE, KT):
                        at_ = (kt - 8) * 256 + j * P
                        mm(bank[7][:, j:j + 1], start_place(k, 1)[:, at_:at_ + P], cact[:, kt:kt + 1],
                           j == 0 and kt == START_DVE, False)
                    ins = mm(bank[7][:, j:j + 1], acc[:, k % 2, 0, j * P:(j + 1) * P], ones[:, 0:1], False, True)
                    if j:
                        ins.then_inc(sem.ada_sum, 1)

            for k in range(START_PAIRS):
                start_unit(k)
            for k in range(4):
                sums(0, k)
            with pe.Fori(0, START_UNITS // START_PAIRS - 1) as i:
                for k in range(START_PAIRS):
                    start_unit(k, i)
            st["finished"] = START_UNITS
            pe_mix1(pe, st, mm, part, finish)
            output(B1_OUT, MIX1, 1, 0, (sem.mix_split, 0), True)
            up(B1_UP, 0, 4, [(NFF, 2)])
            down(B1_DOWN, 0, 2, 4, True)
            st["free"] = {0: (sem.x_ready, 8), 1: (sem.x_ready, 8)}
            pe_mix2(pe, st, mm, part, finish)
            output(B2_OUT, MIX2, 4, 12, (sem.mix_split, 4), True)
            up(B2_UP, 1, 12, [(8, 1), (3, 0)])
            down(B2_DOWN, 1, 5, 16, False)

        @block.vector
        def _(dve):
            at = Count()
            V = nc.vector
            st = {"unit": 0}

            def tt(o, a, b, op_):
                return V.tensor_tensor(o, a, b, op_)

            def ts(o, a, s1, s2, op0, op1=ALU.bypass):
                if s2 is None:
                    return V.tensor_scalar(o, a, s1, None, op0)
                return V.tensor_scalar(o, a, s1, s2, op0, op1)

            def stt(o, a, s, b, op0, op1):
                return V.scalar_tensor_tensor(out=o, in0=a, scalar=s, in1=b, op0=op0, op1=op1)

            def modulation(u, static=True, per=0, i=0):
                dve.wait_ge(sem.ada_sum, u + 1 + per * i)
                s = bass.ds(2 * u + 2 * per * i, 2) if per else slice(2 * u, 2 * u + 2)
                b = bass.ds(COLS["bada"] + 2 * u + 2 * per * i, 2) if per else \
                    slice(COLS["bada"] + 2 * u, COLS["bada"] + 2 * u + 2)
                tt(modc[:, s], bank[7][:, 0:2], cols[:, b], ALU.add).then_inc(*at.up(sem.step))

            def products(kts, src, base, buf, c0, used_at=None):
                marks = st["marks"]
                for kt in kts:
                    w = src[:, (kt - base) * 256:(kt - base + 1) * 256]
                    o = acc[:, buf, kt % 2, :]
                    c = cact[:, c0 + kt:c0 + kt + 1]
                    signal = sem.ada_used if kt == used_at else sem.step
                    if kt < 2:
                        ts(o, w, c, None, ALU.mult).then_inc(*at.up(signal))
                    else:
                        dve.wait_ge(*marks[kt % 2])
                        stt(o, w, c, o, ALU.mult, ALU.add).then_inc(*at.up(signal))
                    marks[kt % 2] = at.last

            def merge(buf):
                dve.wait_ge(*at.last)
                tt(acc[:, buf, 0, :], acc[:, buf, 0, :], acc[:, buf, 1, :], ALU.add).then_inc(*at.up(sem.acc_ready))

            def chunk(s, buf, u, per=0, i=0):
                dve.wait_ge(sem.ada_landed[s], 16 * (u - START_UNITS + 1) + 16 * per * i)
                products(range(8 * s, 8 * s + 8), ada_raw[:, s, :], 8 * s, buf, 16 if u >= 48 else 0,
                         7)
                if s == 1:
                    merge(buf)

            def unit(buf=0):
                u = st["unit"]
                st["unit"] += 1
                st["marks"] = {}
                modulation(u - 1)
                chunk(0, buf, u)
                chunk(1, buf, u)

            def unit_pieces():
                u = st["unit"]
                st["unit"] += 1
                st["marks"] = {}
                modulation(u - 1)
                for n, kts in enumerate((range(4), range(4, 8), range(8, 11), range(11, 14), range(14, 16))):
                    if n in (0, 2):
                        dve.wait_ge(sem.ada_landed[n // 2], 16 * (u - START_UNITS + 1))
                    products(kts, ada_raw[:, n // 2 if n < 3 else 1, :], 0 if n < 2 else 8, 0, 16 if u >= 48 else 0, 7)
                    if n == 4:
                        merge(0)
                    yield

            def start_unit(k, i=None):
                st["marks"] = {}
                turn = 16 if i is None else 16 + 16 * (i + 1)
                dve.wait_ge(sem.start_landed[2 * k], turn)
                products(range(8), start_place(k, 0), 0, k % 2, 0, 7)
                dve.wait_ge(sem.start_landed[2 * k + 1], turn)
                products(range(8, START_DVE), start_place(k, 1), 8, k % 2, 0)
                if i is not None:
                    modulation(START_PAIRS + k - 1, per=START_PAIRS, i=i)
                elif k:
                    modulation(k - 1)
                merge(k % 2)

            def norm(N):
                dve.wait_ge(sem.sq_used, 4 * (N + 1))
                ts(rstd[:], bank[6][:, 0:S], 1.0 / D, EPS, ALU.mult, ALU.add).then_inc(*at.up(sem.ms_ready))
                dve.wait_ge(sem.sd_ready, N + 1)
                V.reciprocal(rstd[:], rstd[:]).then_inc(*at.up(sem.step))
                dve.wait_ge(*at.last)

            def norm2():
                dve.wait_ge(sem.sq_used, 16)
                ts(rstd[:], bank[6][:, 0:S], 1.0 / D, EPS, ALU.mult, ALU.add).then_inc(*at.up(sem.ms_ready))
                dve.wait_ge(sem.sd_ready, 3)
                V.reciprocal(rstd[:], rstd[:]).then_inc(*at.up(sem.step))
                dve.wait_ge(*at.last)
                tt(rstd2, rstd[:], rstd[:], ALU.mult).then_inc(*at.up(sem.step))
                dve.wait_ge(*at.last)
                tt(rstd2, rstd2, bank[6][:, S:2 * S], ALU.mult).then_inc(*at.up(sem.step))
                dve.wait_ge(*at.last)
                ts(rstd2, rstd2, 1.0 / D, EPS, ALU.mult, ALU.add).then_inc(*at.up(sem.ms_ready))
                dve.wait_ge(sem.sd_ready, 4)
                V.reciprocal(rstd2, rstd2).then_inc(*at.up(sem.step))
                dve.wait_ge(*at.last)
                tt(rstd2, rstd2, rstd[:], ALU.mult).then_inc(*at.up(sem.step))

            def rstd4(r=None):
                return (rstd[:] if r is None else r).unsqueeze(1).broadcast_to([P, 4, S])

            def modulated(N, hN, gain, u0, up_at=None):
                shift, scale = u0, u0 + 16
                stt(colA[:], modc[:, scale:scale + 16], 1.0, col(gain, 0, 16), ALU.add, ALU.mult).then_inc(*at.up(sem.step))
                if N == 2:
                    dve.wait_ge(*at.last)
                    tt(colA[:], colA[:], col("norm_final", 0, 16), ALU.mult).then_inc(*at.up(sem.step))
                    norm2()
                else:
                    norm(N)
                dve.wait_ge(*at.last)
                split = []
                for k in range(4):
                    u = tiles(13 + k % 2)
                    if k >= 2:
                        dve.wait_ge(*split[k - 2])
                    tt(u, xT[:, 4 * k:4 * k + 4, :], rstd4(rstd2 if N == 2 else None), ALU.mult).then_inc(*at.up(sem.step))
                    dve.wait_ge(*at.last)
                    for j in range(4):
                        c = 4 * k + j
                        ts(u[:, j, :], u[:, j, :], colA[:, c:c + 1], modc[:, shift + c:shift + c + 1],
                           ALU.mult, ALU.add).then_inc(*at.up(sem.u_ready if j == 3 else sem.step))
                    dve.wait_ge(sem.h_hi, 4 * hN + k + 1)
                    h = hhi[:, 4 * k:4 * k + 4, :]
                    tt(hlo[:, 4 * k:4 * k + 4, :], u, h.bitcast(F32), ALU.subtract).then_inc(*at.up(sem.h_ready))
                    split.append(at.last)
                    if up_at and k >= 1:
                        los(up_at + 2 + k, up_at + 3 + k)

            def scaled(gain, signal):
                for k in range(4):
                    xk = xT[:, 4 * k:4 * k + 4, :]
                    tt(xk, xk, rstd4(), ALU.mult).then_inc(*at.up(sem.step))
                    dve.wait_ge(*at.last)
                    for j in range(4):
                        c = 4 * k + j
                        ts(xT[:, c, :], xT[:, c, :], col(gain, c), None, ALU.mult).then_inc(*at.up(signal if j == 3 else sem.step))

            def residual(n_used, p, k, gate, signal=sem.x_ready):
                dve.wait_ge(sem.slab_used, n_used)
                for j in range(4):
                    c = 4 * k + j
                    stt(xT[:, c, :], pair(p)[:, j, :], modc[:, gate + c:gate + c + 1], xT[:, c, :],
                        ALU.mult, ALU.add).then_inc(*at.up(signal if j == 3 else sem.step))

            def lo2(n, per=0, i=0):
                if n % 2 == 0 or n in split_ahead:
                    return
                q = n % RING
                dve.wait_ge(sem.hi_ready, n + 1 + per * i)
                tt(wlo[:, q, :], raw[:, q, :], whi[:, q, :].bitcast(F32), ALU.subtract).then_inc(*at.up(sem.lo2_ready))

            split_ahead = []

            def los(n0, n1):
                for n in range(n0, n1):
                    if n < N_SLABS:
                        lo2(n)
                        split_ahead.append(n)

            def gs_lo(b, kk, per=0, i=0):
                kc = kk % NFF
                dve.wait_ge(sem.gs_hi, 2 * NFF * b + kk + 1 + per * i)
                src = gT[:, 4 * kc:4 * kc + 4, :] if not per else gT[:, bass.ds(4 * kc + 8 * i, 4), :]
                tt(gslo[:, kk % 2, :, :], src, gshi[:, kk % 2, :, :].bitcast(F32), ALU.subtract).then_inc(*at.up(sem.gs_lo))

            def ffn(n0, b, segments):
                done = 0
                for turns, units, own in segments:
                    u0 = st["unit"]
                    first, last = done == 0, done == NFF - 1
                    with at.loop(dve, turns, {sem.lo2_ready: GS - first, sem.gs_lo: 2 * last, sem.cw_ready: 1, sem.free_val: 1, sem.free_gate: 1,
                                                sem.g_made: 1, sem.acc_ready: units, sem.ada_used: units,
                                                sem.step: own}) as i:
                        n1 = n0 + 2 * GS * done
                        for half in range(2):
                            if half == 0:
                                V.tensor_copy(cw[:].rearrange("p (a c) -> p a c", a=1),
                                                   conv[:, b, bass.ds(done + i, 1), :]).then_inc(*at.up(sem.cw_ready))
                            has = half < units
                            uu = u0 + half
                            lo_at = n1 + half * GS + 3
                            if half == 1:
                                lo2(lo_at, 2 * GS, i)
                            lo2(lo_at + 1, 2 * GS, i)
                            if has:
                                st["marks"] = {}
                                modulation(uu - 1, per=units, i=i)
                                chunk(0, 0, uu, units, i)
                            for k in range(2, 5):
                                lo2(lo_at + k, 2 * GS, i)
                            if has:
                                chunk(1, 0, uu, units, i)
                            for k in range(5, GS):
                                lo2(lo_at + k, 2 * GS, i)
                            if last and half == 1:
                                for kk in range(2):
                                    gs_lo(b, kk)
                            dve.wait_ge((sem.val_tap, sem.gate_tap)[half], NFF * b + done + 1 + i)
                            u, t = pair(1 - half), tiles(11 + half)
                            marks = []
                            for j in range(4):
                                c = 16 * half + 4 * j
                                stt(t[:, j, 1:S], u[:, j, 0:S - 1], cw[:, c + 1:c + 2],
                                                 t[:, j, 1:S], ALU.mult, ALU.add).then_inc(*at.up(sem.step))
                                marks.append(at.last)
                            for j in range(4):
                                c = 16 * half + 4 * j
                                dve.wait_ge(*marks[j])
                                o, f = (slice(2, S), slice(0, S - 2)) if b == 0 else (slice(0, S - 1), slice(1, S))
                                stt(t[:, j, o], u[:, j, f], cw[:, c + 2:c + 3], t[:, j, o], ALU.mult, ALU.add).then_inc(*at.up((sem.free_val, sem.free_gate)[half] if j == 3 else sem.step))
                        lo2(n1 + 2 * GS + 3, 2 * GS, i)
                        dve.wait_ge(sem.gate_act, NFF * b + done + 1 + i)
                        tt(gT[:, bass.ds(4 * (done + i), 4), :], tiles(11), tiles(12), ALU.mult).then_inc(*at.up(sem.g_made))
                        dve.wait_ge(*at.last)
                    st["unit"] = u0 + units * turns
                    done += turns
                split_ahead.append(n0 + 2 * GS * NFF + 3)

            def down(n0, b, gate, x0, units, own):
                def gs(kk, per=0, i=0):
                    gs_lo(b, kk, per, i)

                for half in range(2):
                    kk0 = NFF * half
                    if half == 1:
                        residual(n0 + 4 * NFF, 1, 0, gate)
                    if half == 1:
                        gs(kk0 + 1)
                    los(n0 + 4 * kk0 + 3, n0 + 4 * kk0 + 7)
                    if half == 1:
                        residual(n0 + 4 * NFF, 0, 1, gate)
                    u0 = st["unit"]
                    with at.loop(dve, 4, {sem.gs_lo: 2, sem.lo2_ready: 4, sem.acc_ready: units, sem.ada_used: units,
                                              sem.step: own}) as i:
                        n1 = n0 + 4 * kk0
                        gs(kk0 + 2, 2, i)
                        for c in range(4):
                            lo2(n1 + 4 + 3 + c, 8, i)
                        if units:
                            st["marks"] = {}
                            modulation(u0 - 1, per=1, i=i)
                            chunk(0, 0, u0, 1, i)
                        gs(kk0 + 3, 2, i)
                        for c in range(2):
                            lo2(n1 + 8 + 3 + c, 8, i)
                        if units:
                            chunk(1, 0, u0, 1, i)
                        for c in range(2, 4):
                            lo2(n1 + 8 + 3 + c, 8, i)
                    st["unit"] = u0 + 4 * units
                    gs(kk0 + 10)
                    los(n0 + 4 * (kk0 + 9) + 3, n0 + 4 * (kk0 + 9) + 7)
                    if units:
                        unit()
                    if half == 0:
                        gs(kk0 + 11)
                    los2 = min(n0 + 4 * (kk0 + 10) + 7, n0 + 8 * NFF)
                    los(n0 + 4 * (kk0 + 10) + 3, los2)
                for k, p in enumerate((2, 1)):
                    residual(n0 + 8 * NFF, p, 2 + k, gate)


            dve.wait_ge(sem.cact_ready, 1)
            dve.wait_ge(sem.cols_landed, 16)
            for k in range(START_PAIRS):
                start_unit(k)
            with at.loop(dve, START_UNITS // START_PAIRS - 1,
                         {sem.acc_ready: START_PAIRS, sem.ada_used: START_PAIRS, sem.step: 12 * START_PAIRS}) as i:
                for k in range(START_PAIRS):
                    start_unit(k, i)
            st["unit"] = START_UNITS
            modulation(START_UNITS - 1)
            dve.wait_ge(*at.last)
            modulated(0, 0, "norm_mix", 0)
            dve_mix1(dve, at, st, tt, ts, stt, unit, unit_pieces)
            for g in range(4):
                unit()
                if g == 0:
                    dve.wait_ge(sem.x_landed, 128)
                residual(B1_OUT + (g + 1) * GS, (MIX1 + g) % 2, g, 32)
            los(B1_UP, B1_UP + 3)
            modulation(st["unit"] - 1)
            dve.wait_ge(*at.last)
            modulated(1, 1, "norm_ffn", 48, B1_UP)
            ffn(B1_UP, 0, [(1, 2, 46), (3, 2, 46), (NFF - 5, 2, 46), (1, 2, 46)])
            down(B1_DOWN, 0, 80, 4, 1, 16)
            dve.wait_ge(*at.last)
            modulated(2, 2, "norm1", 96)
            dve.wait_ge(*at.last)
            scaled("norm_final", sem.x_ready)
            dve_mix2(dve, at, st, tt, ts, stt, unit, modulation)
            for g in range(4):
                unit()
                residual(B2_OUT + (g + 1) * GS, (MIX2 + g) % 2, g, 96 + 32)
            los(B2_UP, B2_UP + 3)
            modulation(st["unit"] - 1)
            dve.wait_ge(*at.last)
            modulated(4, 3, "norm2", 96 + 48, B2_UP)
            ffn(B2_UP, 1, [(1, 1, 30), (7, 1, 30), (NFF - 9, 0, 14), (1, 0, 14)])
            modulation(st["unit"] - 1)
            dve.wait_ge(*at.last)
            down(B2_DOWN, 1, 96 + 80, 16, 0, 0)
            dve.wait_ge(*at.last)
            norm(5)
            scaled("norm_f", sem.y_ready)


def _slabs(w):
    k, n = w.shape
    return w.reshape(k // 256, 2, P, n // 512, 512).transpose(3, 0, 2, 1, 4).reshape(-1, P, SLAB)


def _down_slabs(w):
    return w.reshape(NFF, 2, 2, P, 2, 2, 512).transpose(4, 0, 5, 1, 3, 2, 6).reshape(-1, P, SLAB)


def _value_first(a):
    return np.concatenate([a[..., DFF:], a[..., :DFF]], -1)


def _up_slabs(w):
    v, g = _slabs(w[:, :DFF]), _slabs(w[:, DFF:])
    return np.concatenate([v.reshape(NFF, GS, P, SLAB), g.reshape(NFF, GS, P, SLAB)], 1).reshape(-1, P, SLAB)


def _ada(w):
    return w.reshape(2, 8, P, 48, 256).transpose(3, 0, 2, 1, 4).reshape(-1, P, 2048)


def _columns(v):
    return np.asarray(v).reshape(-1, P).T


def _padded_lora(w, axis):
    a = np.moveaxis(np.asarray(w), axis, 0)
    z = np.zeros((32,) + a.shape[1:], a.dtype)
    return np.moveaxis(np.concatenate([a[:96], z, a[96:192], z, a[192:]]), 0, axis)


def lay_out(inp):
    g = {k: np.asarray(v) for k, v in inp.items()}
    w = g["w_in"][0]
    ret, rw, mo = w[:, :1536], w[:, 1536:3520], w[:, 3520:]
    lora = _padded_lora(rw[:, 1536:], 1)
    w1 = np.concatenate([rw[:, :1536], lora, ret] + [mo[:, 1024 * c + 512 * h:1024 * c + 512 * h + 512]
                                                     for h in range(2) for c in range(3)], 1)
    w2 = g["w_in_2"]
    in2 = np.concatenate([w2[:, a:a + 512] for a in (1024, 1536, 2048, 0, 2560, 512, 3072, 3584)], 1)
    gate_order = [4 * k + h for k in (0, 2, 1, 3) for h in range(4)]
    wstream = np.concatenate([
        _slabs(w1), _slabs(g["w_out"][0]), _up_slabs(g["w_ffn_up"][0]), _down_slabs(g["w_ffn_down"][0]),
        _slabs(in2), _slabs(g["w_out_2"]), _up_slabs(_value_first(g["w_up_2"])), _down_slabs(g["w_down_2"])])
    assert wstream.shape[0] == N_SLABS
    ada = np.concatenate([_ada(g["w_ada"][0]), _ada(g["w_ada_2"])])
    mu = g["rwkv_mu"][0]
    mu = np.concatenate([mu[:1536], _padded_lora(mu[1536:], 0)])
    cols = np.concatenate([_columns(v) for v in (
        g["c"], g["c_2"], g["b_ada"], g["b_ada_2"], g["norm_mix"], g["norm_ffn"], g["norm_final"], g["norm1_w_2"],
        g["norm2_w_2"], g["norm_f_w_2"], mu, g["rwkv_w0"], g["rwkv_a0"], g["rwkv_k_k"], g["rwkv_k_a"],
        g["rwkv_r_k"], g["rwkv_ln_w"], g["rwkv_ln_b"], g["mlstm_norm_w_2"])]
        + [np.broadcast_to(g["b_gates_2"][None, gate_order], (P, 16))], 1)

    def conv(cw, cb, order):
        rows = np.stack([cw[order[0]], cw[order[1]], cw[order[2]], cb])
        return rows.reshape(4, 2, NFF, 4, P).transpose(4, 2, 1, 3, 0).reshape(P, NFF, 32)

    convs = np.stack([conv(g["ffn_conv_w"][0], g["ffn_conv_b"][0], (2, 1, 0)),
                      conv(_value_first(g["w_conv_2"]), _value_first(g["b_conv_2"]), (1, 0, 2))], 1)
    z = np.zeros((32, 512), np.float32)
    gup = g["rwkv_g_up"][0]
    rw_up = np.stack([np.concatenate([np.concatenate([g["rwkv_w_up"][0], z]), np.concatenate([g["rwkv_a_up"][0], z])], 1),
                      np.concatenate([gup[:P], gup[P:]], 1)], 1)
    wg = w2[:, 4096:][:, gate_order].reshape(KT, P, 16).transpose(1, 0, 2).reshape(P, 256)
    x = g["x"][0].T.reshape(KT, P, S).transpose(1, 0, 2)
    arrays = {"wstream": wstream, "adastream": ada, "x_in": x, "cols_in": cols, "conv_in": convs,
              "tabs_in": tables(), "rw_in": rw_up, "wg_in": wg}
    return {k: np.ascontiguousarray(v, dtype=np.float32) for k, v in arrays.items()}


def kernel(**inputs):
    import concourse.bacc as bacc
    from concourse.bass_utils import run_bass_kernel_spmd

    nc = bacc.Bacc("TRN2", target_bir_lowering=False, num_devices=1)
    arrays = lay_out(inputs)
    args = [nc.dram_tensor(k, v.shape, F32, kind="ExternalInput").ap() for k, v in arrays.items()]
    out = nc.dram_tensor("y_out", (P, KT, S), F32, kind="ExternalOutput").ap()
    build(nc, *args, out)
    r = run_bass_kernel_spmd(nc, [arrays], core_ids=[0])
    y = r.results[0]["y_out"]
    return np.asarray(y).transpose(2, 1, 0).reshape(1, S, D)
```
